# Optimizing a Trainium2 kernel written in Bass

```python
import jax, jax.numpy as jnp
from jax import lax
import numpy as np

D_MODEL = 1024
BATCH = 1
SEQ = 256
DEPTH = 2
DEC_BATCH = 1
DEC_SEQ = 32
PAST_LEN = 512

CHUNK = 64
HEAD_DIM = 64
FOX_HEADS = 8
RWKV_HEADS = 4
RET_HEADS = 4
FOX_WIDTH = FOX_HEADS * HEAD_DIM
RWKV_WIDTH = RWKV_HEADS * HEAD_DIM
RET_WIDTH = RET_HEADS * HEAD_DIM
MIX_WIDTH = FOX_WIDTH + RWKV_WIDTH + RET_WIDTH
FOX_QBLOCK = 128
RWKV_DECAY_RANK = 32
RWKV_A_RANK = 32
RWKV_GATE_RANK = 32
D_FF = 2816
PLE_DIM = 256
ROPE_BASE = 10000.0
NORM_EPS = 1e-6
RWKV_GN_EPS = 64e-5
RET_GN_EPS = 1e-6
FORGET_BIAS_MEAN = 2.0

FOX_SPLITS = (FOX_WIDTH, FOX_WIDTH, FOX_WIDTH, FOX_HEADS, FOX_WIDTH)
RWKV_SPLITS = (RWKV_WIDTH, RWKV_DECAY_RANK, RWKV_WIDTH, RWKV_WIDTH, RWKV_A_RANK, RWKV_GATE_RANK)
RET_SPLITS = (RET_WIDTH, RET_WIDTH, RET_WIDTH, RET_WIDTH)
FOX_COLS = sum(FOX_SPLITS)
RWKV_COLS = sum(RWKV_SPLITS)
RET_COLS = sum(RET_SPLITS)
IN_COLS = FOX_COLS + RWKV_COLS + RET_COLS

kernel_name = 'hybrid_fox_rwkv7_retention_stream'

F32 = jnp.float32

def _split(z, sizes):
    cuts = [int(c) for c in np.cumsum(sizes)[:-1]]
    return jnp.split(z, cuts, axis=-1)

def rmsnorm(x, g):
    xf = x.astype(F32)
    y = xf * lax.rsqrt(jnp.mean(xf * xf, axis=-1, keepdims=True) + NORM_EPS)
    return (y * g.astype(F32)).astype(x.dtype)

def head_norm(x, eps):
    xf = x.astype(F32)
    mu = jnp.mean(xf, axis=-1, keepdims=True)
    var = jnp.mean(jnp.square(xf - mu), axis=-1, keepdims=True)
    return (xf - mu) * lax.rsqrt(var + eps)

def swiglu(h, wg, wu, wd):
    return (jax.nn.silu(h @ wg) * (h @ wu)) @ wd

def rotary(x, pos):
    half = HEAD_DIM // 2
    inv = 1.0 / (ROPE_BASE ** (jnp.arange(half, dtype=F32) / half))
    ang = pos.astype(F32)[:, None] * inv[None, :]
    cos = jnp.cos(ang)[None, :, None, :]
    sin = jnp.sin(ang)[None, :, None, :]
    xf = x.astype(F32)
    x1, x2 = xf[..., :half], xf[..., half:]
    return jnp.concatenate([x1 * cos - x2 * sin, x2 * cos + x1 * sin], axis=-1).astype(x.dtype)

def fox_block(q, k, v, cq, ck, mask):
    s = jnp.einsum('bqhd,bkhd->bhqk', q, k).astype(F32) * (HEAD_DIM ** -0.5)
    s = s + jnp.swapaxes(cq, 1, 2)[:, :, :, None] - jnp.swapaxes(ck, 1, 2)[:, :, None, :]
    s = jnp.where(mask[None, None], s, -jnp.inf)
    p = jax.nn.softmax(s, axis=-1).astype(v.dtype)
    return jnp.einsum('bhqk,bkhd->bqhd', p, v)

def fox_prompt(q, k, v, logf):
    T = q.shape[1]
    c = jnp.cumsum(logf.astype(F32), axis=1)
    outs = []
    for i in range(T // FOX_QBLOCK):
        s0, e = i * FOX_QBLOCK, (i + 1) * FOX_QBLOCK
        mask = jnp.arange(s0, e)[:, None] >= jnp.arange(e)[None, :]
        outs.append(fox_block(q[:, s0:e], k[:, :e], v[:, :e], c[:, s0:e], c[:, :e], mask))
    return jnp.concatenate(outs, axis=1)

def fox_sample(q, k, v, logf, ck_cache, cv_cache, clf_cache):
    P, n = ck_cache.shape[1], q.shape[1]
    k_all = jnp.concatenate([ck_cache.astype(k.dtype), k], axis=1)
    v_all = jnp.concatenate([cv_cache.astype(v.dtype), v], axis=1)
    c = jnp.cumsum(jnp.concatenate([clf_cache.astype(F32), logf.astype(F32)], axis=1), axis=1)
    mask = (P + jnp.arange(n))[:, None] >= jnp.arange(P + n)[None, :]
    return fox_block(q, k_all, v_all, c[:, P:], c, mask)

def rwkv_mix(z, prev, S0, mu, w0, w_up, a0, a_up, g_up, k_k, k_a, r_k, ln_w, ln_b):
    B, T, _ = z.shape
    shifted = jnp.concatenate([prev.astype(z.dtype), z[:, :-1]], axis=1)
    zs = z + mu * (shifted - z)
    r, wd, k, v, ad, gd = _split(zs, RWKV_SPLITS)
    w = -jax.nn.softplus(-(w0 + jnp.tanh(wd) @ w_up).astype(F32)) - 0.5
    decay = jnp.exp(-jnp.exp(w))
    a = jax.nn.sigmoid((a0 + ad @ a_up).astype(F32))
    g = (jax.nn.sigmoid(gd) @ g_up).astype(F32)
    hd = lambda t: t.astype(F32).reshape(B, T, RWKV_HEADS, HEAD_DIM)
    r, k, v, a, decay = hd(r), hd(k), hd(v), hd(a), hd(decay)
    kk = k * k_k.astype(F32).reshape(RWKV_HEADS, HEAD_DIM)
    kk = kk * lax.rsqrt(jnp.maximum(jnp.sum(kk * kk, axis=-1, keepdims=True), 1e-24))
    k = k * (1.0 + (a - 1.0) * k_a.astype(F32).reshape(RWKV_HEADS, HEAD_DIM))

    def step(S, inp):
        r_t, w_t, k_t, v_t, kk_t, a_t = inp
        Skk = jnp.einsum('bhvk,bhk->bhv', S, kk_t)
        S = S * w_t[:, :, None, :] - Skk[..., None] * (kk_t * a_t)[:, :, None, :] + v_t[..., None] * k_t[:, :, None, :]
        return S, jnp.einsum('bhvk,bhk->bhv', S, r_t)

    xs = tuple(jnp.swapaxes(t, 0, 1) for t in (r, decay, k, v, kk, a))
    S, o = lax.scan(step, S0.astype(F32), xs)
    o = jnp.swapaxes(o, 0, 1)
    o = head_norm(o, RWKV_GN_EPS).reshape(B, T, RWKV_WIDTH) * ln_w.astype(F32) + ln_b.astype(F32)
    bonus = jnp.sum(r * k * r_k.astype(F32)[None, None], axis=-1, keepdims=True) * v
    out = (o + bonus.reshape(B, T, RWKV_WIDTH)) * g
    return out.astype(z.dtype), S.astype(z.dtype), z[:, -1:]

def retention_mix(z, R0, pos_offset, chunk_len):
    B, T, _ = z.shape
    q, k, v, g = _split(z, RET_SPLITS)
    hd = lambda t: t.reshape(B, T, RET_HEADS, HEAD_DIM)
    pos = jnp.arange(T) + pos_offset
    q = rotary(hd(q), pos).astype(F32)
    k = rotary(hd(k), pos).astype(F32) * (HEAD_DIM ** -0.5)
    v = hd(v).astype(F32)
    L = chunk_len
    NC = T // L
    log_g = jnp.log(1.0 - jnp.power(2.0, -5.0 - jnp.arange(RET_HEADS, dtype=F32)))
    idx = jnp.arange(L, dtype=F32)
    d_intra = jnp.exp(log_g[:, None, None] * jnp.abs(idx[:, None] - idx[None, :]))
    d_state = jnp.exp(log_g[:, None] * (L - 1.0 - idx)[None, :])
    d_query = jnp.exp(log_g[:, None] * (idx + 1.0)[None, :])
    d_chunk = jnp.exp(log_g * L)
    qc = q.reshape(B, NC, L, RET_HEADS, HEAD_DIM)
    kc = k.reshape(B, NC, L, RET_HEADS, HEAD_DIM)
    vc = v.reshape(B, NC, L, RET_HEADS, HEAD_DIM)
    s = jnp.einsum('bnqhd,bnkhd->bnhqk', qc, kc) * d_intra[None, None]
    o_intra = jnp.einsum('bnhqk,bnkhe->bnqhe', s, vc)
    kv = jnp.einsum('bnkhd,bnkhe,hk->bnhde', kc, vc, d_state)

    def step(R, kv_n):
        return R * d_chunk[None, :, None, None] + kv_n, R

    R_fin, R_start = lax.scan(step, R0.astype(F32), jnp.swapaxes(kv, 0, 1))
    R_start = jnp.swapaxes(R_start, 0, 1)
    o_inter = jnp.einsum('bnqhd,bnhde->bnqhe', qc * d_query.T[None, None, :, :, None], R_start)
    o = (o_intra + o_inter).reshape(B, T, RET_HEADS, HEAD_DIM)
    o = head_norm(o, RET_GN_EPS).reshape(B, T, RET_WIDTH) * jax.nn.silu(g.astype(F32))
    return o.astype(z.dtype), R_fin.astype(z.dtype)

def layer(x, pe, hist, lw):
    (n1, f1g, f1u, f1d, nm, w_in_l, b_f, mu, w0, w_up, a0, a_up, g_up, k_k, k_a, r_k, ln_w, ln_b,
     w_out_l, n2, f2g, f2u, f2d, w_pp, pn, w_pg) = lw
    B, T, _ = x.shape
    x = x + 0.5 * swiglu(rmsnorm(x, n1), f1g, f1u, f1d)
    z = rmsnorm(x, nm) @ w_in_l
    z_fox, z_rwkv, z_ret = _split(z, (FOX_COLS, RWKV_COLS, RET_COLS))
    fq, fk, fv, ff, fg = _split(z_fox, FOX_SPLITS)
    fq, fk, fv = (t.reshape(B, T, FOX_HEADS, HEAD_DIM) for t in (fq, fk, fv))
    logf = jax.nn.log_sigmoid((ff + b_f).astype(F32))
    if hist is None:
        o_fox = fox_prompt(fq, fk, fv, logf)
        prev = jnp.zeros((B, 1, RWKV_COLS), z.dtype)
        S0 = jnp.zeros((B, RWKV_HEADS, HEAD_DIM, HEAD_DIM), F32)
        R0 = jnp.zeros((B, RET_HEADS, HEAD_DIM, HEAD_DIM), F32)
        pos0, L = 0, CHUNK
    else:
        ck, cv, clf, S0, prev, R0 = hist
        o_fox = fox_sample(fq, fk, fv, logf, ck, cv, clf)
        pos0, L = ck.shape[1], T
    o_fox = (o_fox.reshape(B, T, FOX_WIDTH) * jax.nn.sigmoid(fg)).astype(x.dtype)
    o_rwkv, S_new, shift_new = rwkv_mix(z_rwkv, prev, S0, mu, w0, w_up, a0, a_up, g_up, k_k, k_a, r_k, ln_w, ln_b)
    o_ret, R_new = retention_mix(z_ret, R0, pos0, L)
    x = x + jnp.concatenate([o_fox, o_rwkv.astype(x.dtype), o_ret.astype(x.dtype)], axis=-1) @ w_out_l
    x = x + 0.5 * swiglu(rmsnorm(x, n2), f2g, f2u, f2d)
    e = rmsnorm(pe @ w_pp, pn)
    x = x + jax.nn.sigmoid(x @ w_pg) * e
    return x, (fk.astype(x.dtype), fv.astype(x.dtype), logf.astype(x.dtype), S_new, shift_new, R_new)

def setup_inputs(seed: int = 0) -> dict:
    key = jax.random.key(seed)
    ks = iter(jax.random.split(key, 48))

    def nrm(shape, scale):
        return jax.random.normal(next(ks), shape, F32) * scale

    def gain(shape):
        return 1.0 + nrm(shape, 0.02)

    L, D = DEPTH, D_MODEL
    decay_ramp = jnp.linspace(-7.0, -2.0, RWKV_WIDTH, dtype=F32) + 0.5
    return {
        'x_prompt': nrm((BATCH, SEQ, D), 1.0),
        'x_sample': nrm((DEC_BATCH, DEC_SEQ, D), 1.0),
        'cache_fox_k': nrm((L, DEC_BATCH, PAST_LEN, FOX_HEADS, HEAD_DIM), 1.0),
        'cache_fox_v': nrm((L, DEC_BATCH, PAST_LEN, FOX_HEADS, HEAD_DIM), 1.0),
        'cache_fox_logf': jax.nn.log_sigmoid(nrm((L, DEC_BATCH, PAST_LEN, FOX_HEADS), 1.0) + FORGET_BIAS_MEAN),
        'state_rwkv': nrm((L, DEC_BATCH, RWKV_HEADS, HEAD_DIM, HEAD_DIM), 0.5),
        'state_rwkv_shift': nrm((L, DEC_BATCH, 1, RWKV_COLS), 1.0),
        'state_ret': nrm((L, DEC_BATCH, RET_HEADS, HEAD_DIM, HEAD_DIM), 0.5),
        'p_prompt': nrm((L, BATCH, SEQ, PLE_DIM), 1.0),
        'p_sample': nrm((L, DEC_BATCH, DEC_SEQ, PLE_DIM), 1.0),
        'norm_ffn1': gain((L, D)),
        'w_ffn1_gate': nrm((L, D, D_FF), D ** -0.5),
        'w_ffn1_up': nrm((L, D, D_FF), D ** -0.5),
        'w_ffn1_down': nrm((L, D_FF, D), D_FF ** -0.5),
        'norm_mix': gain((L, D)),
        'w_in': nrm((L, D, IN_COLS), D ** -0.5),
        'fox_forget_bias': FORGET_BIAS_MEAN + nrm((L, FOX_HEADS), 0.1),
        'rwkv_mu': jax.random.uniform(next(ks), (L, RWKV_COLS), F32),
        'rwkv_w0': decay_ramp[None, :] + nrm((L, RWKV_WIDTH), 0.1),
        'rwkv_w_up': nrm((L, RWKV_DECAY_RANK, RWKV_WIDTH), 0.1),
        'rwkv_a0': nrm((L, RWKV_WIDTH), 0.1),
        'rwkv_a_up': nrm((L, RWKV_A_RANK, RWKV_WIDTH), 0.1),
        'rwkv_g_up': nrm((L, RWKV_GATE_RANK, RWKV_WIDTH), RWKV_GATE_RANK ** -0.5),
        'rwkv_k_k': 0.85 + nrm((L, RWKV_WIDTH), 0.02),
        'rwkv_k_a': gain((L, RWKV_WIDTH)),
        'rwkv_r_k': nrm((L, RWKV_HEADS, HEAD_DIM), 0.1),
        'rwkv_ln_w': gain((L, RWKV_WIDTH)),
        'rwkv_ln_b': nrm((L, RWKV_WIDTH), 0.02),
        'w_out': nrm((L, MIX_WIDTH, D), MIX_WIDTH ** -0.5),
        'norm_ffn2': gain((L, D)),
        'w_ffn2_gate': nrm((L, D, D_FF), D ** -0.5),
        'w_ffn2_up': nrm((L, D, D_FF), D ** -0.5),
        'w_ffn2_down': nrm((L, D_FF, D), D_FF ** -0.5),
        'w_ple_proj': nrm((L, PLE_DIM, D), PLE_DIM ** -0.5),
        'ple_norm': gain((L, D)),
        'w_ple_gate': nrm((L, D, D), D ** -0.5),
        'norm_final': gain((D,)),
    }

def reference(x_prompt, x_sample, cache_fox_k, cache_fox_v, cache_fox_logf, state_rwkv, state_rwkv_shift, state_ret,
              p_prompt, p_sample, norm_ffn1, w_ffn1_gate, w_ffn1_up, w_ffn1_down, norm_mix, w_in, fox_forget_bias,
              rwkv_mu, rwkv_w0, rwkv_w_up, rwkv_a0, rwkv_a_up, rwkv_g_up, rwkv_k_k, rwkv_k_a, rwkv_r_k, rwkv_ln_w,
              rwkv_ln_b, w_out, norm_ffn2, w_ffn2_gate, w_ffn2_up, w_ffn2_down, w_ple_proj, ple_norm, w_ple_gate,
              norm_final):
    xp, xs = x_prompt, x_sample
    p_states, s_states = [], []
    for l in range(DEPTH):
        lw = (norm_ffn1[l], w_ffn1_gate[l], w_ffn1_up[l], w_ffn1_down[l], norm_mix[l], w_in[l], fox_forget_bias[l],
              rwkv_mu[l], rwkv_w0[l], rwkv_w_up[l], rwkv_a0[l], rwkv_a_up[l], rwkv_g_up[l], rwkv_k_k[l], rwkv_k_a[l],
              rwkv_r_k[l], rwkv_ln_w[l], rwkv_ln_b[l], w_out[l], norm_ffn2[l], w_ffn2_gate[l], w_ffn2_up[l],
              w_ffn2_down[l], w_ple_proj[l], ple_norm[l], w_ple_gate[l])
        xp, sp = layer(xp, p_prompt[l], None, lw)
        hist = (cache_fox_k[l], cache_fox_v[l], cache_fox_logf[l], state_rwkv[l], state_rwkv_shift[l], state_ret[l])
        xs, ss = layer(xs, p_sample[l], hist, lw)
        p_states.append(sp)
        s_states.append(ss)
    y_prompt = rmsnorm(xp, norm_final)
    y_sample = rmsnorm(xs, norm_final)
    prompt_fox_k = jnp.stack([s[0] for s in p_states])
    prompt_fox_v = jnp.stack([s[1] for s in p_states])
    prompt_fox_logf = jnp.stack([s[2] for s in p_states])
    prompt_rwkv = jnp.stack([s[3] for s in p_states])
    prompt_rwkv_shift = jnp.stack([s[4] for s in p_states])
    prompt_ret = jnp.stack([s[5] for s in p_states])
    sample_fox_k = jnp.stack([s[0] for s in s_states])
    sample_fox_v = jnp.stack([s[1] for s in s_states])
    sample_fox_logf = jnp.stack([s[2] for s in s_states])
    sample_rwkv = jnp.stack([s[3] for s in s_states])
    sample_rwkv_shift = jnp.stack([s[4] for s in s_states])
    sample_ret = jnp.stack([s[5] for s in s_states])
    return (y_prompt, y_sample, prompt_fox_k, prompt_fox_v, prompt_fox_logf, prompt_rwkv, prompt_rwkv_shift, prompt_ret,
            sample_fox_k, sample_fox_v, sample_fox_logf, sample_rwkv, sample_rwkv_shift, sample_ret)


_drawn_inputs = setup_inputs


def setup_inputs(seed=0):
    import zlib

    import numpy as np

    out = dict(_drawn_inputs(seed))
    spreads = {}
    factors = {'cache_fox_logf': 40.208,
     'norm_ffn1': 3.771,
     'rwkv_ln_w': 35.59,
     'rwkv_ln_b': 35.83,
     'norm_ffn2': 6.072,
     'ple_norm': 38.048,
     'norm_final': 7.164,
     'cache_fox_k': 5.175,
     'cache_fox_v': 3.376,
     'rwkv_r_k': 2.704}
    for name, (base, spread) in spreads.items():
        noise = np.random.default_rng([zlib.crc32(name.encode()), seed]).standard_normal(out[name].shape)
        drawn = base * np.exp(spread * noise) if base else spread * noise
        out[name] = __import__('jax').numpy.asarray(drawn.astype(out[name].dtype))
    for name, factor in factors.items():
        out[name] = (out[name] * factor).astype(out[name].dtype)
    return out
```

```python
from contextlib import ExitStack

import numpy as np

import concourse.bass as bass
from concourse import mybir

F32 = mybir.dt.float32
ALU = mybir.AluOpType
ACT = mybir.ActivationFunctionType
AX_X = mybir.AxisListType.X

P = 128
DEPTH, D, DFF = 2, 1024, 2816
TP, TS = 256, 32
T = TP + TS
PAST = 512
DB = D // P
FB = DFF // P
HD = 64
FOX_H = 8
EPS = 1e-6
RWKV_EPS = 64e-5
RET_EPS = 1e-6

RING = 4
SLOT = DB * 256
N_FFN_SLOTS = FB
N_Z_SLOTS = 16
POS_FFN = (0, N_FFN_SLOTS + N_Z_SLOTS + 4)
POS_Z = N_FFN_SLOTS
POS_OUT = POS_Z + N_Z_SLOTS
POS_PROJ = POS_FFN[1] + N_FFN_SLOTS
POS_GATE = POS_PROJ + 1
N_SLOTS = POS_GATE + 4
DSTEPS = FB // 2
N_DOWN = 4 * DSTEPS

Z_SMALL, Z_R, Z_K, Z_V = 0, 1, 3, 5
Z_TQ, Z_TK, Z_TV, Z_TG = 7, 9, 11, 13
Z_FQ, Z_FK, Z_FV, Z_FG = 15, 19, 23, 27
NZ = 31
N_SHIFTED = 7

TILES = ((0, 128), (128, 128), (256, 32))
CH = 32
NCH = T // CH

CONSTS = {}
_at = 0
for _name, _n in (("ident", 128), ("mean", 128), ("headsum", 128), ("headmean", 128), ("rot", 128),
                  ("cos", T), ("sin", T), ("causal", 128), ("causal4", 32), ("levels", 5 * 128),
                  ("level0T", 128), ("before", 128), ("upto", 128), ("restart", 512), ("retmask", 512),
                  ("retmask_s", 128), ("dquery", 2 * T), ("dstate", 2 * T), ("dchunk", 4),
                  ("fox8", 8), ("cols", 8)):
    CONSTS[_name] = (_at, _n)
    _at += _n
N_CONST = _at
C_EPS, C_ONE, C_REPS, C_TEPS, C_KKB, C_SMALLSC, C_SMALLM, C_SMALLA = range(8)

PARAMS = {}
_at = 0
for _name, _n in (("n1", DB), ("nm", DB), ("n2", DB), ("pn", DB), ("mu", 7), ("prev", 7), ("bf", 1), ("w0", 2),
                  ("a0", 2), ("kk", 2), ("ka", 2), ("rk", 2), ("lnw", 2), ("lnb", 2), ("low", 256)):
    PARAMS[_name] = (_at, _n)
    _at += _n
N_PARAM = _at

MIXIN_PER_LAYER, ZSTORE_PER_LAYER, SH_OUT_PER_LAYER, P_IN_PER_LAYER = 16 * 10, 16 * 13, 16, 16

KK_SCALE = float(2.0 ** 30)
LOG_DECAY = -float(np.exp(-0.5))


def head_of(g):
    return 64 * (g // 2), g % 2


def program(nc, wcol, wdown, x_in, p_in, consts_in, params_in, foxl_in, kc_in, vc_in, clf_in, srwkv_in, sret_in,
            nf_in, y_out, k_out, v_out, logf_out, shift_out, rwkv_out, ret_out):
    with ExitStack() as ctx:
        def sb(name, *shape):
            return ctx.enter_context(nc.sbuf_tensor(name, list(shape), F32))

        xT = sb("xT", P, DB, T)
        hT = sb("hT", P, DB, T)
        zT = sb("zT", P, NZ, T)
        wc = sb("wc", P, RING, SLOT)
        rs = sb("rs", P, T)
        con = sb("con", P, N_CONST)
        par = sb("par", P, N_PARAM)
        negp = sb("negp", P, 4)
        nf = sb("nf", P, DB)
        foxL = sb("foxL", P, FOX_H, T)
        foxR = sb("foxR", P, TP + PAST + TS)
        ARENA = FB * T + DSTEPS * 1024
        arena = sb("arena", P, ARENA)
        hid = arena[:, 0:FB * T].rearrange("p (c t) -> p c t", c=FB)
        wd = arena[:, FB * T:ARENA].rearrange("p (s k n) -> p s k n", s=DSTEPS, k=2)
        EXTRA = 4480
        extra = sb("extra", P, EXTRA)
        et = sb("et", P, 2, T)

        class Space:

            def __init__(self, t, size):
                self.t, self.size, self.at = t, size, 0

            def take(self, *shape):
                n = int(np.prod(shape))
                v = self.t[:, self.at:self.at + n]
                self.at += n
                assert self.at <= self.size, (self.at, self.size)
                if len(shape) == 2:
                    v = v.rearrange("p (a b) -> p a b", a=shape[0])
                if len(shape) == 3:
                    v = v.rearrange("p (a b c) -> p a b c", a=shape[0], b=shape[1])
                return v

        A = Space(arena, ARENA)
        dz = A.take(N_SHIFTED, T)
        esm = A.take(T)
        sig4 = A.take(4, T)
        gate = A.take(2, T)
        lc = A.take(2, T)
        einc = A.take(2, T)
        einv = A.take(2, T)
        eexc = A.take(2, T)
        eend = A.take(2, T)
        kkf = A.take(2, T)
        bon = A.take(2, T)
        ar = A.take(2, 2, T)
        beta = A.take(2, T)
        bhat = A.take(2, T)
        kappa = A.take(2, T)
        khat = A.take(2, T)
        X = Space(extra, EXTRA)
        tok = X.take(3, 8, 128)
        st = X.take(11, 2, HD)
        M = Space(dz.rearrange("p a b -> p (a b)"), N_SHIFTED * T)
        am = M.take(4, 128)
        ml = M.take(4, 128)
        xx = M.take(4, 128)
        M = Space(arena, ARENA)
        M.at = A.at
        u0 = M.take(3, 256)
        tt = M.take(4, 128)
        yy = M.take(4, 128)
        bt = M.take(4, 128)
        ctm = M.take(3, 512)
        dtm = M.take(3, 512)
        bv = ml[:, 0:2, :].rearrange("p a b -> p (a b)")
        atT = eexc
        R = Space(arena, ARENA)
        qdec = R.take(2, T)
        kdec = R.take(2, T)
        rott = R.take(4, T)
        rtok = R.take(3, 512)
        smx = R.take(3, 512)
        rst = R.take(7, 2, HD)
        og = R.take(2, T)
        osq = R.take(2, T)
        rg = R.take(2, T)
        F = Space(arena, ARENA)
        vtok = F.take(3, 512)
        kc = F.take(4, PAST + TS)
        vc = F.take(4, 512)
        pq = F.take(2, 384)
        pt = F.take(2, 384)
        ps_s = F.take(2, PAST + TS)
        pt_s = F.take(2, 5, 128)
        fm = F.take(32)
        fg = F.take(4, T)
        cbuf = F.take(TP + PAST + TS)
        clf = F.take(PAST)
        fu = F.take(T)
        fe = F.take(T)
        lgf = F.take(T)
        shc = sb("shc", P, N_SHIFTED, 2)
        ow = kkf

        squares = (hT, hT, zT)

        bank = [ctx.enter_context(nc.psum_tensor(f"bank{i}", [P, 512], F32)) for i in range(8)]

        def c(name, rows=slice(0, P)):
            a, n = CONSTS[name]
            return con[rows, a:a + n]

        def col(i, rows=slice(0, P)):
            a = CONSTS["cols"][0] + i
            return con[rows, a:a + 1]

        def pa(name, i=0, rows=slice(0, P)):
            a = PARAMS[name][0] + i
            return par[rows, a:a + 1]

        names = ["col0", "col1", "col2", "col3", "col_used"] + [f"down{j}" for j in range(DSTEPS)] + """
            down_used down_ps x_ready sq norm_ps ln rstd h gate_ps up_ps exp_ps silu hidden z_ps z_ev
            par_in negp vchain schain sh_cp out_ps
            small e_small lowin low_ps e_low gcp ccs kraw ksq kk_ps kln rn bonin bon_ps bon_ok
            lcs dexc dend exps prods tr_ps trc mats_ps masks lev y_ps ycp d_ps lvl bv_ps bvc ua_ps uac
            u_ps u_ok s_ps s_ok o_ps o_ok gn_ps gn_sq gn_ln gn_rs gn_done
            rotsrc rot_ps rotd rtr_ps rtrc sm_ps smd kv_ps rsd ro_ps ro_ok rgate
            fu_ok fe_ok fl_ok lgf_ok fc_ok fmask vt_ps vtc fs_ps fmx fexp fpn ft_ps ftc fo_ps fo_ok fg_e fg_ok
            ss_ps smk smx sexp spn st_ps stc so_ps so_ok kcnew
            mixout pj_ps pj_cp pj_sq g_ps g_max g_exp g_t""".split()
        sems = {n: ctx.enter_context(nc.semaphore(n)) for n in names}
        S = sems
        numbers = [s.num for s in sems.values()]
        layer_sems = range(min(numbers), max(numbers) + 1)
        assert len(layer_sems) == len(names)
        for n in ("mixin", "zstore", "sh_out", "p_in"):
            S[n] = ctx.enter_context(nc.semaphore(n))
        start_sem = ctx.enter_context(nc.semaphore("start"))
        clear_sem = ctx.enter_context(nc.semaphore("zeroed"))
        end_sem = {n: ctx.enter_context(nc.semaphore("end_" + n)) for n in ("sq", "ps", "ln", "rs", "y", "st")}

        with nc.Block() as block:
            @block.sync
            def _(sp):
                sp.dma_start(xT[:], x_in).then_inc(start_sem, 16)
                sp.dma_start(con[:], consts_in).then_inc(start_sem, 16)
                sp.dma_start(nf[:], nf_in).then_inc(start_sem, 16)
                sp.wait_ge(clear_sem, 2)
                sp.dma_start(foxL[32:40, :, :], foxl_in).then_inc(start_sem, 16)
                sp.wait_ge(start_sem, 64)

            @block.gpsimd
            def _(pool):
                pool.memset(foxL[:], 0.0).then_inc(clear_sem, 1)
                pool.memset(foxR[:], 0.0).then_inc(clear_sem, 1)
                pool.wait_ge(clear_sem, 2)
                pool.memset(foxR[0:8, :], 1.0).then_inc(clear_sem, 1)

            @block.scalar
            def _(act):
                act.preload_act_table_set("natural_log_exp_and_others")

        with nc.Fori(0, DEPTH) as layer:
            with nc.Block() as block:

                @block.sync
                def _(sp):
                    sp.dma_start(par[:], params_in[layer]).then_inc(S["par_in"], 16)

                    def load_cols(p0, n):
                        for p in range(p0, p0 + n):
                            if p >= RING:
                                sp.wait_ge(S["col_used"], p - RING + 1)
                            sp.dma_start(wc[:, p % RING, :], wcol[layer, p]).then_inc(S[f"col{p % RING}"], 16)

                    def load_down(f):
                        for j in range(2 * DSTEPS):
                            n = 2 * DSTEPS * f + j
                            if j >= DSTEPS:
                                sp.wait_ge(S["down_used"], n - DSTEPS + 1)
                            elif f:
                                sp.wait_ge(S["mixout"], 1)
                            sp.dma_start(wd[:, j % DSTEPS].rearrange("p k n -> p (k n)"), wdown[layer, n])\
                              .then_inc(S[f"down{j % DSTEPS}"], 16)

                    load_cols(POS_FFN[0], N_FFN_SLOTS)
                    load_down(0)
                    load_cols(POS_Z, N_Z_SLOTS + 4)
                    load_cols(POS_FFN[1], N_FFN_SLOTS)
                    load_down(1)
                    load_cols(POS_PROJ, 5)

                @block.gpsimd
                def _(pool):
                    pool.dma_start(st[:, 0, :, :], srwkv_in[layer, 0]).then_inc(S["mixin"], 16)
                    pool.dma_start(st[:, 9, :, :], srwkv_in[layer, 1]).then_inc(S["mixin"], 16)
                    pool.wait_ge(S["z_ev"], 8 + NZ)
                    for b in range(4):
                        pool.dma_start(k_out[layer, b], zT[:, Z_FK + b, :]).then_inc(S["zstore"], 16)
                        pool.dma_start(v_out[layer, b], zT[:, Z_FV + b, :]).then_inc(S["zstore"], 16)
                    pool.wait_ge(S["sh_cp"], 1)
                    pool.dma_start(shift_out[layer], shc[:]).then_inc(S["sh_out"], 16)
                    pool.wait_ge(S["s_ok"], 18)
                    pool.dma_start(rwkv_out[layer, 0], st[:, 8, :, :]).then_inc(S["zstore"], 16)
                    pool.dma_start(rwkv_out[layer, 1], st[:, 10, :, :]).then_inc(S["zstore"], 16)
                    pool.wait_ge(S["gn_done"], 1)
                    pool.dma_start(rst[:, 0, :, :], sret_in[layer, 0]).then_inc(S["mixin"], 16)
                    pool.dma_start(rst[:, 5, :, :], sret_in[layer, 1]).then_inc(S["mixin"], 16)
                    pool.wait_ge(S["rsd"], 10)
                    pool.dma_start(ret_out[layer, 0], rst[:, 4, :, :]).then_inc(S["zstore"], 16)
                    pool.dma_start(ret_out[layer, 1], rst[:, 6, :, :]).then_inc(S["zstore"], 16)
                    pool.wait_ge(S["zstore"], layer * ZSTORE_PER_LAYER + 16 * 12)
                    pool.wait_ge(S["gn_done"], 2)
                    for b in range(4):
                        pool.dma_start(kc[:, b, 0:PAST], kc_in[layer, b]).then_inc(S["mixin"], 16)
                    pool.dma_start(vc[:], vc_in[layer]).then_inc(S["mixin"], 16)
                    pool.dma_start(clf[0:8, :], clf_in[layer]).then_inc(S["mixin"], 16)
                    pool.wait_ge(S["lgf_ok"], 1)
                    pool.dma_start(logf_out[layer], lgf[0:8, :]).then_inc(S["zstore"], 16)
                    pool.wait_ge(S["zstore"], layer * ZSTORE_PER_LAYER + 16 * 13)
                    pool.wait_ge(S["sh_out"], layer * SH_OUT_PER_LAYER + 16)
                    pool.wait_ge(S["x_ready"], 24)
                    pool.nop().then_inc(S["mixout"], 1)
                    pool.dma_start(zT[:, 16:18, :], p_in[layer]).then_inc(S["p_in"], 16)
                    pool.wait_ge(S["p_in"], layer * P_IN_PER_LAYER + 16)

                @block.scalar
                def _(act):
                    n_chain = [0]

                    def link(ins):
                        n_chain[0] += 1
                        ins.then_inc(S["schain"], 1)
                        act.wait_ge(S["schain"], n_chain[0])

                    def norm(s):
                        for b in range(DB):
                            act.wait_ge(S["x_ready"], 8 * s + b + 1)
                            act.activation(squares[s][:, b, :], xT[:, b, :], ACT.Square).then_inc(S["sq"], 1)
                        act.wait_ge(S["norm_ps"], s + 1)
                        act.activation(rs[:], bank[0][:, 0:T], ACT.Ln, bias=col(C_EPS)).then_inc(S["ln"], 1)
                        act.wait_ge(S["ln"], s + 1)
                        act.activation(rs[:], rs[:], ACT.Exp, scale=-0.5).then_inc(S["rstd"], 1)

                    def ffn(f):
                        def chunk(n, q):
                            act.wait_ge(S["gate_ps"], n + (FB * f + 1))
                            act.wait_ge(S["hidden"], n + (FB * f + 3))
                            act.activation(et[:, q % 2, :], bank[2 * q][:, 0:T], ACT.Exp, scale=-1.0)\
                               .then_inc(S["exp_ps"], 1)
                        with act.Fori(0, FB // 4) as i:
                            for q in range(4):
                                chunk(i * 4 + q, q)
                        for q in range(FB % 4):
                            chunk(FB // 4 * 4 + q, q)

                    norm(0)
                    ffn(0)
                    norm(1)

                    def z_copy(n, q):
                        act.wait_ge(S["z_ps"], n + 1)
                        return act.activation(zT[:, n, :] if isinstance(n, int) else zT[:, bass.ds(n, 1), :],
                                              bank[q][:, 0:T], ACT.Copy).then_inc(S["z_ev"], 1)
                    with act.Fori(0, NZ // 8) as i:
                        for q in range(8):
                            z_copy(i * 8 + q, q)
                    for q in range(NZ % 8):
                        z_copy(NZ // 8 * 8 + q, q)

                    act.wait_ge(S["small"], N_SHIFTED)
                    act.activation(esm, zT[:, Z_SMALL, :], ACT.Exp, scale=col(C_SMALLSC)).then_inc(S["e_small"], 1)
                    act.wait_ge(S["negp"], 1)
                    for i in range(4):
                        act.wait_ge(S["low_ps"], i + 1)
                        act.activation(sig4[:, i, :], bank[i][:, 0:T], ACT.Exp, scale=-1.0,
                                       bias=negp[:, i:i + 1]).then_inc(S["e_low"], 1)
                    for b in range(2):
                        act.wait_ge(S["low_ps"], 5 + b)
                        act.activation(gate[:, b, :], bank[4 + b][:, 0:T], ACT.Copy).then_inc(S["gcp"], 1)
                    act.wait_ge(S["kraw"], 2)
                    act.activation(bhat, kkf, ACT.Square).then_inc(S["ksq"], 1)
                    for b in range(2):
                        act.wait_ge(S["kln"], b + 1)
                        act.wait_ge(S["ksq"], 1)
                        link(act.activation(khat[:, b, :], khat[:, b, :], ACT.Ln, scale=KK_SCALE))
                        act.activation(khat[:, b, :], khat[:, b, :], ACT.Exp, scale=-0.5, bias=col(C_KKB))\
                           .then_inc(S["rn"], 1)
                    act.wait_ge(S["lcs"], 2)
                    act.activation(einc, lc, ACT.Exp).then_inc(S["exps"], 1)
                    act.activation(einv, lc, ACT.Exp, scale=-1.0).then_inc(S["exps"], 1)
                    act.wait_ge(S["dexc"], 1)
                    act.activation(eexc, eexc, ACT.Exp).then_inc(S["exps"], 1)
                    act.wait_ge(S["dend"], 1)
                    act.activation(eend, eend, ACT.Exp).then_inc(S["exps"], 1)
                    for j in range(3):
                        n = TILES[j][1]
                        for k in range(2):
                            act.wait_ge(S["tr_ps"], 2 * j + k + 1)
                            act.activation(tok[0:n, j, 4 * k:4 * k + 4, :].rearrange("p a b -> p (a b)"),
                                           bank[k][0:n, :], ACT.Copy).then_inc(S["trc"], 1)
                    for j in range(3):
                        n = TILES[j][1]
                        for s in range(4):
                            act.wait_ge(S["y_ps"], 4 * j + s + 1)
                            act.activation(yy[0:n, :, 0:n], bank[6][0:n, :].rearrange("p (g t) -> p g t", g=4)[:, :, 0:n],
                                           ACT.Copy).then_inc(S["ycp"], 1)
                        act.wait_ge(S["bv_ps"], j + 1)
                        act.activation(bv[0:n, :], bank[6][0:n, 0:256], ACT.Copy).then_inc(S["bvc"], 1)
                        act.wait_ge(S["ua_ps"], 2 * j + 1)
                        act.activation(u0[0:n, j, :], bank[6][0:n, 0:256], ACT.Copy).then_inc(S["uac"], 1)
                        act.wait_ge(S["ua_ps"], 2 * j + 2)
                        t0 = TILES[j][0]
                        act.activation(atT[:, :, t0:t0 + n],
                                       bank[7][:, 0:256].rearrange("p (b t) -> p b t", b=2)[:, :, 0:n],
                                       ACT.Copy).then_inc(S["uac"], 1)

                    def head_norm(which, eps):
                        act.wait_ge(S["gn_sq"], 1 + 2 * which)
                        for b in range(2):
                            act.wait_ge(S["gn_ps"], 4 * which + 3 + b)
                            act.activation(rs2[which][:, b, :], bank[4 + b][:, 0:T], ACT.Ln, bias=eps)\
                               .then_inc(S["gn_ln"], 1)
                        act.wait_ge(S["gn_ln"], 2 * which + 2)
                        act.activation(rs2[which], rs2[which], ACT.Exp, scale=-0.5).then_inc(S["gn_rs"], 1)

                    rs2 = (einv, osq)
                    head_norm(0, col(C_REPS))

                    act.wait_ge(S["gn_done"], 1)
                    for j in range(3):
                        n = TILES[j][1]
                        act.wait_ge(S["rtr_ps"], j + 1)
                        act.activation(rtok[0:n, j, :], bank[6][0:n, :], ACT.Copy).then_inc(S["rtrc"], 1)
                    act.activation(rg, zT[:, Z_TG:Z_TG + 2, :], ACT.Exp, scale=-1.0).then_inc(S["rgate"], 1)
                    head_norm(1, col(C_TEPS))

                    act.wait_ge(S["gn_done"], 2)
                    act.wait_ge(S["fu_ok"], 1)
                    link(act.activation(fe[0:8, :], fe[0:8, :], ACT.Exp))
                    act.activation(fe[0:8, :], fe[0:8, :], ACT.Ln, bias=col(C_ONE, slice(0, 8))).then_inc(S["fl_ok"], 1)
                    act.activation(fg, zT[:, Z_FG:Z_FG + 4, :], ACT.Exp, scale=-1.0).then_inc(S["fg_e"], 1)
                    for j in range(3):
                        n = TILES[j][1]
                        act.wait_ge(S["vt_ps"], j + 1)
                        act.activation(vtok[0:n, j, :], bank[6 + j % 2][0:n, :], ACT.Copy).then_inc(S["vtc"], 1)
                    for h in range(FOX_H):
                        act.wait_ge(S["fmx"], h + 1)
                        if h >= 2:
                            act.wait_ge(S["ft_ps"], h - 1)
                        sp_ = bank[h % 2]
                        act.activation(pq[:, h % 2, 0:128], sp_[:, 0:128], ACT.Exp, scale=0.125,
                                       bias=fm[:, 8 + 2 * (h % 2):9 + 2 * (h % 2)],
                                       accum_out=fm[:, 12 + 2 * (h % 2):13 + 2 * (h % 2)]).then_inc(S["fexp"], 1)
                        act.activation(pq[:, h % 2, 128:384], sp_[:, 128:384], ACT.Exp, scale=0.125,
                                       bias=fm[:, 9 + 2 * (h % 2):10 + 2 * (h % 2)],
                                       accum_out=fm[:, 13 + 2 * (h % 2):14 + 2 * (h % 2)]).then_inc(S["fexp"], 1)
                        act.wait_ge(S["ft_ps"], h + 1)
                        if h >= 2:
                            act.wait_ge(S["fo_ps"], h - 1)
                        act.activation(pt[:, h % 2, :], bank[2 + h % 2][:, 0:384], ACT.Copy).then_inc(S["ftc"], 1)
                    for g in range(2):
                        act.wait_ge(S["smx"], g + 1)
                        act.activation(ps_s[:, g, 0:PAST], bank[2 * g][:, :], ACT.Exp, scale=0.125,
                                       bias=fm[:, 20 + g:21 + g], accum_out=fm[:, 22 + g:23 + g]).then_inc(S["sexp"], 1)
                        act.activation(ps_s[:, g, PAST:], ps_s[:, g, PAST:], ACT.Exp, scale=0.125,
                                       bias=fm[:, 20 + g:21 + g], accum_out=fm[:, 24 + g:25 + g]).then_inc(S["sexp"], 1)
                        act.wait_ge(S["st_ps"], 2 * g + 1)
                        act.activation(pt_s[:, g, 0:4, :].rearrange("p a b -> p (a b)"), bank[4][:, :], ACT.Copy)\
                           .then_inc(S["stc"], 1)
                        act.wait_ge(S["st_ps"], 2 * g + 2)
                        act.activation(pt_s[0:TS, g, 4, :], bank[5][0:TS, 0:128], ACT.Copy).then_inc(S["stc"], 1)

                    norm(2)
                    ffn(1)

                    for b in range(DB):
                        act.wait_ge(S["pj_ps"], b + 1)
                        act.activation(zT[:, b, :], bank[b % 4][:, 0:T], ACT.Copy).then_inc(S["pj_cp"], 1)
                        act.wait_ge(S["pj_cp"], b + 1)
                        act.activation(zT[:, 8 + b, :], zT[:, b, :], ACT.Square).then_inc(S["pj_sq"], 1)
                    act.wait_ge(S["norm_ps"], 4)
                    act.activation(rs[:], bank[7][:, 0:T], ACT.Ln, bias=col(C_EPS)).then_inc(S["ln"], 1)
                    act.wait_ge(S["ln"], 4)
                    act.activation(rs[:], rs[:], ACT.Exp, scale=-0.5).then_inc(S["rstd"], 1)
                    for b in range(DB):
                        act.wait_ge(S["g_max"], b + 1)
                        act.activation(zT[:, 18 + b, :], zT[:, 18 + b, :], ACT.Exp, scale=-1.0).then_inc(S["g_exp"], 1)

                @block.vector
                def _(dve):
                    n_chain = [0]

                    def link(ins):
                        n_chain[0] += 1
                        ins.then_inc(S["vchain"], 1)
                        dve.wait_ge(S["vchain"], n_chain[0])

                    def norm(s, gains):
                        dve.wait_ge(S["rstd"], s + 1)
                        dve.wait_ge(S["x_ready"], 8 * (s + 1))
                        for b in range(DB):
                            dve.scalar_tensor_tensor(hT[:, b, :], xT[:, b, :], pa(gains, b), rs[:],
                                                     ALU.mult, ALU.mult).then_inc(S["h"], 1)

                    def ffn(f):
                        def chunk(n, q):
                            e = et[:, q % 2, :]
                            base = 3 * FB * f
                            dve.wait_ge(S["exp_ps"], n + (FB * f + 1))
                            dve.tensor_scalar(e, e, 1.0, None, ALU.add).then_inc(S["silu"], 1)
                            dve.wait_ge(S["silu"], n * 3 + (base + 1))
                            dve.reciprocal(e, e).then_inc(S["silu"], 1)
                            dve.wait_ge(S["silu"], n * 3 + (base + 2))
                            dve.tensor_tensor(e, e, bank[2 * q][:, 0:T], ALU.mult).then_inc(S["silu"], 1)
                            dve.wait_ge(S["silu"], n * 3 + (base + 3))
                            dve.wait_ge(S["up_ps"], n + (FB * f + 1))
                            dst = hid[:, n, :] if isinstance(n, int) else hid[:, bass.ds(n, 1), :]
                            dve.tensor_tensor(dst, e, bank[2 * q + 1][:, 0:T], ALU.mult).then_inc(S["hidden"], 1)
                        with dve.Fori(0, FB // 4) as i:
                            for q in range(4):
                                chunk(i * 4 + q, q)
                        for q in range(FB % 4):
                            chunk(FB // 4 * 4 + q, q)
                        for b in range(DB):
                            dve.wait_ge(S["down_ps"], DB * f + b + 1)
                            dve.scalar_tensor_tensor(xT[:, b, :], bank[4 + b % 4][:, 0:T], 0.5, xT[:, b, :],
                                                     ALU.mult, ALU.add).then_inc(S["x_ready"], 1)

                    def sigmoid_of(e):
                        link(dve.tensor_scalar(e, e, 1.0, None, ALU.add))
                        link(dve.reciprocal(e, e))

                    dve.nop().then_inc(S["x_ready"], 8)
                    dve.nop().then_inc(S["hidden"], 4)
                    dve.nop().then_inc(S["z_ev"], 8)
                    dve.wait_ge(S["par_in"], 16)
                    a = PARAMS["w0"][0]
                    dve.tensor_scalar(negp[:], par[:, a:a + 4], -1.0, None, ALU.mult).then_inc(S["negp"], 1)
                    norm(0, "n1")
                    ffn(0)
                    norm(1, "nm")

                    dve.wait_ge(S["z_ev"], 8 + NZ)
                    zs = zT[:, 0:N_SHIFTED, :]
                    link(dve.tensor_tensor(dz[:, :, 1:T], zs[:, :, 0:T - 1], zs[:, :, 1:T], ALU.subtract))
                    link(dve.tensor_scalar(dz[:, :, 0:1], zs[:, :, 0:1], -1.0, None, ALU.mult))
                    prev = par[:, PARAMS["prev"][0]:PARAMS["prev"][0] + 7].unsqueeze(2)
                    link(dve.tensor_tensor(dz[:, :, TP:TP + 1], prev, zs[:, :, TP:TP + 1], ALU.subtract))
                    link(dve.tensor_copy(shc[:, :, 0:1], zs[:, :, TP - 1:TP]))
                    dve.tensor_copy(shc[:, :, 1:2], zs[:, :, T - 1:T]).then_inc(S["sh_cp"], 1)
                    dve.wait_ge(S["sh_cp"], 1)
                    for b in range(N_SHIFTED):
                        dve.scalar_tensor_tensor(zT[:, b, :], dz[:, b, :], pa("mu", b), zT[:, b, :],
                                                 ALU.mult, ALU.add).then_inc(S["small"], 1)
                    dve.wait_ge(S["small"], N_SHIFTED)
                    dve.wait_ge(S["e_small"], 1)
                    sigmoid_of(esm)
                    dve.tensor_scalar(dz[:, 0, :], esm, col(C_SMALLM), col(C_SMALLA), ALU.mult, ALU.add)\
                       .then_inc(S["lowin"], 1)
                    r, k, v = (zT[:, z:z + 2, :] for z in (Z_R, Z_K, Z_V))
                    for b in range(2):
                        dve.tensor_scalar(kkf[:, b, :], k[:, b, :], pa("kk", b), None, ALU.mult)\
                           .then_inc(S["kraw"], 1)
                    dve.wait_ge(S["e_low"], 4)
                    sigmoid_of(sig4)
                    lw, aa = sig4[:, 0:2, :], sig4[:, 2:4, :]
                    link(dve.tensor_scalar(lw, lw, LOG_DECAY, None, ALU.mult))
                    for b in range(2):
                        dve.tensor_tensor_scan(lc[:, b, :], c("restart")[:, 0:T], lw[:, b, :], 0.0,
                                               ALU.mult, ALU.add).then_inc(S["lcs"], 1)
                    dve.wait_ge(S["lcs"], 2)
                    dve.tensor_tensor(eexc, lc, lw, ALU.subtract).then_inc(S["dexc"], 1)
                    chunks = lc.rearrange("p b (n u) -> p (b n) u", u=CH)
                    dve.tensor_tensor(eend.rearrange("p b (n u) -> p (b n) u", u=CH),
                                      chunks[:, :, CH - 1:CH].to_broadcast([P, 2 * NCH, CH]), chunks,
                                      ALU.subtract).then_inc(S["dend"], 1)
                    for b in range(2):
                        dve.wait_ge(S["kk_ps"], b + 1)
                        dve.tensor_scalar(khat[:, b, :], bank[b][:, 0:T], 1e-24, None, ALU.max).then_inc(S["kln"], 1)
                    dve.wait_ge(S["rn"], 2)
                    link(dve.tensor_tensor(kkf, kkf, khat, ALU.mult))
                    for b in range(2):
                        link(dve.tensor_scalar(khat[:, b, :], aa[:, b, :], -1.0, pa("ka", b), ALU.add, ALU.mult))
                    link(dve.scalar_tensor_tensor(k, khat, 1.0, k, ALU.add, ALU.mult))
                    for b in range(2):
                        dve.scalar_tensor_tensor(bon[:, b, :], r[:, b, :], pa("rk", b), k[:, b, :],
                                                 ALU.mult, ALU.mult).then_inc(S["bonin"], 1)
                    dve.wait_ge(S["exps"], 4)
                    link(dve.tensor_tensor(aa, kkf, aa, ALU.mult))
                    link(dve.tensor_tensor(ar[:, :, 0, :], kkf, eexc, ALU.mult))
                    link(dve.tensor_tensor(ar[:, :, 1, :], r, einc, ALU.mult))
                    link(dve.scalar_tensor_tensor(beta, aa, -1.0, einv, ALU.mult, ALU.mult))
                    link(dve.scalar_tensor_tensor(bhat, aa, -1.0, eend, ALU.mult, ALU.mult))
                    link(dve.tensor_tensor(kappa, k, einv, ALU.mult))
                    dve.tensor_tensor(khat, k, eend, ALU.mult).then_inc(S["prods"], 1)
                    dve.wait_ge(S["prods"], 1)
                    for b in range(2):
                        dve.wait_ge(S["bon_ps"], b + 1)
                        dve.tensor_tensor(bon[:, b, :], bank[2 + b][:, 0:T], v[:, b, :], ALU.mult).then_inc(S["bon_ok"], 1)

                    for j in range(3):
                        n = TILES[j][1]
                        rows = slice(0, n)

                        def four(x):
                            return x[rows, :, 0:n]

                        def half(bk):
                            return bk[rows, 0:256].rearrange("p (g t) -> p g t", g=2)[:, :, 0:n]

                        def mask(name, k, i=0):
                            m = c(name)[rows, i * 128:i * 128 + n]
                            return m.unsqueeze(1).to_broadcast([n, k, n])

                        for par_ in range(2):
                            gs = slice(2 * par_, 2 * par_ + 2)
                            dve.wait_ge(S["mats_ps"], 6 * j + 3 * par_ + 1)
                            link(dve.tensor_copy(am[rows, gs, 0:n], half(bank[3 * par_])))
                            second = bank[3 * par_ + 1][rows, :].rearrange("p (g w t) -> p g w t", g=2, w=2)
                            third = bank[3 * par_ + 2][rows, :].rearrange("p (g w t) -> p g w t", g=2, w=2)
                            dve.wait_ge(S["mats_ps"], 6 * j + 3 * par_ + 2)
                            link(dve.tensor_tensor(xx[rows, gs, 0:n], second[:, :, 0, 0:n], mask("level0T", 2), ALU.mult))
                            cts = ctm[rows, j, :].rearrange("p (g t) -> p g t", g=4)[:, gs, 0:n]
                            link(dve.tensor_tensor(cts, second[:, :, 1, 0:n], mask("upto", 2), ALU.mult))
                            dve.wait_ge(S["mats_ps"], 6 * j + 3 * par_ + 3)
                            link(dve.tensor_tensor(bt[rows, gs, 0:n], third[:, :, 0, 0:n], mask("before", 2), ALU.mult))
                            dts = dtm[rows, j, :].rearrange("p (g t) -> p g t", g=4)[:, gs, 0:n]
                            dve.tensor_tensor(dts, third[:, :, 1, 0:n], mask("upto", 2), ALU.mult)\
                               .then_inc(S["masks"], 1)
                            dve.wait_ge(S["masks"], 2 * j + par_ + 1)
                        link(dve.tensor_tensor(four(xx), four(xx), mask("ident", 4), ALU.add))
                        link(dve.tensor_tensor(four(tt), four(am), mask("levels", 4, 0), ALU.mult))
                        link(dve.tensor_tensor(four(tt), four(tt), mask("ident", 4), ALU.add))
                        for s in range(1, 5):
                            dve.tensor_tensor(four(ml), four(am), mask("levels", 4, s), ALU.mult).then_inc(S["lev"], 1)
                            full = [bank[q][rows, :].rearrange("p (g t) -> p g t", g=4)[:, :, 0:n] for q in (7, 0)]
                            dve.wait_ge(S["d_ps"], 8 * j + 2 * (s - 1) + 1)
                            link(dve.tensor_tensor(four(xx), four(xx), full[0], ALU.add))
                            dve.wait_ge(S["d_ps"], 8 * j + 2 * (s - 1) + 2)
                            dve.tensor_tensor(four(tt), four(tt), full[1], ALU.add).then_inc(S["lvl"], 1)
                            dve.wait_ge(S["lvl"], 4 * j + s)

                    dve.wait_ge(S["uac"], 6)
                    for i in range(NCH):
                        j, q = (i // 4, i % 4) if i < 8 else (2, 0)
                        rows = slice(32 * q, 32 * q + 32)
                        old, new = (i, i + 1) if i < 8 else (9, 10)
                        dve.wait_ge(S["u_ps"], i + 1)
                        for e in range(2):
                            dve.tensor_tensor(u0[rows, j, 128 * e:128 * e + 128], u0[rows, j, 128 * e:128 * e + 128],
                                              bank[e][rows, 0:128], ALU.add).then_inc(S["u_ok"], 1)
                        for b in range(2):
                            dve.wait_ge(S["s_ps"], 2 * i + b + 1)
                            end = CH * (i + 1) - 1
                            dve.scalar_tensor_tensor(st[:, new, b, :], st[:, old, b, :], einc[:, b, end:end + 1],
                                                     bank[2 + b][:, 0:HD], ALU.mult, ALU.add).then_inc(S["s_ok"], 1)
                    for j in range(3):
                        t0, n = TILES[j]
                        for e in range(2):
                            dve.wait_ge(S["o_ps"], 2 * j + e + 1)
                            rows = slice(64 * e, 64 * e + 64)
                            dve.tensor_copy(ow[rows, :, t0:t0 + n],
                                            bank[4 + 2 * (j % 2) + e][rows, 0:256].rearrange("p (b t) -> p b t", b=2)[:, :, 0:n])\
                               .then_inc(S["o_ok"], 1)

                    def head_norm(which, o, sq, rstd):
                        dve.wait_ge(S["o_ok"] if which == 0 else S["ro_ok"], 6)
                        for b in range(2):
                            dve.wait_ge(S["gn_ps"], 4 * which + 1 + b)
                            link(dve.tensor_tensor(o[:, b, :], o[:, b, :], bank[2 + b][:, 0:T], ALU.subtract))
                        dve.tensor_tensor(sq, o, o, ALU.mult).then_inc(S["gn_sq"], 2)
                        dve.wait_ge(S["gn_rs"], which + 1)
                        link(dve.tensor_tensor(o, o, rstd, ALU.mult))

                    head_norm(0, ow, kappa, einv)
                    for b in range(2):
                        link(dve.tensor_scalar(ow[:, b, :], ow[:, b, :], pa("lnw", b), pa("lnb", b), ALU.mult, ALU.add))
                    dve.wait_ge(S["bon_ok"], 2)
                    link(dve.tensor_tensor(ow, ow, bon, ALU.add))
                    dve.wait_ge(S["gcp"], 2)
                    dve.tensor_tensor(hT[:, 4:6, :], ow, gate, ALU.mult).then_inc(S["gn_done"], 1)
                    dve.wait_ge(S["gn_done"], 1)

                    qk = zT[:, Z_TQ:Z_TQ + 4, :]
                    for b in range(4):
                        dve.wait_ge(S["rot_ps"], b + 1)
                        link(dve.tensor_tensor(rott[:, b, :], bank[b][:, 0:T], c("sin"), ALU.mult))
                    cos4 = c("cos").unsqueeze(1).to_broadcast([P, 4, T])
                    link(dve.tensor_tensor(qk, qk, cos4, ALU.mult))
                    link(dve.tensor_tensor(qk, qk, rott, ALU.add))
                    dq, ds_ = (c(x).rearrange("p (b t) -> p b t", b=2) for x in ("dquery", "dstate"))
                    link(dve.tensor_tensor(qdec, qk[:, 0:2, :], dq, ALU.mult))
                    dve.tensor_tensor(kdec, qk[:, 2:4, :], ds_, ALU.mult).then_inc(S["rotd"], 1)
                    for j in range(3):
                        n = TILES[j][1]
                        m = (c("retmask")[0:n, :] if j < 2 else c("retmask_s")[0:n, :]).rearrange("p (g t) -> p g t", g=4)
                        for e in range(2):
                            dve.wait_ge(S["sm_ps"], 2 * j + e + 1)
                            dve.tensor_tensor(smx[0:n, j, :].rearrange("p (g t) -> p g t", g=4)[:, 2 * e:2 * e + 2, 0:n],
                                              bank[e][0:n, 0:256].rearrange("p (g t) -> p g t", g=2)[:, :, 0:n],
                                              m[:, 2 * e:2 * e + 2, :], ALU.mult).then_inc(S["smd"], 1)
                    dve.wait_ge(S["mixin"], layer * MIXIN_PER_LAYER + 64)
                    dch = c("dchunk")
                    for i in range(5):
                        old, new = (i, i + 1) if i < 4 else (5, 6)
                        dve.wait_ge(S["kv_ps"], 5)
                        if 1 <= i < 4:
                            dve.wait_ge(S["rsd"], 2 * i)
                        for b in range(2):
                            s = 128 * (i // 2) + 64 * b
                            dve.scalar_tensor_tensor(rst[:, new, b, :], rst[:, old, b, :],
                                                     dch[:, 2 * (i // 4) + b:2 * (i // 4) + b + 1],
                                                     bank[2 + i % 2][:, s:s + HD], ALU.mult, ALU.add).then_inc(S["rsd"], 1)
                    for j in range(3):
                        t0, n = TILES[j]
                        for e in range(2):
                            dve.wait_ge(S["ro_ps"], 2 * j + e + 1)
                            rows = slice(64 * e, 64 * e + 64)
                            dve.tensor_copy(og[rows, :, t0:t0 + n],
                                            bank[4 + 2 * (j % 2) + e][rows, 0:256].rearrange("p (b t) -> p b t", b=2)[:, :, 0:n])\
                               .then_inc(S["ro_ok"], 1)
                    head_norm(1, og, osq, osq)
                    dve.wait_ge(S["rgate"], 1)
                    sigmoid_of(rg)
                    link(dve.tensor_tensor(rg, rg, zT[:, Z_TG:Z_TG + 2, :], ALU.mult))
                    dve.tensor_tensor(hT[:, 6:8, :], og, rg, ALU.mult).then_inc(S["gn_done"], 1)
                    dve.wait_ge(S["gn_done"], 2)

                    dve.wait_ge(S["zstore"], layer * ZSTORE_PER_LAYER + 16 * 12)
                    e8 = slice(0, 8)
                    link(dve.tensor_scalar(fu[e8, :], zT[e8, Z_SMALL, :], pa("bf", 0, e8), None, ALU.add))
                    link(dve.tensor_scalar(fe[e8, :], fu[e8, :], -1.0, None, ALU.mult))
                    dve.tensor_tensor(fe[e8, :], fe[e8, :], fu[e8, :], ALU.min).then_inc(S["fu_ok"], 1)
                    dve.wait_ge(S["fl_ok"], 1)
                    dve.scalar_tensor_tensor(lgf[e8, :], fu[e8, :], 0.0, fe[e8, :], ALU.min, ALU.subtract)\
                       .then_inc(S["lgf_ok"], 1)
                    dve.wait_ge(S["lgf_ok"], 1)
                    dve.wait_ge(S["mixin"], layer * MIXIN_PER_LAYER + 160)
                    w = con[e8, CONSTS["fox8"][0]:CONSTS["fox8"][0] + 8]
                    unit = foxR[e8, :]
                    link(dve.tensor_tensor_scan(cbuf[e8, 0:TP], unit[:, 0:TP], lgf[e8, 0:TP], 0.0, ALU.mult, ALU.add))
                    link(dve.tensor_tensor_scan(cbuf[e8, TP:TP + PAST], unit[:, 0:PAST], clf[e8, :], 0.0, ALU.mult, ALU.add))
                    link(dve.tensor_tensor_scan(cbuf[e8, TP + PAST:], unit[:, 0:TS], lgf[e8, TP:T],
                                                cbuf[e8, TP + PAST - 1:TP + PAST], ALU.mult, ALU.add))
                    link(dve.tensor_copy(foxR[32:40, :], cbuf[e8, :]))
                    for q0, k0, n in ((0, 0, TP), (TP, TP + PAST, TS)):
                        link(dve.tensor_tensor(foxL[e8, :, q0:q0 + n],
                                               cbuf[e8, k0:k0 + n].unsqueeze(1).to_broadcast([8, FOX_H, n]),
                                               w.unsqueeze(2).to_broadcast([8, FOX_H, n]), ALU.mult))
                    dve.tensor_copy(kc[:, :, PAST:], zT[:, Z_FK:Z_FK + 4, TP:T]).then_inc(S["fc_ok"], 1)
                    dve.wait_ge(S["fg_e"], 1)
                    sigmoid_of(fg)
                    for h in range(FOX_H):
                        b, e = h // 2, h % 2
                        sc = bank[e]
                        diag = sc[:, 0:384].rearrange("p (k t) -> p k t", k=3)[:, 0:3:2, :]
                        dve.wait_ge(S["fs_ps"], h + 1)
                        link(dve.tensor_tensor(diag, diag, c("causal").unsqueeze(1).to_broadcast([P, 2, 128]), ALU.add))
                        link(dve.tensor_reduce(fm[:, 0:1], sc[:, 0:128], AX_X, ALU.max))
                        link(dve.tensor_reduce(fm[:, 1:2], sc[:, 128:384], AX_X, ALU.max))
                        dve.tensor_scalar(fm[:, 8 + 2 * e:10 + 2 * e], fm[:, 0:2], -0.125, None, ALU.mult)\
                           .then_inc(S["fmx"], 1)
                        dve.wait_ge(S["fexp"], 2 * h + 2)
                        link(dve.reciprocal(fm[:, 16 + 2 * e:18 + 2 * e], fm[:, 12 + 2 * e:14 + 2 * e]))
                        link(dve.tensor_scalar(pq[:, e, 0:128], pq[:, e, 0:128], fm[:, 16 + 2 * e:17 + 2 * e], None, ALU.mult))
                        dve.tensor_scalar(pq[:, e, 128:384], pq[:, e, 128:384], fm[:, 17 + 2 * e:18 + 2 * e], None, ALU.mult)\
                           .then_inc(S["fpn"], 1)
                        dve.wait_ge(S["fo_ps"], h + 1)
                        rows = slice(64 * e, 64 * e + 64)
                        dve.tensor_tensor(hT[rows, b, 0:TP], bank[4 + b % 2][rows, 0:TP], fg[rows, b, 0:TP], ALU.mult)\
                           .then_inc(S["fo_ok"], 1)
                    for g in range(2):
                        dve.wait_ge(S["ss_ps"], g + 1)
                        link(dve.tensor_tensor(ps_s[:, g, PAST:], bank[2 * g + 1][:, 0:TS], c("causal4"), ALU.add))
                        link(dve.tensor_reduce(fm[:, 26:27], ps_s[:, g, PAST:], AX_X, ALU.max))
                        link(dve.tensor_reduce(fm[:, 27:28], bank[2 * g][:, :], AX_X, ALU.max))
                        link(dve.tensor_tensor(fm[:, 28:29], fm[:, 26:27], fm[:, 27:28], ALU.max))
                        dve.tensor_scalar(fm[:, 20 + g:21 + g], fm[:, 28:29], -0.125, None, ALU.mult).then_inc(S["smx"], 1)
                        dve.wait_ge(S["sexp"], 2 * g + 2)
                        link(dve.tensor_tensor(fm[:, 29:30], fm[:, 22 + g:23 + g], fm[:, 24 + g:25 + g], ALU.add))
                        link(dve.reciprocal(fm[:, 30:31], fm[:, 29:30]))
                        dve.tensor_scalar(ps_s[:, g, :], ps_s[:, g, :], fm[:, 30:31], None, ALU.mult).then_inc(S["spn"], 1)
                    for e in range(2):
                        dve.wait_ge(S["so_ps"], e + 1)
                        rows = slice(64 * e, 64 * e + 64)
                        dve.tensor_tensor(hT[rows, 0:4, TP:T], bank[6 + e][rows, 0:128].rearrange("p (b t) -> p b t", b=4),
                                          fg[rows, :, TP:T], ALU.mult).then_inc(S["so_ok"], 1)

                    for b in range(DB):
                        dve.wait_ge(S["out_ps"], b + 1)
                        dve.tensor_tensor(xT[:, b, :], bank[b][:, 0:T], xT[:, b, :], ALU.add).then_inc(S["x_ready"], 1)

                    norm(2, "n2")
                    ffn(1)

                    dve.wait_ge(S["rstd"], 4)
                    for b in range(DB):
                        link(dve.scalar_tensor_tensor(zT[:, b, :], zT[:, b, :], pa("pn", b), rs[:], ALU.mult, ALU.mult))
                    for b in range(DB):
                        dve.wait_ge(S["g_ps"], b + 1)
                        dve.tensor_scalar(zT[:, 18 + b, :], bank[b][:, 0:T], -80.0, None, ALU.max).then_inc(S["g_max"], 1)
                    for b in range(DB):
                        dve.wait_ge(S["g_exp"], b + 1)
                        sigmoid_of(zT[:, 18 + b, :])
                        link(dve.tensor_tensor(zT[:, b, :], zT[:, b, :], zT[:, 18 + b, :], ALU.mult))
                    for b in range(DB):
                        dve.tensor_tensor(xT[:, b, :], xT[:, b, :], zT[:, b, :], ALU.add).then_inc(S["x_ready"], 1)

                @block.tensor
                def _(pe):
                    def slot(p):
                        return wc[:, p % RING, :].rearrange("p (k n) -> p k n", k=DB)

                    def norm(s):
                        for b in range(DB):
                            pe.wait_ge(S["sq"], 8 * s + b + 1)
                            mm = pe.matmul(bank[0][:, 0:T], c("mean"), squares[s][:, b, :], start=(b == 0), stop=(b == DB - 1))
                        mm.then_inc(S["norm_ps"], 1)

                    def arrived(p, more=0):
                        pe.wait_ge(S[f"col{p % RING}"], more * 16 + 16 * (p // RING + 1))

                    def ffn(f):
                        p0 = POS_FFN[f]

                        def pair(i, jj):
                            for w in range(2):
                                p = p0 + 2 * jj + w
                                arrived(p, i)
                                for cc in range(2):
                                    q = 2 * jj + cc
                                    if w == 0:
                                        pe.wait_ge(S["hidden"], i * 4 + (FB * f + q + 1))
                                    for k in range(DB):
                                        if jj == 0 and w == 0 and cc == 0:
                                            pe.wait_ge(S["h"], DB * 2 * f + k + 1)
                                        mm = pe.matmul(bank[2 * q + w][:, 0:T], slot(p)[:, k, cc * 128:cc * 128 + 128],
                                                       hT[:, k, :], start=(k == 0), stop=(k == DB - 1))
                                    mm.then_inc(S["up_ps" if w else "gate_ps"], 1)
                                pe.wait_ge(S["up_ps" if w else "gate_ps"], i * 4 + (FB * f + 2 * jj + 2))
                                pe.nop().then_inc(S["col_used"], 1)

                        with pe.Fori(0, FB // 4) as i:
                            pair(i, 0)
                            pair(i, 1)
                        pair(FB // 4, 0)
                        pe.wait_ge(S["hidden"], FB * f + 4 + FB // 4 * 4)
                        with pe.Fori(0, 2) as h:
                            pe.wait_ge(S["x_ready"], h * 4 + 8 * (2 * f + 1))
                            for j in range(DSTEPS):
                                pe.wait_ge(S[f"down{j}"], h * 16 + 16 * (2 * f + 1))
                                for kk in range(2):
                                    k = 2 * j + kk
                                    pe.wait_ge(S["hidden"], FB * f + 4 + k + 1)
                                    for m in range(4):
                                        mm = pe.matmul(bank[4 + m][:, 0:T], wd[:, j, kk, m * 128:m * 128 + 128],
                                                       hid[:, k, :], start=(k == 0), stop=(k == FB - 1))
                                        if k == FB - 1:
                                            mm.then_inc(S["down_ps"], 1)
                                        elif kk == 1 and m == 3:
                                            mm.then_inc(S["down_used"], 1)
                            pe.wait_ge(S["down_ps"], h * 4 + (DB * f + 4))
                            pe.nop().then_inc(S["down_used"], 1)

                    def heads(fn):
                        for g in range(4):
                            fn(g, *head_of(g))

                    norm(0)
                    ffn(0)
                    norm(1)

                    def z_slot(i, s, blocks=2):
                        p = POS_Z + s
                        arrived(p, i)
                        for cc in range(blocks):
                            q = 2 * (s % 4) + cc
                            pe.wait_ge(S["z_ev"], i * 8 + q + 1 + (s // 4) * 8)
                            for k in range(DB):
                                if s == 0 and cc == 0:
                                    pe.wait_ge(S["h"], DB + k + 1)
                                mm = pe.matmul(bank[q][:, 0:T], slot(p)[:, k, cc * 128:cc * 128 + 128], hT[:, k, :],
                                               start=(k == 0), stop=(k == DB - 1))
                            mm.then_inc(S["z_ps"], 1)
                        pe.wait_ge(S["z_ps"], i * 8 + 2 * s + blocks)
                        pe.nop().then_inc(S["col_used"], 1)

                    with pe.Fori(0, NZ // 8) as i:
                        for s in range(4):
                            z_slot(i, s)
                    for s in range(12, 16):
                        z_slot(0, s, 2 if s < 15 else 1)

                    pe.wait_ge(S["lowin"], 1)
                    pe.wait_ge(S["z_ev"], 8 + NZ)
                    low = par[:, PARAMS["low"][0]:PARAMS["low"][0] + 256]
                    for i in range(6):
                        rows = slice(32 * (i // 2 + 1), 32 * (i // 2 + 2))
                        rhs = zT[rows, Z_SMALL, :] if i // 2 == 1 else dz[rows, 0, :]
                        pe.matmul(bank[i][:, 0:T], low[rows, (i % 2) * 128:(i % 2) * 128 + 128], rhs,
                                  start=True, stop=True).then_inc(S["low_ps"], 1)
                    pe.wait_ge(S["ksq"], 1)
                    pe.wait_ge(S["e_low"], 4)
                    for b in range(2):
                        pe.matmul(bank[b][:, 0:T], c("headsum"), bhat[:, b, :], start=True, stop=True)\
                          .then_inc(S["kk_ps"], 1)
                    for b in range(2):
                        pe.wait_ge(S["bonin"], b + 1)
                        pe.matmul(bank[2 + b][:, 0:T], c("headsum"), bon[:, b, :], start=True, stop=True)\
                          .then_inc(S["bon_ps"], 1)
                    pe.wait_ge(S["prods"], 1)
                    pe.wait_ge(S["mixin"], layer * MIXIN_PER_LAYER + 32)
                    for j in range(3):
                        t0, n = TILES[j]
                        for k in range(2):
                            if j:
                                pe.wait_ge(S["trc"], 2 * (j - 1) + k + 1)
                            srcs = ((ar[:, :, 0, :], bhat), (khat, zT[:, Z_V:Z_V + 2, :]))[k]
                            for i in range(4):
                                mm = pe.transpose(bank[k][0:n, 128 * i:128 * i + 128], srcs[i // 2][:, i % 2, t0:t0 + n],
                                                  c("ident"))
                            mm.then_inc(S["tr_ps"], 1)
                    pe.wait_ge(S["trc"], 6)
                    pe.wait_ge(S["bon_ok"], 2)
                    for j in range(3):
                        t0, n = TILES[j]
                        ts_ = slice(t0, t0 + n)
                        for e in range(2):
                            rows = slice(64 * e, 64 * e + 64)
                            if j:
                                pe.wait_ge(S["lvl"], 4 * j)
                            for b in range(2):
                                mm = pe.matmul(bank[3 * e][0:n, 128 * b:128 * b + n], ar[rows, b, 0, ts_],
                                               beta[rows, b, ts_], start=True, stop=True)
                            mm.then_inc(S["mats_ps"], 1)
                            for i, lhs in enumerate((beta, kappa)):
                                for b in range(2):
                                    o = bank[3 * e + 1 + i][0:n, 256 * b:256 * b + 256].rearrange("p (w t) -> p w t", w=2)
                                    mm = pe.matmul(o[:, :, 0:n], lhs[rows, b, ts_], ar[rows, b, :, ts_],
                                                   start=True, stop=True)
                                mm.then_inc(S["mats_ps"], 1)
                        def four(bk, g):
                            return bk[0:n, 128 * g:128 * g + n]
                        pe.wait_ge(S["masks"], 2 * j + 2)
                        for s in range(1, 5):
                            pe.wait_ge(S["lev"], 4 * j + s)
                            for g in range(4):
                                mm = pe.matmul(four(bank[6], g), ml[0:n, g, 0:n], xx[0:n, g, 0:n], start=True, stop=True)
                            mm.then_inc(S["y_ps"], 1)
                            pe.wait_ge(S["ycp"], 4 * j + s)
                            for g in range(4):
                                mm = pe.matmul(four(bank[7], g), tt[0:n, g, 0:n], yy[0:n, g, 0:n], start=True, stop=True)
                            mm.then_inc(S["d_ps"], 1)
                            for g in range(4):
                                mm = pe.matmul(four(bank[0], g), yy[0:n, g, 0:n], tt[0:n, g, 0:n], start=True, stop=True)
                            mm.then_inc(S["d_ps"], 1)
                        pe.wait_ge(S["lvl"], 4 * j + 4)
                        for g in range(4):
                            par_, b = g // 2, g % 2
                            mm = pe.matmul(bank[6][0:n, HD * g:HD * g + HD], bt[0:n, g, 0:n],
                                           tok[0:n, j, 6 + b, 64 * par_:64 * par_ + 64], start=True, stop=True)
                        mm.then_inc(S["bv_ps"], 1)
                        pe.wait_ge(S["bvc"], j + 1)
                        for g in range(4):
                            mm = pe.matmul(bank[6][0:n, HD * g:HD * g + HD], xx[0:n, g, 0:n], bv[0:n, HD * g:HD * g + HD],
                                           start=True, stop=True)
                        mm.then_inc(S["ua_ps"], 1)
                        for g in range(4):
                            par_, b = g // 2, g % 2
                            mm = pe.matmul(bank[7][64 * par_:64 * par_ + 64, 128 * b:128 * b + n],
                                           tok[0:n, j, b, 64 * par_:64 * par_ + 64], xx[0:n, g, 0:n], start=True, stop=True)
                        mm.then_inc(S["ua_ps"], 1)
                        pe.wait_ge(S["uac"], 2 * j + 2)

                    for i in range(NCH):
                        j, q = (i // 4, i % 4) if i < 8 else (2, 0)
                        rows = slice(32 * q, 32 * q + 32)
                        s_at = i if i < 8 else 9
                        if i:
                            pe.wait_ge(S["s_ok"], 2 * i)
                        for g in range(4):
                            hp, b = head_of(g)
                            mm = pe.matmul(bank[g // 2][rows, HD * b:HD * b + HD], atT[hp:hp + 64, b, CH * i:CH * i + CH],
                                           st[hp:hp + 64, s_at, b, :], start=True, stop=True)
                        mm.then_inc(S["u_ps"], 1)
                        for b in range(2):
                            for e in range(2):
                                hs = slice(64 * e, 64 * e + 64)
                                pe.matmul(bank[2 + b][hs, 0:HD], tok[rows, j, 4 + b, hs], tok[rows, j, 6 + b, hs],
                                          start=True, stop=False)
                        pe.wait_ge(S["u_ok"], 2 * i + 2)
                        for b in range(2):
                            for e in range(2):
                                hs = slice(64 * e, 64 * e + 64)
                                g = 2 * e + b
                                mm = pe.matmul(bank[2 + b][hs, 0:HD], tok[rows, j, 2 + b, hs],
                                               u0[rows, j, HD * g:HD * g + HD], start=False, stop=True)
                            mm.then_inc(S["s_ps"], 1)
                    for j in range(3):
                        t0, n = TILES[j]
                        for e in range(2):
                            if j >= 2:
                                pe.wait_ge(S["o_ok"], 2 * (j - 2) + e + 1)
                            hs = slice(64 * e, 64 * e + 64)
                            bk = bank[4 + 2 * (j % 2) + e]
                            for b in range(2):
                                g = 2 * e + b
                                o = bk[hs, 128 * b:128 * b + n]
                                pe.matmul(o, tok[0:n, j, 6 + b, hs], dtm[0:n, j, 128 * g:128 * g + n], start=True, stop=False)
                                for q in range(n // CH):
                                    i = 4 * j + q
                                    pe.matmul(o[:, CH * q:CH * q + CH], st[hs, i if i < 8 else 9, b, :],
                                              ar[hs, b, 1, CH * i:CH * i + CH], start=False, stop=False)
                                mm = pe.matmul(o, u0[0:n, j, HD * g:HD * g + HD], ctm[0:n, j, 128 * g:128 * g + n],
                                               start=False, stop=True)
                            mm.then_inc(S["o_ps"], 1)

                    def head_norm(which, o, sq):
                        pe.wait_ge(S["o_ok"] if which == 0 else S["ro_ok"], 6)
                        for b in range(2):
                            pe.matmul(bank[2 + b][:, 0:T], c("headmean"), o[:, b, :], start=True, stop=True)\
                              .then_inc(S["gn_ps"], 1)
                        pe.wait_ge(S["gn_sq"], 2 * which + 2)
                        for b in range(2):
                            pe.matmul(bank[4 + b][:, 0:T], c("headmean"), sq[:, b, :], start=True, stop=True)\
                              .then_inc(S["gn_ps"], 1)

                    head_norm(0, ow, kappa)

                    pe.wait_ge(S["gn_done"], 1)
                    for b in range(4):
                        pe.matmul(bank[b][:, 0:T], c("rot"), zT[:, Z_TQ + b, :], start=True, stop=True)\
                          .then_inc(S["rot_ps"], 1)
                    pe.wait_ge(S["rotd"], 1)
                    for j in range(3):
                        t0, n = TILES[j]
                        if j:
                            pe.wait_ge(S["rtrc"], j)
                        for i in range(4):
                            src = kdec[:, i, t0:t0 + n] if i < 2 else zT[:, Z_TV + i - 2, t0:t0 + n]
                            mm = pe.transpose(bank[6][0:n, 128 * i:128 * i + 128], src, c("ident"))
                        mm.then_inc(S["rtr_ps"], 1)
                    for j in range(3):
                        t0, n = TILES[j]
                        for e in range(2):
                            if j:
                                pe.wait_ge(S["smd"], 2 * (j - 1) + e + 1)
                            hs = slice(64 * e, 64 * e + 64)
                            for b in range(2):
                                mm = pe.matmul(bank[e][0:n, 128 * b:128 * b + n], zT[hs, Z_TK + b, t0:t0 + n],
                                               zT[hs, Z_TQ + b, t0:t0 + n], start=True, stop=True)
                            mm.then_inc(S["sm_ps"], 1)
                    pe.wait_ge(S["rtrc"], 3)
                    for i in range(5):
                        j, rows = (i // 2, slice(64 * (i % 2), 64 * (i % 2) + 64)) if i < 4 else (2, slice(0, TS))
                        for b in range(2):
                            for e in range(2):
                                s = 128 * (i // 2) + 64 * b
                                fs = slice(128 * b + 64 * e, 128 * b + 64 * e + 64)
                                mm = pe.matmul(bank[2 + i % 2][64 * e:64 * e + 64, s:s + HD], rtok[rows, j, fs],
                                               rtok[rows, j, 256 + fs.start:256 + fs.stop], start=True, stop=True)
                        mm.then_inc(S["kv_ps"], 1)
                    pe.wait_ge(S["smd"], 6)
                    pe.wait_ge(S["rsd"], 8)
                    for j in range(3):
                        t0, n = TILES[j]
                        for e in range(2):
                            if j >= 2:
                                pe.wait_ge(S["ro_ok"], 2 * (j - 2) + e + 1)
                            hs = slice(64 * e, 64 * e + 64)
                            bk = bank[4 + 2 * (j % 2) + e]
                            for b in range(2):
                                g = 2 * e + b
                                o = bk[hs, 128 * b:128 * b + n]
                                pe.matmul(o, rtok[0:n, j, 256 + 128 * b + 64 * e:256 + 128 * b + 64 * e + 64],
                                          smx[0:n, j, 128 * g:128 * g + n], start=True, stop=False)
                                nch = 2 if j < 2 else 1
                                w = n // nch
                                for q in range(nch):
                                    i = 2 * j + q if j < 2 else 5
                                    mm = pe.matmul(o[:, w * q:w * q + w], rst[hs, i, b, :],
                                                   qdec[hs, b, t0 + w * q:t0 + w * q + w], start=False, stop=(q == nch - 1))
                            mm.then_inc(S["ro_ps"], 1)
                    head_norm(1, og, osq)

                    pe.wait_ge(S["gn_done"], 2)
                    for j in range(3):
                        t0, n = TILES[j]
                        if j == 2:
                            pe.wait_ge(S["vtc"], 1)
                        for b in range(4):
                            mm = pe.transpose(bank[6 + j % 2][0:n, 128 * b:128 * b + 128], zT[:, Z_FV + b, t0:t0 + n],
                                              c("ident"))
                        mm.then_inc(S["vt_ps"], 1)
                    pe.wait_ge(S["vtc"], 3)
                    pe.wait_ge(S["fc_ok"], 1)

                    def scores(h):
                        b, hs = h // 2, slice(64 * (h % 2), 64 * (h % 2) + 64)
                        if h >= 2:
                            pe.wait_ge(S["fexp"], 2 * h - 2)
                        for q, k1, at in ((0, 128, 0), (128, 256, 128)):
                            o = bank[h % 2][:, at:at + k1]
                            pe.matmul(o, zT[hs, Z_FQ + b, q:q + 128], zT[hs, Z_FK + b, 0:k1], start=True, stop=False)
                            mm = pe.matmul(o, foxL[:, h, q:q + 128], foxR[:, 0:k1], start=False, stop=True)
                        mm.then_inc(S["fs_ps"], 1)

                    scores(0)
                    for h in range(FOX_H):
                        if h + 1 < FOX_H:
                            scores(h + 1)
                        b, e = h // 2, h % 2
                        hs = slice(64 * e, 64 * e + 64)
                        pe.wait_ge(S["fpn"], h + 1)
                        if h >= 2:
                            pe.wait_ge(S["ftc"], h - 1)
                        for i in range(3):
                            mm = pe.transpose(bank[2 + e][:, 128 * i:128 * i + 128], pq[:, e, 128 * i:128 * i + 128], c("ident"))
                        mm.then_inc(S["ft_ps"], 1)
                        pe.wait_ge(S["ftc"], h + 1)
                        if h >= 4:
                            pe.wait_ge(S["fo_ok"], h - 3)
                        o = bank[4 + b % 2][hs, :]
                        pe.matmul(o[:, 0:256], vtok[:, 0, HD * h:HD * h + HD], pt[:, e, 0:256], start=True, stop=False)
                        pe.matmul(o[:, 128:256], vtok[:, 1, HD * h:HD * h + HD], pt[:, e, 256:384], start=False, stop=True)\
                          .then_inc(S["fo_ps"], 1)
                    pe.wait_ge(S["fexp"], 16)
                    pe.wait_ge(S["ftc"], 8)
                    for g in range(2):
                        hs = slice(64 * g, 64 * g + 64)
                        for i, (k0, k1) in enumerate(((0, PAST), (PAST, PAST + TS))):
                            for b in range(4):
                                o = bank[2 * g + i][TS * b:TS * b + TS, 0:k1 - k0]
                                pe.matmul(o, zT[hs, Z_FQ + b, TP:T], kc[hs, b, k0:k1], start=True, stop=False)
                                mm = pe.matmul(o, foxL[:, 2 * b + g, TP:T], foxR[:, TP + k0:TP + k1], start=False, stop=True)
                        mm.then_inc(S["ss_ps"], 1)
                    pe.wait_ge(S["fo_ok"], 8)
                    for g in range(2):
                        hs = slice(64 * g, 64 * g + 64)
                        pe.wait_ge(S["spn"], g + 1)
                        if g:
                            pe.wait_ge(S["stc"], 2)
                        for i in range(4):
                            mm = pe.transpose(bank[4][:, 128 * i:128 * i + 128], ps_s[:, g, 128 * i:128 * i + 128], c("ident"))
                        mm.then_inc(S["st_ps"], 1)
                        pe.transpose(bank[5][0:TS, 0:128], ps_s[:, g, PAST:], c("ident")).then_inc(S["st_ps"], 1)
                        pe.wait_ge(S["stc"], 2 * g + 2)
                        for b in range(4):
                            h = 2 * b + g
                            o = bank[6 + g][hs, TS * b:TS * b + TS]
                            for i in range(4):
                                pe.matmul(o, vc[:, i, HD * h:HD * h + HD], pt_s[:, g, i, TS * b:TS * b + TS],
                                          start=(i == 0), stop=False)
                            mm = pe.matmul(o, vtok[0:TS, 2, HD * h:HD * h + HD], pt_s[0:TS, g, 4, TS * b:TS * b + TS],
                                           start=False, stop=True)
                        mm.then_inc(S["so_ps"], 1)

                    pe.wait_ge(S["so_ok"], 2)
                    for s in range(4):
                        p = POS_OUT + s
                        arrived(p)
                        for cc in range(2):
                            for k in range(DB):
                                mm = pe.matmul(bank[2 * s + cc][:, 0:T], slot(p)[:, k, cc * 128:cc * 128 + 128],
                                               hT[:, k, :], start=(k == 0), stop=(k == DB - 1))
                            mm.then_inc(S["out_ps"], 1)
                        pe.wait_ge(S["out_ps"], 2 * s + 2)
                        pe.nop().then_inc(S["col_used"], 1)

                    pe.wait_ge(S["x_ready"], 24)
                    norm(2)
                    ffn(1)

                    pe.wait_ge(S["p_in"], layer * P_IN_PER_LAYER + 16)
                    arrived(POS_PROJ)
                    proj = wc[:, POS_PROJ % RING, :].rearrange("p (k n) -> p k n", k=2)
                    for b in range(DB):
                        if b >= 4:
                            pe.wait_ge(S["pj_cp"], b - 3)
                        for k in range(2):
                            mm = pe.matmul(bank[b % 4][:, 0:T], proj[:, k, b * 128:b * 128 + 128], zT[:, 16 + k, :],
                                           start=(k == 0), stop=(k == 1))
                        mm.then_inc(S["pj_ps"], 1)
                    pe.wait_ge(S["pj_ps"], DB)
                    pe.nop().then_inc(S["col_used"], 1)
                    pe.wait_ge(S["x_ready"], 32)
                    for b in range(DB):
                        pe.wait_ge(S["pj_sq"], b + 1)
                        mm = pe.matmul(bank[7][:, 0:T], c("mean"), zT[:, 8 + b, :], start=(b == 0), stop=(b == DB - 1))
                    mm.then_inc(S["norm_ps"], 1)
                    for s in range(4):
                        p = POS_GATE + s
                        arrived(p)
                        for cc in range(2):
                            if 2 * s + cc == 7:
                                pe.wait_ge(S["ln"], 4)
                            for k in range(DB):
                                mm = pe.matmul(bank[2 * s + cc][:, 0:T], slot(p)[:, k, cc * 128:cc * 128 + 128],
                                               xT[:, k, :], start=(k == 0), stop=(k == DB - 1))
                            mm.then_inc(S["g_ps"], 1)

            nc.all_engine_barrier(sems_to_clear=layer_sems)

        with nc.Block() as block:
            @block.scalar
            def _(act):
                for b in range(DB):
                    act.activation(hT[:, b, :], xT[:, b, :], ACT.Square).then_inc(end_sem["sq"], 1)
                act.wait_ge(end_sem["ps"], 1)
                act.activation(rs[:], bank[7][:, 0:T], ACT.Ln, bias=col(C_EPS)).then_inc(end_sem["ln"], 1)
                act.wait_ge(end_sem["ln"], 1)
                act.activation(rs[:], rs[:], ACT.Exp, scale=-0.5).then_inc(end_sem["rs"], 1)

            @block.tensor
            def _(pe):
                for b in range(DB):
                    pe.wait_ge(end_sem["sq"], b + 1)
                    mm = pe.matmul(bank[7][:, 0:T], c("mean"), hT[:, b, :], start=(b == 0), stop=(b == DB - 1))
                mm.then_inc(end_sem["ps"], 1)

            @block.vector
            def _(dve):
                dve.wait_ge(end_sem["rs"], 1)
                for b in range(DB):
                    dve.scalar_tensor_tensor(hT[:, b, :], xT[:, b, :], nf[:, b:b + 1], rs[:], ALU.mult, ALU.mult)\
                       .then_inc(end_sem["y"], 1)

            @block.sync
            def _(sp):
                for b in range(DB):
                    sp.wait_ge(end_sem["y"], b + 1)
                    sp.dma_start(y_out[:, b, :], hT[:, b, :]).then_inc(end_sem["st"], 16)
                sp.wait_ge(end_sem["st"], 16 * DB)


def constants():
    con = np.zeros((P, N_CONST), np.float32)

    def put(name, a):
        at, n = CONSTS[name]
        a = np.asarray(a, np.float64).reshape(a.shape[0], -1)
        assert a.shape[1] == n, (name, a.shape, n)
        con[:a.shape[0], at:at + n] = a

    i = np.arange(P)
    same = (i[:, None] // HD == i[None, :] // HD).astype(np.float64)
    put("ident", np.eye(P))
    put("mean", np.full((P, P), 1.0 / D))
    put("headsum", same)
    put("headmean", same / HD)
    rot = np.zeros((P, P))
    for b in (0, 64):
        for k in range(32):
            rot[b + 32 + k, b + k] = -1.0
            rot[b + k, b + 32 + k] = 1.0
    put("rot", rot)
    pos = np.concatenate([np.arange(TP), PAST + np.arange(TS)]).astype(np.float32)
    inv = (np.float32(1.0) / np.float32(10000.0) ** (np.arange(32, dtype=np.float32) / np.float32(32))).astype(np.float32)
    ang = (pos[None, :] * inv[i % 32][:, None]).astype(np.float32)
    put("cos", np.cos(ang.astype(np.float64)))
    put("sin", np.sin(ang.astype(np.float64)))
    put("causal", np.where(i[:, None] >= i[None, :], 0.0, -1e30))
    k = np.arange(TS)
    put("causal4", np.where((i % TS)[:, None] >= k[None, :], 0.0, -1e30))
    u = i % CH
    chunk = i[:, None] // CH == i[None, :] // CH
    lv = []
    for s in range(5):
        w = 1 << s
        lv.append(chunk & (u[:, None] // (2 * w) == u[None, :] // (2 * w))
                  & (u[:, None] // w % 2 == 1) & (u[None, :] // w % 2 == 0))
    put("levels", np.concatenate(lv, axis=1))
    put("level0T", lv[0].T)
    put("before", chunk & (i[:, None] < i[None, :]))
    put("upto", chunk & (i[:, None] <= i[None, :]))
    put("restart", np.broadcast_to((np.arange(512) % CH != 0).astype(np.float64), (P, 512)))
    logg = np.log(1.0 - 2.0 ** (-5.0 - np.arange(4)))
    order = [2 * (g % 2) + g // 2 for g in range(4)]
    c64 = i[:, None] // 64 == i[None, :] // 64
    put("retmask", np.stack([np.exp(logg[h] * np.abs(i[:, None] - i[None, :])) * c64 * 0.125 for h in order], 1))
    put("retmask_s", np.stack([np.exp(logg[h] * np.abs(k[:, None] - k[None, :])) * 0.125 for h in order], 1))
    tpos = np.concatenate([np.arange(TP) % 64, np.arange(TS)])
    tlen = np.concatenate([np.full(TP, 64), np.full(TS, TS)])
    lg = np.stack([logg[2 * b + i // 64] for b in range(2)], 1)
    put("dquery", np.exp(lg[:, :, None] * (tpos + 1.0)))
    put("dstate", 0.125 * np.exp(lg[:, :, None] * (tlen - 1.0 - tpos)))
    put("dchunk", np.concatenate([np.exp(lg * 64.0), np.exp(lg * TS)], 1))
    put("fox8", 8.0 * np.eye(8))
    cols = np.zeros((P, 8))
    cols[:, C_EPS] = EPS
    cols[:, C_ONE] = 1.0
    cols[:, C_REPS] = RWKV_EPS
    cols[:, C_TEPS] = RET_EPS
    cols[:, C_KKB] = 15.0 * np.log(2.0)
    cols[32:64, C_SMALLSC], cols[96:128, C_SMALLSC] = -2.0, -1.0
    cols[32:64, C_SMALLM], cols[96:128, C_SMALLM] = 2.0, 1.0
    cols[32:64, C_SMALLA] = -1.0
    put("cols", cols)
    return con


def fox_rows():
    return np.ascontiguousarray(np.broadcast_to(-8.0 * np.eye(8, dtype=np.float32)[:, :, None], (8, FOX_H, T)))


def blocked(w, cols):
    L, d, m = w.shape
    return w.reshape(L, d // P, P, m // cols, cols).transpose(0, 3, 2, 1, 4).reshape(L, m // cols, P, -1)


def feature_major(x):
    y = np.moveaxis(x, -1, -2)
    return np.moveaxis(y.reshape(*y.shape[:-2], -1, P, y.shape[-1]), -3, -2)


def by_partition(v):
    return np.swapaxes(v.reshape(v.shape[0], -1, P), 1, 2)


def in_blocks(w):
    out = np.zeros((*w.shape[:-1], 32 * P), w.dtype)
    fox, rw, ret = 0, 2056, 2920

    def put(block, at, n, off=0):
        out[..., block * P + off:block * P + off + n] = w[..., at:at + n]

    put(Z_SMALL, fox + 1536, 8)
    put(Z_SMALL, rw + 256, 32, 32)
    put(Z_SMALL, rw + 800, 32, 64)
    put(Z_SMALL, rw + 832, 32, 96)
    put(Z_R, rw, 256)
    put(Z_K, rw + 288, 256)
    put(Z_V, rw + 544, 256)
    put(Z_TQ, ret, 1024)
    put(Z_FQ, fox, 1536)
    put(Z_FG, fox + 1544, 512)
    return out


def layout(i):
    L = DEPTH
    gate_up = []
    for f in ("1", "2"):
        g, u = blocked(i[f"w_ffn{f}_gate"], 256), blocked(i[f"w_ffn{f}_up"], 256)
        gate_up.append(np.stack([g, u], 2).reshape(L, -1, P, SLOT))
    z = blocked(in_blocks(i["w_in"]), 256)
    proj = i["w_ple_proj"].reshape(L, 2, P, D).transpose(0, 2, 1, 3).reshape(L, 1, P, SLOT)
    wcol = np.concatenate([gate_up[0], z, blocked(i["w_out"], 256), gate_up[1], proj, blocked(i["w_ple_gate"], 256)], 1)
    down = [i[f"w_ffn{f}_down"].reshape(L, DSTEPS, 2, P, 2, 512).transpose(0, 4, 1, 3, 2, 5).reshape(L, 2 * DSTEPS, P, 1024)
            for f in ("1", "2")]
    wdown = np.concatenate(down, 1)
    x = np.concatenate([i["x_prompt"][0], i["x_sample"][0]], 0)
    p = np.concatenate([i["p_prompt"][:, 0], i["p_sample"][:, 0]], 1)
    pr = np.zeros((L, P, N_PARAM), np.float32)

    def put(name, a):
        at, n = PARAMS[name]
        pr[:, :a.shape[1], at:at + n] = a

    def rwkv_row(v):
        full = np.zeros((L, 3944), np.float32)
        full[:, 2056:2920] = v
        return by_partition(in_blocks(full)[:, :7 * P])

    for name, key in (("n1", "norm_ffn1"), ("nm", "norm_mix"), ("n2", "norm_ffn2"), ("pn", "ple_norm"),
                      ("w0", "rwkv_w0"), ("a0", "rwkv_a0"), ("kk", "rwkv_k_k"), ("ka", "rwkv_k_a"),
                      ("lnw", "rwkv_ln_w"), ("lnb", "rwkv_ln_b")):
        put(name, by_partition(i[key]))
    put("rk", by_partition(i["rwkv_r_k"].reshape(L, 256)))
    put("mu", rwkv_row(i["rwkv_mu"]))
    put("prev", rwkv_row(i["state_rwkv_shift"][:, 0, 0]))
    put("bf", i["fox_forget_bias"][:, :, None])
    at = PARAMS["low"][0]
    pr[:, 32:64, at:at + 256] = i["rwkv_w_up"]
    pr[:, 64:96, at:at + 256] = i["rwkv_a_up"]
    pr[:, 96:128, at:at + 256] = i["rwkv_g_up"]

    def states(s):
        s = s.reshape(L, 2, 2, HD, HD).transpose(0, 2, 3, 1, 4).reshape(L, P, 2, HD)
        return np.stack([np.zeros_like(s), s], 1)

    return {
        "wcol": wcol, "wdown": wdown, "x_in": feature_major(x), "p_in": feature_major(p), "consts_in": constants(),
        "params_in": pr, "foxl_in": fox_rows(),
        "kc_in": i["cache_fox_k"][:, 0].reshape(L, PAST, 4, P).transpose(0, 2, 3, 1),
        "vc_in": i["cache_fox_v"][:, 0].reshape(L, 4, P, 512).transpose(0, 2, 1, 3),
        "clf_in": i["cache_fox_logf"][:, 0].transpose(0, 2, 1),
        "srwkv_in": states(i["state_rwkv"][:, 0].transpose(0, 1, 3, 2)), "sret_in": states(i["state_ret"][:, 0]),
        "nf_in": by_partition(i["norm_final"][None])[0],
    }


OUTS = {"y_out": (P, DB, T), "k_out": (DEPTH, 4, P, T), "v_out": (DEPTH, 4, P, T), "logf_out": (DEPTH, 8, T),
        "shift_out": (DEPTH, P, N_SHIFTED, 2), "rwkv_out": (DEPTH, 2, P, 2, HD), "ret_out": (DEPTH, 2, P, 2, HD)}


def unlayout(o):
    L = DEPTH

    def halves(a):
        return a[..., :TP, :], a[..., TP:, :]

    y = o["y_out"].transpose(2, 1, 0).reshape(T, D)
    yp, ys = (a[None] for a in halves(y))
    kp, ks = (a.reshape(L, 1, -1, FOX_H, HD) for a in halves(o["k_out"].transpose(0, 3, 1, 2).reshape(L, T, 512)))
    vp, vs = (a.reshape(L, 1, -1, FOX_H, HD) for a in halves(o["v_out"].transpose(0, 3, 1, 2).reshape(L, T, 512)))
    lp, ls = (a[:, None] for a in halves(o["logf_out"].transpose(0, 2, 1)))
    row = o["shift_out"].transpose(0, 3, 2, 1).reshape(L, 2, 7 * P)
    sh = np.concatenate([row[..., P:3 * P], row[..., 32:64], row[..., 3 * P:7 * P], row[..., 64:128]], -1)

    def states(s):
        return s.reshape(L, 2, 2, HD, 2, HD).transpose(0, 1, 4, 2, 3, 5).reshape(L, 2, 4, HD, HD)

    rw = states(o["rwkv_out"]).transpose(0, 1, 2, 4, 3)
    rt = states(o["ret_out"])
    outs = (yp, ys, kp, vp, lp, rw[:, 0:1], sh[:, 0][:, None, None], rt[:, 0:1],
            ks, vs, ls, rw[:, 1:2], sh[:, 1][:, None, None], rt[:, 1:2])
    return tuple(np.ascontiguousarray(a) for a in outs)


def build(nc, shapes):
    args = {n: nc.dram_tensor(n, s, F32, kind="ExternalInput").ap() for n, s in shapes.items()}
    args |= {n: nc.dram_tensor(n, s, F32, kind="ExternalOutput").ap() for n, s in OUTS.items()}
    program(nc, **args)


def kernel(**inputs):
    from concourse import bacc
    from concourse.bass_utils import run_bass_kernel_spmd as run

    arrays = {n: np.ascontiguousarray(a) for n, a in layout({k: np.asarray(v) for k, v in inputs.items()}).items()}
    nc = bacc.Bacc("TRN2", target_bir_lowering=False, num_devices=1)
    build(nc, {n: a.shape for n, a in arrays.items()})
    r = run(nc, [arrays], core_ids=[0])
    return unlayout({n: r.results[0][n] for n in OUTS})
```

```python
from contextlib import ExitStack

import numpy as np

import concourse.bass as bass
from concourse import mybir

F32 = mybir.dt.float32
ALU = mybir.AluOpType
ACT = mybir.ActivationFunctionType
AX_X = mybir.AxisListType.X

P = 128
DEPTH, D, DFF = 2, 1024, 2816
TP, TS = 256, 32
T = TP + TS
PAST = 512
DB = D // P
FB = DFF // P
HD = 64
FOX_H = 8
EPS = 1e-6
RWKV_EPS = 64e-5
RET_EPS = 1e-6

RING = 4
SLOT = DB * 256
N_FFN_SLOTS = FB
N_Z_SLOTS = 16
POS_FFN = (0, N_FFN_SLOTS + N_Z_SLOTS + 5)
POS_Z = N_FFN_SLOTS
POS_OUT = POS_Z + N_Z_SLOTS
POS_PROJ = POS_OUT + 4
POS_GATE = POS_FFN[1] + N_FFN_SLOTS
N_SLOTS = POS_GATE + 4
DSTEPS = FB // 2
N_DOWN = 4 * DSTEPS

Z_SMALL, Z_R, Z_K, Z_V = 0, 1, 3, 5
Z_TQ, Z_TK, Z_TV, Z_TG = 7, 9, 11, 13
Z_FQ, Z_FK, Z_FV, Z_FG = 15, 19, 23, 27
NZ = 31
N_SHIFTED = 7

TILES = ((0, 128), (128, 128), (256, 32))
CH = 32
NCH = T // CH

CONSTS = {}
_at = 0
for _name, _n in (("ident", 128), ("mean", 128), ("headsum", 128), ("headmean", 128), ("rot", 128),
                  ("cos", T), ("sin", T), ("causal", 128), ("causal4", 32), ("levels", 5 * 128),
                  ("level0T", 128), ("before", 128), ("upto", 128), ("restart", 512), ("retmask", 512),
                  ("retmask_s", 128), ("dquery", 2 * T), ("dstate", 2 * T), ("dchunk", 4),
                  ("fox8", 8), ("cols", 8)):
    CONSTS[_name] = (_at, _n)
    _at += _n
N_CONST = _at
C_EPS, C_ONE, C_REPS, C_TEPS, C_KKB, C_SMALLSC, C_SMALLM, C_SMALLA = range(8)

PARAMS = {}
_at = 0
for _name, _n in (("n1", DB), ("nm", DB), ("n2", DB), ("pn", DB), ("mu", 7), ("prev", 7), ("bf", 1), ("w0", 2),
                  ("a0", 2), ("kk", 2), ("ka", 2), ("rk", 2), ("lnw", 2), ("lnb", 2), ("low", 256)):
    PARAMS[_name] = (_at, _n)
    _at += _n
N_PARAM = _at

Z_BANKS = 4
MATS_ORDER = (0, 2, 1)
LEVEL_BANKS = ((6, 7), (0, 1), (2, 3))
U_AT = (0, 0, 256)

MIXIN_PER_LAYER, ZSTORE_PER_LAYER, SH_OUT_PER_LAYER, P_IN_PER_LAYER = 16 * 10, 16 * 13, 16, 16

KK_SCALE = float(2.0 ** 30)
LOG_DECAY = -float(np.exp(-0.5))


def head_of(g):
    return 64 * (g // 2), g % 2


def program(nc, wcol, wdown, x_in, p_in, consts_in, params_in, foxl_in, kc_in, vc_in, clf_in, srwkv_in, sret_in,
            nf_in, y_out, k_out, v_out, logf_out, shift_out, rwkv_out, ret_out):
    with ExitStack() as ctx:
        def sb(name, *shape):
            return ctx.enter_context(nc.sbuf_tensor(name, list(shape), F32))

        xT = sb("xT", P, DB, T)
        hT = sb("hT", P, DB, T)
        zT = sb("zT", P, NZ, T)
        wc = sb("wc", P, RING, SLOT)
        rs = sb("rs", P, T)
        con = sb("con", P, N_CONST)
        par = sb("par", P, N_PARAM)
        negp = sb("negp", P, 4)
        nf = sb("nf", P, DB)
        foxL = sb("foxL", P, FOX_H, T)
        foxR = sb("foxR", P, TP + PAST + TS)
        ARENA = FB * T + DSTEPS * 1024
        arena = sb("arena", P, ARENA)
        hid = arena[:, 0:FB * T].rearrange("p (c t) -> p c t", c=FB)
        wd = arena[:, FB * T:ARENA].rearrange("p (s k n) -> p s k n", s=DSTEPS, k=2)
        EXTRA = 4480
        extra = sb("extra", P, EXTRA)
        et = sb("et", P, 2, T)

        class Space:

            def __init__(self, t, size):
                self.t, self.size, self.at = t, size, 0

            def take(self, *shape):
                n = int(np.prod(shape))
                v = self.t[:, self.at:self.at + n]
                self.at += n
                assert self.at <= self.size, (self.at, self.size)
                if len(shape) == 2:
                    v = v.rearrange("p (a b) -> p a b", a=shape[0])
                if len(shape) == 3:
                    v = v.rearrange("p (a b c) -> p a b c", a=shape[0], b=shape[1])
                return v

        A = Space(arena, ARENA)
        dz = A.take(N_SHIFTED, T)
        esm = A.take(T)
        sig4 = A.take(4, T)
        gate = A.take(2, T)
        lc = A.take(2, T)
        einc = A.take(2, T)
        einv = A.take(2, T)
        eexc = A.take(2, T)
        eend = A.take(2, T)
        kkf = A.take(2, T)
        bon = A.take(2, T)
        ar = A.take(2, 2, T)
        beta = A.take(2, T)
        bhat = A.take(2, T)
        kappa = A.take(2, T)
        khat = A.take(2, T)
        X = Space(extra, EXTRA)
        tok = X.take(3, 8, 128)
        st = X.take(11, 2, HD)
        M = Space(arena, ARENA)
        M.at = A.at
        u0 = M.take(3, 256)
        mats0 = [M.take(4, 128) for _ in range(2)]
        mats2 = [M.take(4, CH) for _ in range(6)]
        ctm = M.take(3, 512)
        dtm = M.take(3, 512)
        M = Space(dz.rearrange("p a b -> p (a b)"), N_SHIFTED * T)
        mats0 += [M.take(4, 128) for _ in range(3)]

        def over(t):
            return t.rearrange("p a b -> p (a b)")[:, 0:512].rearrange("p (g t) -> p g t", g=4)

        mats0.append(over(sig4[:, 0:2, :]))
        mats1 = [over(t) for t in (sig4[:, 2:4, :], lc, einv, eend, bhat, khat)]
        am, ml, xx, tt, yy, bt = zip(mats0, mats1, mats2)
        atT = eexc
        rott = et
        rgt = (rs[:], esm)
        qdec, kdec = hT[:, 0:2, :], hT[:, 2:4, :]
        R = Space(arena, N_SHIFTED * T + 5 * T)
        rtok = R.take(3, 512)
        smx = R.take(3, 512)
        R = Space(arena, ARENA)
        R.at = A.at + 3 * 256
        rst = R.take(7, 2, HD)
        osq = R.take(2, T)
        assert R.at <= A.at + 3 * 256 + 2 * 512 + 6 * 4 * CH
        og = lc
        F = Space(extra, 3 * 8 * 128)
        cbuf = F.take(TP + PAST + TS)
        clf = F.take(PAST)
        fu = F.take(T)
        fe = F.take(T)
        lgf = F.take(T)
        F = Space(extra, 3 * 8 * 128)
        vtok = F.take(3, 512)
        pt_s = F.take(2, 5, 128)
        F = Space(arena, ARENA)
        F.at = A.at + 3 * 256 + 2 * 512 + 6 * 4 * CH
        pq = F.take(2, 384)
        pt = F.take(2, 384)
        ps_s = F.take(2, PAST + TS)
        fm = F.take(32)
        F = Space(arena, N_SHIFTED * T + 5 * T)
        kc = F.take(4, PAST + TS)
        F = Space(arena, A.at)
        F.at = A.at - 8 * T
        vc = F.take(4, 512)
        fg = zT[:, Z_FG:Z_FG + 4, :]
        shc = sb("shc", P, N_SHIFTED, 2)
        ow = kkf

        squares = (hT, hT, zT[:, 18:26, :])
        ple_in, proj_e, proj_sq, ple_rs = zT[:, 7:9, :], zT[:, 9:17, :], zT[:, 0:8, :], zT[:, 17, :]
        ple_gate = zT[:, 18:26, :]

        bank = [ctx.enter_context(nc.psum_tensor(f"bank{i}", [P, 512], F32)) for i in range(8)]

        def c(name, rows=slice(0, P)):
            a, n = CONSTS[name]
            return con[rows, a:a + n]

        def col(i, rows=slice(0, P)):
            a = CONSTS["cols"][0] + i
            return con[rows, a:a + 1]

        def pa(name, i=0, rows=slice(0, P)):
            a = PARAMS[name][0] + i
            return par[rows, a:a + 1]

        def mats_psum(j, e):
            if j == 2:
                return [bank[6 + e][:, a:a + 128].rearrange("p (g w t) -> p g w t", g=2, w=2) for a in (0, 128, 256)]
            return [bank[3 * e + i][:, :].rearrange("p (g w t) -> p g w t", g=2, w=2) for i in range(3)]

        names = ["col0", "col1", "col2", "col3"] + [f"down{j}" for j in range(DSTEPS)] + """
            down_used down_ps x_ready sq norm_ps ln rstd h gate_ps up_ps exp_ps silu hidden z_ps z_ev
            par_in negp vchain schain sh_cp out_ps
            small e_small lowin low_ps e_low gcp ccs kraw ksq kk_ps kln rn bonin bon_ps bon_ok
            lcs dexc dend exps prods tr_ps trc mats_ps masks xt lev y_ps ycp dx_ps dt_ps lvl bv_ps bvc ua_ps uac
            u_ps u_ok s_ps s_ok o_ps o_ok gn_ps gn_sq gn_ln gn_rs gn_done
            rot_ps rotd decd fred rtr_ps rtrc sm_ps smd kv_ps rsd ro_ps ro_ok rgate
            fu_ok fe_ok fl_ok lgf_ok fc_ok vt_ps vtc fs_ps fmx fexp fpn ft_ps ftc fo_ps fo_ok
            ss_ps smx sexp spn st_ps stc so_ps so_ok kcnew
            mixout pj_ps pj_cp pj_sq pn_ps ple_rs ple_e g_ps g_max g_exp g_t""".split()
        sems = {n: ctx.enter_context(nc.semaphore(n)) for n in names}
        S = sems
        numbers = [s.num for s in sems.values()]
        layer_sems = range(min(numbers), max(numbers) + 1)
        assert len(layer_sems) == len(names)
        for n in ("mixin", "zstore", "sh_out", "p_in"):
            S[n] = ctx.enter_context(nc.semaphore(n))
        start_sem = ctx.enter_context(nc.semaphore("start"))
        clear_sem = ctx.enter_context(nc.semaphore("zeroed"))
        end_sem = {n: ctx.enter_context(nc.semaphore("end_" + n)) for n in ("sq", "ps", "ln", "rs", "y", "st")}

        with nc.Block() as block:
            @block.sync
            def _(sp):
                sp.dma_start(xT[:], x_in).then_inc(start_sem, 16)
                sp.dma_start(con[:], consts_in).then_inc(start_sem, 16)
                sp.dma_start(nf[:], nf_in).then_inc(start_sem, 16)
                sp.wait_ge(clear_sem, 2)
                sp.dma_start(foxL[32:40, :, :], foxl_in).then_inc(start_sem, 16)
                sp.wait_ge(start_sem, 64)

            @block.gpsimd
            def _(pool):
                pool.memset(foxL[:], 0.0).then_inc(clear_sem, 1)
                pool.memset(foxR[:], 0.0).then_inc(clear_sem, 1)
                pool.wait_ge(clear_sem, 2)
                pool.memset(foxR[0:8, :], 1.0).then_inc(clear_sem, 1)

            @block.scalar
            def _(act):
                act.preload_act_table_set("natural_log_exp_and_others")

        with nc.Fori(0, DEPTH) as layer:
            with nc.Block() as block:

                @block.sync
                def _(sp):
                    sp.dma_start(par[:], params_in[layer]).then_inc(S["par_in"], 16)

                    def last_use(p):
                        for f in range(2):
                            s = p - POS_FFN[f]
                            if 0 <= s < N_FFN_SLOTS:
                                return ("gate_ps", "up_ps")[s % 2], FB * f + 2 * (s // 2) + 2
                        if POS_Z <= p < POS_OUT:
                            return "z_ps", min(2 * (p - POS_Z) + 2, NZ)
                        if POS_OUT <= p < POS_OUT + 4:
                            return "out_ps", 2 * (p - POS_OUT) + 2
                        return "pj_ps", DB

                    def load_cols(p0, n):
                        for p in range(p0, p0 + n):
                            if p >= RING:
                                sem, count = last_use(p - RING)
                                sp.wait_ge(S[sem], count)
                            sp.dma_start(wc[:, p % RING, :], wcol[layer, p]).then_inc(S[f"col{p % RING}"], 16)

                    def load_down(f):
                        for j in range(2 * DSTEPS):
                            n = 2 * DSTEPS * f + j
                            if j == 2 * DSTEPS - 1:
                                sp.wait_ge(S["down_ps"], DB * f + 4)
                            elif j >= DSTEPS:
                                sp.wait_ge(S["down_used"], 2 * (DSTEPS - 1) * f + j - DSTEPS + 1)
                            elif f:
                                sp.wait_ge(S["mixout"], 1)
                            sp.dma_start(wd[:, j % DSTEPS].rearrange("p k n -> p (k n)"), wdown[layer, n])\
                              .then_inc(S[f"down{j % DSTEPS}"], 16)

                    load_cols(POS_FFN[0], N_FFN_SLOTS)
                    load_down(0)
                    load_cols(POS_Z, N_Z_SLOTS + 5)
                    load_cols(POS_FFN[1], N_FFN_SLOTS)
                    load_down(1)
                    load_cols(POS_GATE, 4)

                @block.gpsimd
                def _(pool):
                    pool.dma_start(st[:, 0, :, :], srwkv_in[layer, 0]).then_inc(S["mixin"], 16)
                    pool.dma_start(st[:, 9, :, :], srwkv_in[layer, 1]).then_inc(S["mixin"], 16)
                    pool.dma_start(clf[0:8, :], clf_in[layer]).then_inc(S["mixin"], 16)
                    pool.wait_ge(S["lgf_ok"], 1)
                    pool.dma_start(logf_out[layer], lgf[0:8, :]).then_inc(S["zstore"], 16)
                    pool.wait_ge(S["zstore"], layer * ZSTORE_PER_LAYER + 16)
                    pool.wait_ge(S["z_ev"], Z_BANKS + NZ)
                    for b in range(4):
                        pool.dma_start(k_out[layer, b], zT[:, Z_FK + b, :]).then_inc(S["zstore"], 16)
                        pool.dma_start(v_out[layer, b], zT[:, Z_FV + b, :]).then_inc(S["zstore"], 16)
                    pool.wait_ge(S["sh_cp"], 1)
                    pool.dma_start(shift_out[layer], shc[:]).then_inc(S["sh_out"], 16)
                    pool.wait_ge(S["uac"], 6)
                    pool.dma_start(rst[:, 0, :, :], sret_in[layer, 0]).then_inc(S["mixin"], 16)
                    pool.dma_start(rst[:, 5, :, :], sret_in[layer, 1]).then_inc(S["mixin"], 16)
                    pool.wait_ge(S["s_ok"], 18)
                    pool.dma_start(rwkv_out[layer, 0], st[:, 8, :, :]).then_inc(S["zstore"], 16)
                    pool.dma_start(rwkv_out[layer, 1], st[:, 10, :, :]).then_inc(S["zstore"], 16)
                    pool.wait_ge(S["rsd"], 10)
                    pool.dma_start(ret_out[layer, 0], rst[:, 4, :, :]).then_inc(S["zstore"], 16)
                    pool.dma_start(ret_out[layer, 1], rst[:, 6, :, :]).then_inc(S["zstore"], 16)
                    pool.wait_ge(S["gn_done"], 2)
                    for b in range(4):
                        pool.dma_start(kc[:, b, 0:PAST], kc_in[layer, b]).then_inc(S["mixin"], 16)
                    pool.dma_start(vc[:], vc_in[layer]).then_inc(S["mixin"], 16)
                    pool.dma_start(ple_in, p_in[layer]).then_inc(S["p_in"], 16)
                    pool.wait_ge(S["zstore"], layer * ZSTORE_PER_LAYER + 16 * 13)
                    pool.wait_ge(S["sh_out"], layer * SH_OUT_PER_LAYER + 16)
                    pool.wait_ge(S["p_in"], layer * P_IN_PER_LAYER + 16)
                    pool.wait_ge(S["x_ready"], 24)
                    pool.nop().then_inc(S["mixout"], 1)

                @block.scalar
                def _(act):
                    n_chain = [0]

                    def link(ins):
                        n_chain[0] += 1
                        ins.then_inc(S["schain"], 1)
                        act.wait_ge(S["schain"], n_chain[0])

                    def norm(s):
                        for b in range(DB):
                            act.wait_ge(S["x_ready"], 8 * s + b + 1)
                            act.activation(squares[s][:, b, :], xT[:, b, :], ACT.Square).then_inc(S["sq"], 1)
                        act.wait_ge(S["norm_ps"], s + 1)
                        act.activation(rs[:], bank[0][:, 0:T], ACT.Ln, bias=col(C_EPS)).then_inc(S["ln"], 1)
                        act.wait_ge(S["ln"], s + 1)
                        act.activation(rs[:], rs[:], ACT.Exp, scale=-0.5).then_inc(S["rstd"], 1)

                    def ffn(f):
                        def chunk(n, q):
                            act.wait_ge(S["gate_ps"], n + (FB * f + 1))
                            act.wait_ge(S["hidden"], n + (FB * f + 3))
                            act.activation(et[:, q % 2, :], bank[2 * q][:, 0:T], ACT.Exp, scale=-1.0)\
                               .then_inc(S["exp_ps"], 1)
                        with act.Fori(0, FB // 4) as i:
                            for q in range(4):
                                chunk(i * 4 + q, q)
                        for q in range(FB % 4):
                            chunk(FB // 4 * 4 + q, q)

                    norm(0)
                    ffn(0)
                    norm(1)

                    def z_copy(n, q):
                        act.wait_ge(S["z_ps"], n + 1)
                        if isinstance(n, int) and n >= Z_FG:
                            return act.activation(zT[:, n, :], bank[q][:, 0:T], ACT.Exp, scale=-1.0).then_inc(S["z_ev"], 1)
                        return act.activation(zT[:, n, :] if isinstance(n, int) else zT[:, bass.ds(n, 1), :],
                                              bank[q][:, 0:T], ACT.Copy).then_inc(S["z_ev"], 1)
                    with act.Fori(0, 2) as i:
                        for q in range(8):
                            z_copy(i * 8 + q, q % Z_BANKS)

                    def z_slot(s):
                        for n in range(2 * s, min(2 * s + 2, NZ)):
                            z_copy(n, n % Z_BANKS)

                    act.wait_ge(S["small"], N_SHIFTED)
                    act.activation(esm, zT[:, Z_SMALL, :], ACT.Exp, scale=col(C_SMALLSC)).then_inc(S["e_small"], 1)
                    act.wait_ge(S["kraw"], 2)
                    act.activation(bhat, kkf, ACT.Square).then_inc(S["ksq"], 1)
                    act.wait_ge(S["fu_ok"], 1)
                    link(act.activation(fe[0:8, :], fe[0:8, :], ACT.Exp))
                    act.activation(fe[0:8, :], fe[0:8, :], ACT.Ln, bias=col(C_ONE, slice(0, 8))).then_inc(S["fl_ok"], 1)
                    z_slot(8)
                    act.wait_ge(S["negp"], 1)
                    for i in range(4):
                        act.wait_ge(S["low_ps"], i + 1)
                        act.activation(sig4[:, i, :], bank[4 + i][:, 0:T], ACT.Exp, scale=-1.0,
                                       bias=negp[:, i:i + 1]).then_inc(S["e_low"], 1)
                    z_slot(9)
                    for b in range(2):
                        act.wait_ge(S["low_ps"], 5 + b)
                        act.activation(gate[:, b, :], bank[6 + b][:, 0:T], ACT.Copy).then_inc(S["gcp"], 1)
                    for b in range(2):
                        act.activation(rgt[b], zT[:, Z_TG + b, :], ACT.Exp, scale=-1.0).then_inc(S["rgate"], 1)
                    z_slot(10)
                    for b in range(2):
                        act.wait_ge(S["kln"], b + 1)
                        act.wait_ge(S["ksq"], 1)
                        link(act.activation(khat[:, b, :], khat[:, b, :], ACT.Ln, scale=KK_SCALE))
                        act.activation(khat[:, b, :], khat[:, b, :], ACT.Exp, scale=-0.5, bias=col(C_KKB))\
                           .then_inc(S["rn"], 1)
                    z_slot(11)
                    act.wait_ge(S["lcs"], 2)
                    act.activation(einc, lc, ACT.Exp).then_inc(S["exps"], 1)
                    act.activation(einv, lc, ACT.Exp, scale=-1.0).then_inc(S["exps"], 1)
                    act.wait_ge(S["dexc"], 1)
                    act.activation(eexc, eexc, ACT.Exp).then_inc(S["exps"], 1)
                    act.wait_ge(S["dend"], 1)
                    act.activation(eend, eend, ACT.Exp).then_inc(S["exps"], 1)
                    for s in range(12, 16):
                        z_slot(s)
                    act.wait_ge(S["zstore"], layer * ZSTORE_PER_LAYER + 16)
                    for j in range(3):
                        n = TILES[j][1]
                        for k in range(2):
                            act.wait_ge(S["tr_ps"], 2 * j + k + 1)
                            act.activation(tok[0:n, j, 4 * k:4 * k + 4, :].rearrange("p a b -> p (a b)"),
                                           bank[4 + (2 * j + k + 2) % 4][0:n, :], ACT.Copy).then_inc(S["trc"], 1)
                    for j in range(3):
                        n = TILES[j][1]
                        act.wait_ge(S["bv_ps"], 3)
                        act.activation(u0[0:n, j, :], bank[4 + j % 2][0:n, U_AT[j]:U_AT[j] + 256], ACT.Copy)\
                           .then_inc(S["bvc"], 1)
                    for s in range(1, 5):
                        for j in range(3):
                            n = TILES[j][1]
                            act.wait_ge(S["y_ps"], 3 * (s - 1) + j + 1)
                            act.activation(yy[j][0:n, :, 0:n],
                                           bank[LEVEL_BANKS[j][0]][0:n, :].rearrange("p (g t) -> p g t", g=4)[:, :, 0:n],
                                           ACT.Copy).then_inc(S["ycp"], 1)
                    for j in range(3):
                        t0, n = TILES[j]
                        act.wait_ge(S["ua_ps"], 2 * j + 1)
                        act.activation(u0[0:n, j, :], bank[4 + j % 2][0:n, U_AT[j]:U_AT[j] + 256], ACT.Copy)\
                           .then_inc(S["uac"], 1)
                        act.wait_ge(S["ua_ps"], 2 * j + 2)
                        act.activation(atT[:, :, t0:t0 + n],
                                       bank[LEVEL_BANKS[j][0]][:, 0:256].rearrange("p (b t) -> p b t", b=2)[:, :, 0:n],
                                       ACT.Copy).then_inc(S["uac"], 1)

                    for j in range(3):
                        n = TILES[j][1]
                        act.wait_ge(S["rtr_ps"], j + 1)
                        act.activation(rtok[0:n, j, :], bank[6 + j % 2][0:n, :], ACT.Copy).then_inc(S["rtrc"], 1)

                    for j in range(3):
                        n = TILES[j][1]
                        act.wait_ge(S["vt_ps"], j + 1)
                        act.activation(vtok[0:n, j, :], bank[2 + j % 2][0:n, :], ACT.Copy).then_inc(S["vtc"], 1)

                    rs2 = (einv, osq)
                    for which, eps in enumerate((col(C_REPS), col(C_TEPS))):
                        for b in range(2):
                            act.wait_ge(S["gn_ps"], 5 + 2 * which + b)
                            act.activation(rs2[which][:, b, :], bank[4 + 2 * which + b][:, 0:T], ACT.Ln, bias=eps)\
                               .then_inc(S["gn_ln"], 1)
                        act.wait_ge(S["gn_ln"], 2 * which + 2)
                        act.activation(rs2[which], rs2[which], ACT.Exp, scale=-0.5).then_inc(S["gn_rs"], 1)

                    for h in range(FOX_H):
                        act.wait_ge(S["fmx"], h + 1)
                        if h >= 2:
                            act.wait_ge(S["ft_ps"], h - 1)
                        sp_ = bank[h % 2]
                        act.activation(pq[:, h % 2, 0:128], sp_[:, 0:128], ACT.Exp, scale=0.125,
                                       bias=fm[:, 8 + 2 * (h % 2):9 + 2 * (h % 2)],
                                       accum_out=fm[:, 12 + 2 * (h % 2):13 + 2 * (h % 2)]).then_inc(S["fexp"], 1)
                        act.activation(pq[:, h % 2, 128:384], sp_[:, 128:384], ACT.Exp, scale=0.125,
                                       bias=fm[:, 9 + 2 * (h % 2):10 + 2 * (h % 2)],
                                       accum_out=fm[:, 13 + 2 * (h % 2):14 + 2 * (h % 2)]).then_inc(S["fexp"], 1)
                        act.wait_ge(S["ft_ps"], h + 1)
                        if h >= 2:
                            act.wait_ge(S["fo_ps"], h - 1)
                        act.activation(pt[:, h % 2, :], bank[2 + h % 2][:, 0:384], ACT.Copy).then_inc(S["ftc"], 1)
                    for g in range(2):
                        act.wait_ge(S["smx"], g + 1)
                        act.activation(ps_s[:, g, 0:PAST], bank[2 * g][:, :], ACT.Exp, scale=0.125,
                                       bias=fm[:, 20 + g:21 + g], accum_out=fm[:, 22 + g:23 + g]).then_inc(S["sexp"], 1)
                        act.activation(ps_s[:, g, PAST:], ps_s[:, g, PAST:], ACT.Exp, scale=0.125,
                                       bias=fm[:, 20 + g:21 + g], accum_out=fm[:, 24 + g:25 + g]).then_inc(S["sexp"], 1)
                        act.wait_ge(S["st_ps"], 2 * g + 1)
                        act.activation(pt_s[:, g, 0:4, :].rearrange("p a b -> p (a b)"), bank[4][:, :], ACT.Copy)\
                           .then_inc(S["stc"], 1)
                        act.wait_ge(S["st_ps"], 2 * g + 2)
                        act.activation(pt_s[0:TS, g, 4, :], bank[5][0:TS, 0:128], ACT.Copy).then_inc(S["stc"], 1)

                    norm(2)
                    for b in range(DB):
                        act.wait_ge(S["pj_ps"], b + 1)
                        act.activation(proj_e[:, b, :], bank[4 + b % 4][:, 0:T], ACT.Copy).then_inc(S["pj_cp"], 1)
                        act.wait_ge(S["pj_cp"], b + 1)
                        act.activation(proj_sq[:, b, :], proj_e[:, b, :], ACT.Square).then_inc(S["pj_sq"], 1)
                    act.wait_ge(S["pn_ps"], 1)
                    link(act.activation(ple_rs, bank[7][:, 0:T], ACT.Ln, bias=col(C_EPS)))
                    act.activation(ple_rs, ple_rs, ACT.Exp, scale=-0.5).then_inc(S["ple_rs"], 1)
                    ffn(1)

                    for b in range(DB):
                        act.wait_ge(S["g_max"], b + 1)
                        act.activation(ple_gate[:, b, :], ple_gate[:, b, :], ACT.Exp, scale=-1.0).then_inc(S["g_exp"], 1)

                @block.vector
                def _(dve):
                    n_chain = [0]

                    def link(ins):
                        n_chain[0] += 1
                        ins.then_inc(S["vchain"], 1)
                        dve.wait_ge(S["vchain"], n_chain[0])

                    def norm(s, gains):
                        dve.wait_ge(S["rstd"], s + 1)
                        dve.wait_ge(S["x_ready"], 8 * (s + 1))
                        for b in range(DB):
                            dve.scalar_tensor_tensor(hT[:, b, :], xT[:, b, :], pa(gains, b), rs[:],
                                                     ALU.mult, ALU.mult).then_inc(S["h"], 1)

                    def ffn(f):
                        def chunk(n, q):
                            e = et[:, q % 2, :]
                            base = 3 * FB * f
                            dve.wait_ge(S["exp_ps"], n + (FB * f + 1))
                            dve.tensor_scalar(e, e, 1.0, None, ALU.add).then_inc(S["silu"], 1)
                            dve.wait_ge(S["silu"], n * 3 + (base + 1))
                            dve.reciprocal(e, e).then_inc(S["silu"], 1)
                            dve.wait_ge(S["silu"], n * 3 + (base + 2))
                            dve.tensor_tensor(e, e, bank[2 * q][:, 0:T], ALU.mult).then_inc(S["silu"], 1)
                            dve.wait_ge(S["silu"], n * 3 + (base + 3))
                            dve.wait_ge(S["up_ps"], n + (FB * f + 1))
                            dst = hid[:, n, :] if isinstance(n, int) else hid[:, bass.ds(n, 1), :]
                            dve.tensor_tensor(dst, e, bank[2 * q + 1][:, 0:T], ALU.mult).then_inc(S["hidden"], 1)
                        with dve.Fori(0, FB // 4) as i:
                            for q in range(4):
                                chunk(i * 4 + q, q)
                        for q in range(FB % 4):
                            chunk(FB // 4 * 4 + q, q)
                        for b in range(DB):
                            dve.wait_ge(S["down_ps"], DB * f + b + 1)
                            dve.scalar_tensor_tensor(xT[:, b, :], bank[4 + b % 4][:, 0:T], 0.5, xT[:, b, :],
                                                     ALU.mult, ALU.add).then_inc(S["x_ready"], 1)

                    def sigmoid_of(e):
                        link(dve.tensor_scalar(e, e, 1.0, None, ALU.add))
                        link(dve.reciprocal(e, e))

                    dve.nop().then_inc(S["x_ready"], 8)
                    dve.nop().then_inc(S["hidden"], 4)
                    dve.nop().then_inc(S["z_ev"], Z_BANKS)
                    dve.wait_ge(S["par_in"], 16)
                    a = PARAMS["w0"][0]
                    dve.tensor_scalar(negp[:], par[:, a:a + 4], -1.0, None, ALU.mult).then_inc(S["negp"], 1)
                    norm(0, "n1")
                    ffn(0)
                    norm(1, "nm")

                    dve.wait_ge(S["z_ev"], Z_BANKS + N_SHIFTED)
                    zs = zT[:, 0:N_SHIFTED, :]
                    link(dve.tensor_tensor(dz[:, :, 1:T], zs[:, :, 0:T - 1], zs[:, :, 1:T], ALU.subtract))
                    link(dve.tensor_scalar(dz[:, :, 0:1], zs[:, :, 0:1], -1.0, None, ALU.mult))
                    prev = par[:, PARAMS["prev"][0]:PARAMS["prev"][0] + 7].unsqueeze(2)
                    link(dve.tensor_tensor(dz[:, :, TP:TP + 1], prev, zs[:, :, TP:TP + 1], ALU.subtract))
                    link(dve.tensor_copy(shc[:, :, 0:1], zs[:, :, TP - 1:TP]))
                    dve.tensor_copy(shc[:, :, 1:2], zs[:, :, T - 1:T]).then_inc(S["sh_cp"], 1)
                    dve.wait_ge(S["sh_cp"], 1)
                    for b in range(N_SHIFTED):
                        dve.scalar_tensor_tensor(zT[:, b, :], dz[:, b, :], pa("mu", b), zT[:, b, :],
                                                 ALU.mult, ALU.add).then_inc(S["small"], 1)
                    dve.wait_ge(S["small"], N_SHIFTED)
                    dve.wait_ge(S["e_small"], 1)
                    sigmoid_of(esm)
                    dve.tensor_scalar(dz[:, 0, :], esm, col(C_SMALLM), col(C_SMALLA), ALU.mult, ALU.add)\
                       .then_inc(S["lowin"], 1)
                    r, k, v = (zT[:, z:z + 2, :] for z in (Z_R, Z_K, Z_V))
                    for b in range(2):
                        dve.tensor_scalar(kkf[:, b, :], k[:, b, :], pa("kk", b), None, ALU.mult)\
                           .then_inc(S["kraw"], 1)
                    e8 = slice(0, 8)
                    link(dve.tensor_scalar(fu[e8, :], zT[e8, Z_SMALL, :], pa("bf", 0, e8), None, ALU.add))
                    link(dve.tensor_scalar(fe[e8, :], fu[e8, :], -1.0, None, ALU.mult))
                    dve.tensor_tensor(fe[e8, :], fe[e8, :], fu[e8, :], ALU.min).then_inc(S["fu_ok"], 1)
                    dve.wait_ge(S["fl_ok"], 1)
                    dve.scalar_tensor_tensor(lgf[e8, :], fu[e8, :], 0.0, fe[e8, :], ALU.min, ALU.subtract)\
                       .then_inc(S["lgf_ok"], 1)
                    dve.wait_ge(S["lgf_ok"], 1)
                    dve.wait_ge(S["mixin"], layer * MIXIN_PER_LAYER + 48)
                    w = con[e8, CONSTS["fox8"][0]:CONSTS["fox8"][0] + 8]
                    unit = foxR[e8, :]
                    link(dve.tensor_tensor_scan(cbuf[e8, 0:TP], unit[:, 0:TP], lgf[e8, 0:TP], 0.0, ALU.mult, ALU.add))
                    link(dve.tensor_tensor_scan(cbuf[e8, TP:TP + PAST], unit[:, 0:PAST], clf[e8, :], 0.0, ALU.mult, ALU.add))
                    link(dve.tensor_tensor_scan(cbuf[e8, TP + PAST:], unit[:, 0:TS], lgf[e8, TP:T],
                                                cbuf[e8, TP + PAST - 1:TP + PAST], ALU.mult, ALU.add))
                    link(dve.tensor_copy(foxR[32:40, :], cbuf[e8, :]))
                    for q0, k0, n in ((0, 0, TP), (TP, TP + PAST, TS)):
                        dve.tensor_tensor(foxL[e8, :, q0:q0 + n],
                                          cbuf[e8, k0:k0 + n].unsqueeze(1).to_broadcast([8, FOX_H, n]),
                                          w.unsqueeze(2).to_broadcast([8, FOX_H, n]), ALU.mult).then_inc(S["fc_ok"], 1)
                    dve.wait_ge(S["e_low"], 4)
                    sigmoid_of(sig4)
                    lw, aa = sig4[:, 0:2, :], sig4[:, 2:4, :]
                    link(dve.tensor_scalar(lw, lw, LOG_DECAY, None, ALU.mult))
                    for b in range(2):
                        dve.tensor_tensor_scan(lc[:, b, :], c("restart")[:, 0:T], lw[:, b, :], 0.0,
                                               ALU.mult, ALU.add).then_inc(S["lcs"], 1)
                    dve.wait_ge(S["lcs"], 2)
                    dve.tensor_tensor(eexc, lc, lw, ALU.subtract).then_inc(S["dexc"], 1)
                    chunks = lc.rearrange("p b (n u) -> p (b n) u", u=CH)
                    dve.tensor_tensor(eend.rearrange("p b (n u) -> p (b n) u", u=CH),
                                      chunks[:, :, CH - 1:CH].to_broadcast([P, 2 * NCH, CH]), chunks,
                                      ALU.subtract).then_inc(S["dend"], 1)
                    for b in range(2):
                        dve.wait_ge(S["kk_ps"], b + 1)
                        dve.tensor_scalar(khat[:, b, :], bank[4 + b][:, 0:T], 1e-24, None, ALU.max).then_inc(S["kln"], 1)
                    dve.wait_ge(S["rn"], 2)
                    link(dve.tensor_tensor(kkf, kkf, khat, ALU.mult))
                    for b in range(2):
                        link(dve.tensor_scalar(khat[:, b, :], aa[:, b, :], -1.0, pa("ka", b), ALU.add, ALU.mult))
                    link(dve.scalar_tensor_tensor(k, khat, 1.0, k, ALU.add, ALU.mult))
                    for b in range(2):
                        dve.scalar_tensor_tensor(bon[:, b, :], r[:, b, :], pa("rk", b), k[:, b, :],
                                                 ALU.mult, ALU.mult).then_inc(S["bonin"], 1)
                    dve.wait_ge(S["exps"], 4)
                    link(dve.tensor_tensor(aa, kkf, aa, ALU.mult))
                    link(dve.tensor_tensor(ar[:, :, 0, :], kkf, eexc, ALU.mult))
                    link(dve.tensor_tensor(ar[:, :, 1, :], r, einc, ALU.mult))
                    link(dve.scalar_tensor_tensor(beta, aa, -1.0, einv, ALU.mult, ALU.mult))
                    link(dve.scalar_tensor_tensor(bhat, aa, -1.0, eend, ALU.mult, ALU.mult))
                    link(dve.tensor_tensor(kappa, k, einv, ALU.mult))
                    dve.tensor_tensor(khat, k, eend, ALU.mult).then_inc(S["prods"], 1)
                    dve.wait_ge(S["prods"], 1)
                    for b in range(2):
                        dve.wait_ge(S["bon_ps"], b + 1)
                        dve.tensor_tensor(bon[:, b, :], bank[6 + b][:, 0:T], v[:, b, :], ALU.mult).then_inc(S["bon_ok"], 1)

                    for b in range(2):
                        dve.wait_ge(S["rgate"], b + 1)
                        sigmoid_of(rgt[b])
                        link(dve.tensor_tensor(zT[:, Z_TG + b, :], zT[:, Z_TG + b, :], rgt[b], ALU.mult))
                    cos2 = c("cos").unsqueeze(1).to_broadcast([P, 2, T])
                    for w_ in range(2):
                        qk = zT[:, Z_TQ + 2 * w_:Z_TQ + 2 * w_ + 2, :]
                        for b in range(2):
                            dve.wait_ge(S["rot_ps"], 2 * w_ + b + 1)
                            dve.tensor_tensor(rott[:, b, :], bank[4 + b][:, 0:T], c("sin"), ALU.mult).then_inc(S["rotd"], 1)
                        link(dve.tensor_tensor(qk, qk, cos2, ALU.mult))
                        dve.wait_ge(S["rotd"], 2 * w_ + 2)
                        link(dve.tensor_tensor(qk, qk, rott[:], ALU.add))

                    def four(x, j):
                        n = TILES[j][1]
                        return x[j][0:n, :, 0:n]

                    def mask(name, k, j, i=0):
                        n = TILES[j][1]
                        m = c(name)[0:n, i * 128:i * 128 + n]
                        return m.unsqueeze(1).to_broadcast([n, k, n])

                    for o, j in enumerate(MATS_ORDER):
                        n = TILES[j][1]
                        rows = slice(0, n)
                        for par_ in range(2):
                            gs = slice(2 * par_, 2 * par_ + 2)
                            first, second, third = mats_psum(j, par_)
                            dve.wait_ge(S["mats_ps"], 6 * o + 3 * par_ + (3 if j == 2 else 1))
                            dve.tensor_copy(am[j][rows, gs, 0:n], first[rows, :, 0, 0:n]).then_inc(S["masks"], 1)
                            dve.wait_ge(S["mats_ps"], 6 * o + 3 * par_ + 2)
                            dve.tensor_tensor(xx[j][rows, gs, 0:n], second[rows, :, 0, 0:n], mask("level0T", 2, j),
                                              ALU.mult).then_inc(S["masks"], 1)
                            cts = ctm[rows, j, :].rearrange("p (g t) -> p g t", g=4)[:, gs, 0:n]
                            dve.tensor_tensor(cts, second[rows, :, 1, 0:n], mask("upto", 2, j), ALU.mult)\
                               .then_inc(S["masks"], 1)
                            dve.wait_ge(S["mats_ps"], 6 * o + 3 * par_ + 3)
                            dve.tensor_tensor(bt[j][rows, gs, 0:n], third[rows, :, 0, 0:n], mask("before", 2, j),
                                              ALU.mult).then_inc(S["masks"], 1)
                            dts = dtm[rows, j, :].rearrange("p (g t) -> p g t", g=4)[:, gs, 0:n]
                            dve.tensor_tensor(dts, third[rows, :, 1, 0:n], mask("upto", 2, j), ALU.mult)\
                               .then_inc(S["masks"], 1)
                        dve.wait_ge(S["masks"], 10 * (o + 1))
                        link(dve.tensor_tensor(four(tt, j), four(am, j), mask("levels", 4, j, 0), ALU.mult))
                        dve.tensor_tensor(four(xx, j), four(xx, j), mask("ident", 4, j), ALU.add).then_inc(S["xt"], 1)
                        dve.tensor_tensor(four(tt, j), four(tt, j), mask("ident", 4, j), ALU.add).then_inc(S["xt"], 1)
                    for j in range(3):
                        dve.tensor_tensor(four(ml, j), four(am, j), mask("levels", 4, j, 1), ALU.mult).then_inc(S["lev"], 1)
                    dq, ds_ = (c(x).rearrange("p (b t) -> p b t", b=2) for x in ("dquery", "dstate"))
                    dve.wait_ge(S["z_ev"], Z_BANKS + NZ)
                    dve.tensor_tensor(kdec, zT[:, Z_TK:Z_TK + 2, :], ds_, ALU.mult).then_inc(S["decd"], 1)
                    dve.tensor_tensor(qdec, zT[:, Z_TQ:Z_TQ + 2, :], dq, ALU.mult).then_inc(S["decd"], 1)
                    for s in range(1, 5):
                        if s < 4:
                            for j in range(3):
                                dve.wait_ge(S["y_ps"], 3 * (s - 1) + j + 1)
                                dve.tensor_tensor(four(ml, j), four(am, j), mask("levels", 4, j, s + 1), ALU.mult)\
                                   .then_inc(S["lev"], 1)
                        for j in range(3):
                            n = TILES[j][1]
                            d_x, d_t = (bank[q][0:n, :].rearrange("p (g t) -> p g t", g=4)[:, :, 0:n]
                                        for q in LEVEL_BANKS[j][::-1])
                            dve.wait_ge(S["dx_ps"], 3 * (s - 1) + j + 1)
                            dve.tensor_tensor(four(xx, j), four(xx, j), d_x, ALU.add).then_inc(S["lvl"], 1)
                            if s < 4:
                                dve.wait_ge(S["dt_ps"], 3 * (s - 1) + j + 1)
                                dve.tensor_tensor(four(tt, j), four(tt, j), d_t, ALU.add).then_inc(S["lvl"], 1)
                        sigmoid_of(fg[:, s - 1, :])

                    def ret_scores(j):
                        n = TILES[j][1]
                        m = (c("retmask")[0:n, :] if j < 2 else c("retmask_s")[0:n, :]).rearrange("p (g t) -> p g t", g=4)
                        for e in range(2):
                            dve.wait_ge(S["sm_ps"], 2 * j + e + 1)
                            dve.tensor_tensor(smx[0:n, j, :].rearrange("p (g t) -> p g t", g=4)[:, 2 * e:2 * e + 2, 0:n],
                                              bank[4 + e][0:n, 0:256].rearrange("p (g t) -> p g t", g=2)[:, :, 0:n],
                                              m[:, 2 * e:2 * e + 2, :], ALU.mult).then_inc(S["smd"], 1)

                    def ret_state(i):
                        old, new = (i, i + 1) if i < 4 else (5, 6)
                        dch = c("dchunk")
                        dve.wait_ge(S["kv_ps"], 5)
                        if i == 0:
                            dve.wait_ge(S["mixin"], layer * MIXIN_PER_LAYER + 80)
                        if 1 <= i < 4:
                            dve.wait_ge(S["rsd"], 2 * i)
                        for b in range(2):
                            s = 128 * (i // 2) + 64 * b
                            dve.scalar_tensor_tensor(rst[:, new, b, :], rst[:, old, b, :],
                                                     dch[:, 2 * (i // 4) + b:2 * (i // 4) + b + 1],
                                                     bank[6 + i % 2][:, s:s + HD], ALU.mult, ALU.add).then_inc(S["rsd"], 1)

                    with_chunk = {1: [(ret_scores, 0)], 3: [(ret_scores, 1)], 4: [(ret_scores, 2)],
                                  6: [(ret_state, 0), (ret_state, 1)], 7: [(ret_state, 2), (ret_state, 3)],
                                  8: [(ret_state, 4)]}
                    dve.wait_ge(S["uac"], 6)
                    for i in range(NCH):
                        j, q = (i // 4, i % 4) if i < 8 else (2, 0)
                        rows = slice(32 * q, 32 * q + 32)
                        old, new = (i, i + 1) if i < 8 else (9, 10)
                        dve.wait_ge(S["u_ps"], i + 1)
                        for e in range(2):
                            dve.tensor_tensor(u0[rows, j, 128 * e:128 * e + 128], u0[rows, j, 128 * e:128 * e + 128],
                                              bank[e][rows, 0:128], ALU.add).then_inc(S["u_ok"], 1)
                        for b in range(2):
                            dve.wait_ge(S["s_ps"], 2 * i + b + 1)
                            end = CH * (i + 1) - 1
                            dve.scalar_tensor_tensor(st[:, new, b, :], st[:, old, b, :], einc[:, b, end:end + 1],
                                                     bank[2 + b][:, 0:HD], ALU.mult, ALU.add).then_inc(S["s_ok"], 1)
                        for step, which in with_chunk.get(i, ()):
                            step(which)
                    for j in range(3):
                        t0, n = TILES[j]
                        for e in range(2):
                            dve.wait_ge(S["o_ps"], 2 * j + e + 1)
                            rows = slice(64 * e, 64 * e + 64)
                            dve.tensor_copy(ow[rows, :, t0:t0 + n],
                                            bank[4 + 2 * (j % 2) + e][rows, 0:256].rearrange("p (b t) -> p b t", b=2)[:, :, 0:n])\
                               .then_inc(S["o_ok"], 1)

                    for j in range(3):
                        t0, n = TILES[j]
                        for e in range(2):
                            dve.wait_ge(S["ro_ps"], 2 * j + e + 1)
                            rows = slice(64 * e, 64 * e + 64)
                            dve.tensor_copy(og[rows, :, t0:t0 + n],
                                            bank[2 * (j % 2) + e][rows, 0:256].rearrange("p (b t) -> p b t", b=2)[:, :, 0:n])\
                               .then_inc(S["ro_ok"], 1)

                    for which, (o, sq) in enumerate(((ow, kappa), (og, osq))):
                        dve.wait_ge(S["o_ok"] if which == 0 else S["ro_ok"], 6)
                        for b in range(2):
                            dve.wait_ge(S["gn_ps"], 2 * which + 1 + b)
                            link(dve.tensor_tensor(o[:, b, :], o[:, b, :], bank[4 + 2 * which + b][:, 0:T], ALU.subtract))
                        dve.tensor_tensor(sq, o, o, ALU.mult).then_inc(S["gn_sq"], 1)

                    def fox_max(h):
                        e = h % 2
                        sc = bank[e]
                        diag = sc[:, 0:384].rearrange("p (k t) -> p k t", k=3)[:, 0:3:2, :]
                        dve.wait_ge(S["fs_ps"], h + 1)
                        link(dve.tensor_tensor(diag, diag, c("causal").unsqueeze(1).to_broadcast([P, 2, 128]), ALU.add))
                        dve.tensor_reduce(fm[:, 0:1], sc[:, 0:128], AX_X, ALU.max).then_inc(S["fred"], 1)
                        dve.tensor_reduce(fm[:, 1:2], sc[:, 128:384], AX_X, ALU.max).then_inc(S["fred"], 1)
                        dve.wait_ge(S["fred"], 2 * h + 2)
                        dve.tensor_scalar(fm[:, 8 + 2 * e:10 + 2 * e], fm[:, 0:2], -0.125, None, ALU.mult)\
                           .then_inc(S["fmx"], 1)

                    fox_max(0)
                    dve.wait_ge(S["gn_rs"], 1)
                    link(dve.tensor_tensor(ow, ow, einv, ALU.mult))
                    for b in range(2):
                        link(dve.tensor_scalar(ow[:, b, :], ow[:, b, :], pa("lnw", b), pa("lnb", b), ALU.mult, ALU.add))
                    dve.wait_ge(S["bon_ok"], 2)
                    link(dve.tensor_tensor(ow, ow, bon, ALU.add))
                    dve.wait_ge(S["gcp"], 2)
                    dve.tensor_tensor(hT[:, 4:6, :], ow, gate, ALU.mult).then_inc(S["gn_done"], 1)
                    dve.wait_ge(S["gn_rs"], 2)
                    link(dve.tensor_tensor(og, og, osq, ALU.mult))
                    dve.tensor_tensor(hT[:, 6:8, :], og, zT[:, Z_TG:Z_TG + 2, :], ALU.mult).then_inc(S["gn_done"], 1)
                    dve.wait_ge(S["gn_done"], 2)
                    dve.tensor_copy(kc[:, :, PAST:], zT[:, Z_FK:Z_FK + 4, TP:T]).then_inc(S["kcnew"], 1)

                    def fox_out(h):
                        b, e = h // 2, h % 2
                        rows = slice(64 * e, 64 * e + 64)
                        dve.wait_ge(S["fo_ps"], h + 1)
                        dve.tensor_tensor(hT[rows, b, 0:TP], bank[4 + b % 2][rows, 0:TP], fg[rows, b, 0:TP], ALU.mult)\
                           .then_inc(S["fo_ok"], 1)

                    for h in range(FOX_H):
                        b, e = h // 2, h % 2
                        if h + 1 < FOX_H:
                            fox_max(h + 1)
                        dve.wait_ge(S["fexp"], 2 * h + 2)
                        link(dve.reciprocal(fm[:, 16 + 2 * e:18 + 2 * e], fm[:, 12 + 2 * e:14 + 2 * e]))
                        link(dve.tensor_scalar(pq[:, e, 0:128], pq[:, e, 0:128], fm[:, 16 + 2 * e:17 + 2 * e], None, ALU.mult))
                        dve.tensor_scalar(pq[:, e, 128:384], pq[:, e, 128:384], fm[:, 17 + 2 * e:18 + 2 * e], None, ALU.mult)\
                           .then_inc(S["fpn"], 1)
                        if h:
                            fox_out(h - 1)
                    fox_out(FOX_H - 1)
                    for g in range(2):
                        dve.wait_ge(S["ss_ps"], g + 1)
                        link(dve.tensor_tensor(ps_s[:, g, PAST:], bank[2 * g + 1][:, 0:TS], c("causal4"), ALU.add))
                        link(dve.tensor_reduce(fm[:, 26:27], ps_s[:, g, PAST:], AX_X, ALU.max))
                        link(dve.tensor_reduce(fm[:, 27:28], bank[2 * g][:, :], AX_X, ALU.max))
                        link(dve.tensor_tensor(fm[:, 28:29], fm[:, 26:27], fm[:, 27:28], ALU.max))
                        dve.tensor_scalar(fm[:, 20 + g:21 + g], fm[:, 28:29], -0.125, None, ALU.mult).then_inc(S["smx"], 1)
                        dve.wait_ge(S["sexp"], 2 * g + 2)
                        link(dve.tensor_tensor(fm[:, 29:30], fm[:, 22 + g:23 + g], fm[:, 24 + g:25 + g], ALU.add))
                        link(dve.reciprocal(fm[:, 30:31], fm[:, 29:30]))
                        dve.tensor_scalar(ps_s[:, g, :], ps_s[:, g, :], fm[:, 30:31], None, ALU.mult).then_inc(S["spn"], 1)
                    for e in range(2):
                        dve.wait_ge(S["so_ps"], e + 1)
                        rows = slice(64 * e, 64 * e + 64)
                        dve.tensor_tensor(hT[rows, 0:4, TP:T], bank[6 + e][rows, 0:128].rearrange("p (b t) -> p b t", b=4),
                                          fg[rows, :, TP:T], ALU.mult).then_inc(S["so_ok"], 1)

                    for b in range(DB):
                        dve.wait_ge(S["out_ps"], b + 1)
                        dve.tensor_tensor(xT[:, b, :], bank[b][:, 0:T], xT[:, b, :], ALU.add).then_inc(S["x_ready"], 1)

                    norm(2, "n2")
                    ffn(1)

                    dve.wait_ge(S["ple_rs"], 1)
                    for b in range(DB):
                        dve.scalar_tensor_tensor(proj_e[:, b, :], proj_e[:, b, :], pa("pn", b), ple_rs, ALU.mult, ALU.mult)\
                           .then_inc(S["ple_e"], 1)
                    for b in range(DB):
                        dve.wait_ge(S["g_ps"], b + 1)
                        dve.tensor_scalar(ple_gate[:, b, :], bank[b][:, 0:T], -80.0, None, ALU.max).then_inc(S["g_max"], 1)
                        dve.wait_ge(S["g_exp"], b + 1)
                        sigmoid_of(ple_gate[:, b, :])
                        dve.wait_ge(S["ple_e"], b + 1)
                        link(dve.tensor_tensor(proj_e[:, b, :], proj_e[:, b, :], ple_gate[:, b, :], ALU.mult))
                    for b in range(DB):
                        dve.tensor_tensor(xT[:, b, :], xT[:, b, :], proj_e[:, b, :], ALU.add).then_inc(S["x_ready"], 1)

                @block.tensor
                def _(pe):
                    def slot(p):
                        return wc[:, p % RING, :].rearrange("p (k n) -> p k n", k=DB)

                    def norm(s):
                        for b in range(DB):
                            pe.wait_ge(S["sq"], 8 * s + b + 1)
                            mm = pe.matmul(bank[0][:, 0:T], c("mean"), squares[s][:, b, :], start=(b == 0), stop=(b == DB - 1))
                        mm.then_inc(S["norm_ps"], 1)

                    def arrived(p, more=0):
                        pe.wait_ge(S[f"col{p % RING}"], more * 16 + 16 * (p // RING + 1))

                    def ffn(f):
                        p0 = POS_FFN[f]

                        def pair(i, jj):
                            for w in range(2):
                                p = p0 + 2 * jj + w
                                arrived(p, i)
                                for cc in range(2):
                                    q = 2 * jj + cc
                                    if w == 0:
                                        pe.wait_ge(S["hidden"], i * 4 + (FB * f + q + 1))
                                    for k in range(DB):
                                        if jj == 0 and w == 0 and cc == 0:
                                            pe.wait_ge(S["h"], DB * 2 * f + k + 1)
                                        mm = pe.matmul(bank[2 * q + w][:, 0:T], slot(p)[:, k, cc * 128:cc * 128 + 128],
                                                       hT[:, k, :], start=(k == 0), stop=(k == DB - 1))
                                    mm.then_inc(S["up_ps" if w else "gate_ps"], 1)

                        with pe.Fori(0, FB // 4) as i:
                            pair(i, 0)
                            pair(i, 1)
                        pair(FB // 4, 0)
                        pe.wait_ge(S["hidden"], FB * f + 4 + FB // 4 * 4)
                        with pe.Fori(0, 2) as h:
                            pe.wait_ge(S["x_ready"], h * 4 + 8 * (2 * f + 1))
                            for j in range(DSTEPS):
                                pe.wait_ge(S[f"down{j}"], h * 16 + 16 * (2 * f + 1))
                                for kk in range(2):
                                    k = 2 * j + kk
                                    pe.wait_ge(S["hidden"], FB * f + 4 + k + 1)
                                    for m in range(4):
                                        mm = pe.matmul(bank[4 + m][:, 0:T], wd[:, j, kk, m * 128:m * 128 + 128],
                                                       hid[:, k, :], start=(k == 0), stop=(k == FB - 1))
                                        if k == FB - 1:
                                            mm.then_inc(S["down_ps"], 1)
                                        elif kk == 1 and m == 3:
                                            mm.then_inc(S["down_used"], 1)

                    def heads(fn):
                        for g in range(4):
                            fn(g, *head_of(g))

                    norm(0)
                    ffn(0)
                    norm(1)

                    def z_slot(i, s, blocks=2):
                        p = POS_Z + s
                        arrived(p, i)
                        for cc in range(blocks):
                            q = (2 * s + cc) % Z_BANKS
                            pe.wait_ge(S["z_ev"], i * 8 + 2 * s + cc + 1)
                            for k in range(DB):
                                if s == 0 and cc == 0:
                                    pe.wait_ge(S["h"], DB + k + 1)
                                mm = pe.matmul(bank[q][:, 0:T], slot(p)[:, k, cc * 128:cc * 128 + 128], hT[:, k, :],
                                               start=(k == 0), stop=(k == DB - 1))
                            mm.then_inc(S["z_ps"], 1)

                    with pe.Fori(0, 2) as i:
                        for s in range(4):
                            z_slot(i, s)
                    z_slot(0, 8)

                    pe.wait_ge(S["lowin"], 1)
                    low = par[:, PARAMS["low"][0]:PARAMS["low"][0] + 256]
                    def low_rank(i):
                        rows = slice(32 * (i // 2 + 1), 32 * (i // 2 + 2))
                        rhs = zT[rows, Z_SMALL, :] if i // 2 == 1 else dz[rows, 0, :]
                        pe.matmul(bank[4 + i if i < 4 else 2 + i][:, 0:T], low[rows, (i % 2) * 128:(i % 2) * 128 + 128],
                                  rhs, start=True, stop=True).then_inc(S["low_ps"], 1)

                    for i in range(4):
                        low_rank(i)
                    z_slot(0, 9)
                    pe.wait_ge(S["e_low"], 4)
                    for i in range(4, 6):
                        low_rank(i)
                    pe.wait_ge(S["ksq"], 1)
                    for b in range(2):
                        pe.matmul(bank[4 + b][:, 0:T], c("headsum"), bhat[:, b, :], start=True, stop=True)\
                          .then_inc(S["kk_ps"], 1)
                    for s in range(10, 13):
                        z_slot(0, s)

                    def rotate(b):
                        pe.matmul(bank[4 + b % 2][:, 0:T], c("rot"), zT[:, Z_TQ + b, :], start=True, stop=True)\
                          .then_inc(S["rot_ps"], 1)

                    pe.wait_ge(S["kln"], 2)
                    rotate(0)
                    rotate(1)
                    pe.wait_ge(S["gcp"], 2)
                    for b in range(2):
                        pe.wait_ge(S["bonin"], b + 1)
                        pe.matmul(bank[6 + b][:, 0:T], c("headsum"), bon[:, b, :], start=True, stop=True)\
                          .then_inc(S["bon_ps"], 1)
                    for s in range(13, 15):
                        z_slot(0, s)
                    pe.wait_ge(S["prods"], 1)
                    pe.wait_ge(S["mixin"], layer * MIXIN_PER_LAYER + 48)
                    pe.wait_ge(S["bon_ok"], 2)
                    pe.wait_ge(S["rotd"], 2)
                    rotate(2)
                    rotate(3)
                    z_slot(0, 15, 1)
                    for j in range(3):
                        t0, n = TILES[j]
                        for k in range(2):
                            i4 = 2 * j + k
                            if i4 == 2:
                                pe.wait_ge(S["rotd"], 4)
                            if i4 >= 4:
                                pe.wait_ge(S["trc"], i4 - 3)
                            srcs = ((ar[:, :, 0, :], bhat), (khat, zT[:, Z_V:Z_V + 2, :]))[k]
                            for i in range(4):
                                mm = pe.transpose(bank[4 + (2 * j + k + 2) % 4][0:n, 128 * i:128 * i + 128], srcs[i // 2][:, i % 2, t0:t0 + n],
                                                  c("ident"))
                            mm.then_inc(S["tr_ps"], 1)
                    pe.wait_ge(S["trc"], 6)
                    pe.wait_ge(S["z_ev"], Z_BANKS + NZ)
                    for o, j in enumerate(MATS_ORDER):
                        t0, n = TILES[j]
                        ts_ = slice(t0, t0 + n)
                        for e in range(2):
                            rows = slice(64 * e, 64 * e + 64)
                            for i, view in enumerate(mats_psum(j, e)):
                                if o == 2:
                                    pe.wait_ge(S["masks"], 5 * e + (1, 3, 5)[i])
                                for b in range(2):
                                    if i == 0:
                                        mm = pe.matmul(view[0:n, b, 0, 0:n], ar[rows, b, 0, ts_],
                                                       beta[rows, b, ts_], start=True, stop=True)
                                    else:
                                        mm = pe.matmul(view[0:n, b, :, 0:n], (beta, kappa)[i - 1][rows, b, ts_],
                                                       ar[rows, b, :, ts_], start=True, stop=True)
                                mm.then_inc(S["mats_ps"], 1)
                    pe.wait_ge(S["masks"], 30)
                    for j in range(3):
                        n = TILES[j][1]
                        for g in range(4):
                            par_, b = g // 2, g % 2
                            at = U_AT[j] + HD * g
                            mm = pe.matmul(bank[4 + j % 2][0:n, at:at + HD], bt[j][0:n, g, 0:n],
                                           tok[0:n, j, 6 + b, 64 * par_:64 * par_ + 64], start=True, stop=True)
                        mm.then_inc(S["bv_ps"], 1)
                    pe.wait_ge(S["xt"], 6)
                    for s in range(1, 5):
                        for j in range(3):
                            n = TILES[j][1]
                            pe.wait_ge(S["lev"], 3 * (s - 1) + j + 1)
                            if s > 1:
                                pe.wait_ge(S["lvl"], 6 * (s - 2) + 2 * j + 2)
                            for g in range(4):
                                mm = pe.matmul(bank[LEVEL_BANKS[j][0]][0:n, 128 * g:128 * g + n], ml[j][0:n, g, 0:n],
                                               xx[j][0:n, g, 0:n], start=True, stop=True)
                            mm.then_inc(S["y_ps"], 1)
                        for j in range(3):
                            n = TILES[j][1]
                            pe.wait_ge(S["ycp"], 3 * (s - 1) + j + 1)
                            for g in range(4):
                                mm = pe.matmul(bank[LEVEL_BANKS[j][1]][0:n, 128 * g:128 * g + n], tt[j][0:n, g, 0:n],
                                               yy[j][0:n, g, 0:n], start=True, stop=True)
                            mm.then_inc(S["dx_ps"], 1)
                            if s < 4:
                                for g in range(4):
                                    mm = pe.matmul(bank[LEVEL_BANKS[j][0]][0:n, 128 * g:128 * g + n],
                                                   yy[j][0:n, g, 0:n], tt[j][0:n, g, 0:n], start=True, stop=True)
                                mm.then_inc(S["dt_ps"], 1)
                    pe.wait_ge(S["bvc"], 3)
                    for j in range(3):
                        n = TILES[j][1]
                        pe.wait_ge(S["lvl"], 18 + j + 1)
                        if j == 2:
                            pe.wait_ge(S["uac"], 1)
                        for g in range(4):
                            at = U_AT[j] + HD * g
                            mm = pe.matmul(bank[4 + j % 2][0:n, at:at + HD], xx[j][0:n, g, 0:n],
                                           u0[0:n, j, HD * g:HD * g + HD], start=True, stop=True)
                        mm.then_inc(S["ua_ps"], 1)
                        for g in range(4):
                            par_, b = g // 2, g % 2
                            mm = pe.matmul(bank[LEVEL_BANKS[j][0]][64 * par_:64 * par_ + 64, 128 * b:128 * b + n],
                                           tok[0:n, j, b, 64 * par_:64 * par_ + 64], xx[j][0:n, g, 0:n],
                                           start=True, stop=True)
                        mm.then_inc(S["ua_ps"], 1)
                    pe.wait_ge(S["uac"], 6)

                    def ret_tok(j):
                        t0, n = TILES[j]
                        if j == 2:
                            pe.wait_ge(S["rtrc"], 1)
                        pe.wait_ge(S["decd"], 2)
                        for i in range(4):
                            src = kdec[:, i, t0:t0 + n] if i < 2 else zT[:, Z_TV + i - 2, t0:t0 + n]
                            mm = pe.transpose(bank[6 + j % 2][0:n, 128 * i:128 * i + 128], src, c("ident"))
                        mm.then_inc(S["rtr_ps"], 1)

                    def ret_scores(j):
                        t0, n = TILES[j]
                        for e in range(2):
                            if j:
                                pe.wait_ge(S["smd"], 2 * (j - 1) + e + 1)
                            hs = slice(64 * e, 64 * e + 64)
                            for b in range(2):
                                mm = pe.matmul(bank[4 + e][0:n, 128 * b:128 * b + n], zT[hs, Z_TK + b, t0:t0 + n],
                                               zT[hs, Z_TQ + b, t0:t0 + n], start=True, stop=True)
                            mm.then_inc(S["sm_ps"], 1)

                    def ret_kv(i):
                        j, rows = (i // 2, slice(64 * (i % 2), 64 * (i % 2) + 64)) if i < 4 else (2, slice(0, TS))
                        if i == 0:
                            pe.wait_ge(S["rtrc"], 3)
                        for b in range(2):
                            for e in range(2):
                                s = 128 * (i // 2) + 64 * b
                                fs = slice(128 * b + 64 * e, 128 * b + 64 * e + 64)
                                mm = pe.matmul(bank[6 + i % 2][64 * e:64 * e + 64, s:s + HD], rtok[rows, j, fs],
                                               rtok[rows, j, 256 + fs.start:256 + fs.stop], start=True, stop=True)
                        mm.then_inc(S["kv_ps"], 1)

                    with_chunk = {0: [(ret_tok, 0)], 1: [(ret_scores, 0)], 2: [(ret_tok, 1)], 3: [(ret_scores, 1)],
                                  4: [(ret_tok, 2), (ret_scores, 2)], 5: [(ret_kv, 0), (ret_kv, 1), (ret_kv, 2)],
                                  6: [(ret_kv, 3), (ret_kv, 4)]}
                    for i in range(NCH):
                        j, q = (i // 4, i % 4) if i < 8 else (2, 0)
                        rows = slice(32 * q, 32 * q + 32)
                        s_at = i if i < 8 else 9
                        if i:
                            pe.wait_ge(S["s_ok"], 2 * i)
                        for g in range(4):
                            hp, b = head_of(g)
                            mm = pe.matmul(bank[g // 2][rows, HD * b:HD * b + HD], atT[hp:hp + 64, b, CH * i:CH * i + CH],
                                           st[hp:hp + 64, s_at, b, :], start=True, stop=True)
                        mm.then_inc(S["u_ps"], 1)
                        for b in range(2):
                            for e in range(2):
                                hs = slice(64 * e, 64 * e + 64)
                                pe.matmul(bank[2 + b][hs, 0:HD], tok[rows, j, 4 + b, hs], tok[rows, j, 6 + b, hs],
                                          start=True, stop=False)
                        pe.wait_ge(S["u_ok"], 2 * i + 2)
                        for b in range(2):
                            for e in range(2):
                                hs = slice(64 * e, 64 * e + 64)
                                g = 2 * e + b
                                mm = pe.matmul(bank[2 + b][hs, 0:HD], tok[rows, j, 2 + b, hs],
                                               u0[rows, j, HD * g:HD * g + HD], start=False, stop=True)
                            mm.then_inc(S["s_ps"], 1)
                        for step, which in with_chunk.get(i, ()):
                            step(which)
                    pe.wait_ge(S["rsd"], 10)
                    pe.wait_ge(S["smd"], 6)
                    for j in range(3):
                        t0, n = TILES[j]
                        for e in range(2):
                            if j >= 2:
                                pe.wait_ge(S["o_ok"], 2 * (j - 2) + e + 1)
                            hs = slice(64 * e, 64 * e + 64)
                            bk = bank[4 + 2 * (j % 2) + e]
                            for b in range(2):
                                g = 2 * e + b
                                o = bk[hs, 128 * b:128 * b + n]
                                pe.matmul(o, tok[0:n, j, 6 + b, hs], dtm[0:n, j, 128 * g:128 * g + n], start=True, stop=False)
                                for q in range(n // CH):
                                    i = 4 * j + q
                                    pe.matmul(o[:, CH * q:CH * q + CH], st[hs, i if i < 8 else 9, b, :],
                                              ar[hs, b, 1, CH * i:CH * i + CH], start=False, stop=False)
                                mm = pe.matmul(o, u0[0:n, j, HD * g:HD * g + HD], ctm[0:n, j, 128 * g:128 * g + n],
                                               start=False, stop=True)
                            mm.then_inc(S["o_ps"], 1)

                    for j in range(3):
                        t0, n = TILES[j]
                        for e in range(2):
                            if j >= 2:
                                pe.wait_ge(S["ro_ok"], 2 * (j - 2) + e + 1)
                            hs = slice(64 * e, 64 * e + 64)
                            bk = bank[2 * (j % 2) + e]
                            for b in range(2):
                                g = 2 * e + b
                                o = bk[hs, 128 * b:128 * b + n]
                                pe.matmul(o, rtok[0:n, j, 256 + 128 * b + 64 * e:256 + 128 * b + 64 * e + 64],
                                          smx[0:n, j, 128 * g:128 * g + n], start=True, stop=False)
                                nch = 2 if j < 2 else 1
                                w = n // nch
                                for q in range(nch):
                                    i = 2 * j + q if j < 2 else 5
                                    mm = pe.matmul(o[:, w * q:w * q + w], rst[hs, i, b, :],
                                                   qdec[hs, b, t0 + w * q:t0 + w * q + w], start=False, stop=(q == nch - 1))
                            mm.then_inc(S["ro_ps"], 1)
                    def head_sums(which, src):
                        for b in range(2):
                            pe.matmul(bank[4 + 2 * which + b][:, 0:T], c("headmean"), src[:, b, :], start=True, stop=True)\
                              .then_inc(S["gn_ps"], 1)

                    pe.wait_ge(S["o_ok"], 6)
                    head_sums(0, ow)
                    pe.wait_ge(S["ro_ok"], 6)
                    head_sums(1, og)
                    for j in range(3):
                        t0, n = TILES[j]
                        if j == 2:
                            pe.wait_ge(S["vtc"], 1)
                        for b in range(4):
                            mm = pe.transpose(bank[2 + j % 2][0:n, 128 * b:128 * b + 128], zT[:, Z_FV + b, t0:t0 + n],
                                              c("ident"))
                        mm.then_inc(S["vt_ps"], 1)
                    pe.wait_ge(S["fc_ok"], 2)

                    def scores(h):
                        b, hs = h // 2, slice(64 * (h % 2), 64 * (h % 2) + 64)
                        if h >= 2:
                            pe.wait_ge(S["fexp"], 2 * h - 2)
                        for q, k1, at in ((0, 128, 0), (128, 256, 128)):
                            o = bank[h % 2][:, at:at + k1]
                            pe.matmul(o, zT[hs, Z_FQ + b, q:q + 128], zT[hs, Z_FK + b, 0:k1], start=True, stop=False)
                            mm = pe.matmul(o, foxL[:, h, q:q + 128], foxR[:, 0:k1], start=False, stop=True)
                        mm.then_inc(S["fs_ps"], 1)

                    for which, sq in enumerate((kappa, osq)):
                        pe.wait_ge(S["gn_sq"], which + 1)
                        head_sums(which, sq)
                        scores(which)
                    pe.wait_ge(S["vtc"], 3)
                    for h in range(FOX_H):
                        b, e = h // 2, h % 2
                        hs = slice(64 * e, 64 * e + 64)
                        if h == FOX_H - 1:
                            pe.wait_ge(S["mixin"], layer * MIXIN_PER_LAYER + 160)
                        pe.wait_ge(S["fpn"], h + 1)
                        if h >= 2:
                            pe.wait_ge(S["ftc"], h - 1)
                        for i in range(3):
                            mm = pe.transpose(bank[2 + e][:, 128 * i:128 * i + 128], pq[:, e, 128 * i:128 * i + 128], c("ident"))
                        mm.then_inc(S["ft_ps"], 1)
                        if h + 2 < FOX_H:
                            scores(h + 2)
                        if h == 0:
                            pe.wait_ge(S["gn_ln"], 4)
                        pe.wait_ge(S["ftc"], h + 1)
                        if h >= 4:
                            pe.wait_ge(S["fo_ok"], h - 3)
                        o = bank[4 + b % 2][hs, :]
                        pe.matmul(o[:, 0:256], vtok[:, 0, HD * h:HD * h + HD], pt[:, e, 0:256], start=True, stop=False)
                        pe.matmul(o[:, 128:256], vtok[:, 1, HD * h:HD * h + HD], pt[:, e, 256:384], start=False, stop=True)\
                          .then_inc(S["fo_ps"], 1)
                    pe.wait_ge(S["fexp"], 16)
                    pe.wait_ge(S["ftc"], 8)
                    pe.wait_ge(S["kcnew"], 1)
                    for g in range(2):
                        hs = slice(64 * g, 64 * g + 64)
                        for i, (k0, k1) in enumerate(((0, PAST), (PAST, PAST + TS))):
                            for b in range(4):
                                o = bank[2 * g + i][TS * b:TS * b + TS, 0:k1 - k0]
                                pe.matmul(o, zT[hs, Z_FQ + b, TP:T], kc[hs, b, k0:k1], start=True, stop=False)
                                mm = pe.matmul(o, foxL[:, 2 * b + g, TP:T], foxR[:, TP + k0:TP + k1], start=False, stop=True)
                        mm.then_inc(S["ss_ps"], 1)
                    pe.wait_ge(S["fo_ok"], 8)
                    for g in range(2):
                        hs = slice(64 * g, 64 * g + 64)
                        pe.wait_ge(S["spn"], g + 1)
                        if g:
                            pe.wait_ge(S["stc"], 2)
                        for i in range(4):
                            mm = pe.transpose(bank[4][:, 128 * i:128 * i + 128], ps_s[:, g, 128 * i:128 * i + 128], c("ident"))
                        mm.then_inc(S["st_ps"], 1)
                        pe.transpose(bank[5][0:TS, 0:128], ps_s[:, g, PAST:], c("ident")).then_inc(S["st_ps"], 1)
                        pe.wait_ge(S["stc"], 2 * g + 2)
                        for b in range(4):
                            h = 2 * b + g
                            o = bank[6 + g][hs, TS * b:TS * b + TS]
                            for i in range(4):
                                pe.matmul(o, vc[:, i, HD * h:HD * h + HD], pt_s[:, g, i, TS * b:TS * b + TS],
                                          start=(i == 0), stop=False)
                            mm = pe.matmul(o, vtok[0:TS, 2, HD * h:HD * h + HD], pt_s[0:TS, g, 4, TS * b:TS * b + TS],
                                           start=False, stop=True)
                        mm.then_inc(S["so_ps"], 1)

                    pe.wait_ge(S["so_ok"], 2)
                    for s in range(4):
                        p = POS_OUT + s
                        arrived(p)
                        for cc in range(2):
                            for k in range(DB):
                                mm = pe.matmul(bank[2 * s + cc][:, 0:T], slot(p)[:, k, cc * 128:cc * 128 + 128],
                                               hT[:, k, :], start=(k == 0), stop=(k == DB - 1))
                            mm.then_inc(S["out_ps"], 1)

                    norm(2)

                    pe.wait_ge(S["x_ready"], 24)
                    pe.wait_ge(S["p_in"], layer * P_IN_PER_LAYER + 16)
                    arrived(POS_PROJ)
                    proj = wc[:, POS_PROJ % RING, :].rearrange("p (k n) -> p k n", k=2)
                    for b in range(DB):
                        if b >= 4:
                            pe.wait_ge(S["pj_cp"], b - 3)
                        for k in range(2):
                            mm = pe.matmul(bank[4 + b % 4][:, 0:T], proj[:, k, b * 128:b * 128 + 128], ple_in[:, k, :],
                                           start=(k == 0), stop=(k == 1))
                        mm.then_inc(S["pj_ps"], 1)
                    pe.wait_ge(S["pj_cp"], DB)
                    for b in range(DB):
                        pe.wait_ge(S["pj_sq"], b + 1)
                        mm = pe.matmul(bank[7][:, 0:T], c("mean"), proj_sq[:, b, :], start=(b == 0), stop=(b == DB - 1))
                    mm.then_inc(S["pn_ps"], 1)
                    pe.wait_ge(S["ple_rs"], 1)
                    ffn(1)

                    pe.wait_ge(S["x_ready"], 32)
                    for s in range(4):
                        p = POS_GATE + s
                        arrived(p)
                        for cc in range(2):
                            for k in range(DB):
                                mm = pe.matmul(bank[2 * s + cc][:, 0:T], slot(p)[:, k, cc * 128:cc * 128 + 128],
                                               xT[:, k, :], start=(k == 0), stop=(k == DB - 1))
                            mm.then_inc(S["g_ps"], 1)

            nc.all_engine_barrier(sems_to_clear=layer_sems)

        with nc.Block() as block:
            @block.scalar
            def _(act):
                for b in range(DB):
                    act.activation(hT[:, b, :], xT[:, b, :], ACT.Square).then_inc(end_sem["sq"], 1)
                act.wait_ge(end_sem["ps"], 1)
                act.activation(rs[:], bank[7][:, 0:T], ACT.Ln, bias=col(C_EPS)).then_inc(end_sem["ln"], 1)
                act.wait_ge(end_sem["ln"], 1)
                act.activation(rs[:], rs[:], ACT.Exp, scale=-0.5).then_inc(end_sem["rs"], 1)

            @block.tensor
            def _(pe):
                for b in range(DB):
                    pe.wait_ge(end_sem["sq"], b + 1)
                    mm = pe.matmul(bank[7][:, 0:T], c("mean"), hT[:, b, :], start=(b == 0), stop=(b == DB - 1))
                mm.then_inc(end_sem["ps"], 1)

            @block.vector
            def _(dve):
                dve.wait_ge(end_sem["rs"], 1)
                for b in range(DB):
                    dve.scalar_tensor_tensor(hT[:, b, :], xT[:, b, :], nf[:, b:b + 1], rs[:], ALU.mult, ALU.mult)\
                       .then_inc(end_sem["y"], 1)

            @block.sync
            def _(sp):
                for b in range(DB):
                    sp.wait_ge(end_sem["y"], b + 1)
                    sp.dma_start(y_out[:, b, :], hT[:, b, :]).then_inc(end_sem["st"], 16)
                sp.wait_ge(end_sem["st"], 16 * DB)


def constants():
    con = np.zeros((P, N_CONST), np.float32)

    def put(name, a):
        at, n = CONSTS[name]
        a = np.asarray(a, np.float64).reshape(a.shape[0], -1)
        assert a.shape[1] == n, (name, a.shape, n)
        con[:a.shape[0], at:at + n] = a

    i = np.arange(P)
    same = (i[:, None] // HD == i[None, :] // HD).astype(np.float64)
    put("ident", np.eye(P))
    put("mean", np.full((P, P), 1.0 / D))
    put("headsum", same)
    put("headmean", same / HD)
    rot = np.zeros((P, P))
    for b in (0, 64):
        for k in range(32):
            rot[b + 32 + k, b + k] = -1.0
            rot[b + k, b + 32 + k] = 1.0
    put("rot", rot)
    pos = np.concatenate([np.arange(TP), PAST + np.arange(TS)]).astype(np.float32)
    inv = (np.float32(1.0) / np.float32(10000.0) ** (np.arange(32, dtype=np.float32) / np.float32(32))).astype(np.float32)
    ang = (pos[None, :] * inv[i % 32][:, None]).astype(np.float32)
    put("cos", np.cos(ang.astype(np.float64)))
    put("sin", np.sin(ang.astype(np.float64)))
    put("causal", np.where(i[:, None] >= i[None, :], 0.0, -1e30))
    k = np.arange(TS)
    put("causal4", np.where((i % TS)[:, None] >= k[None, :], 0.0, -1e30))
    u = i % CH
    chunk = i[:, None] // CH == i[None, :] // CH
    lv = []
    for s in range(5):
        w = 1 << s
        lv.append(chunk & (u[:, None] // (2 * w) == u[None, :] // (2 * w))
                  & (u[:, None] // w % 2 == 1) & (u[None, :] // w % 2 == 0))
    put("levels", np.concatenate(lv, axis=1))
    put("level0T", lv[0].T)
    put("before", chunk & (i[:, None] < i[None, :]))
    put("upto", chunk & (i[:, None] <= i[None, :]))
    put("restart", np.broadcast_to((np.arange(512) % CH != 0).astype(np.float64), (P, 512)))
    logg = np.log(1.0 - 2.0 ** (-5.0 - np.arange(4)))
    order = [2 * (g % 2) + g // 2 for g in range(4)]
    c64 = i[:, None] // 64 == i[None, :] // 64
    put("retmask", np.stack([np.exp(logg[h] * np.abs(i[:, None] - i[None, :])) * c64 * 0.125 for h in order], 1))
    put("retmask_s", np.stack([np.exp(logg[h] * np.abs(k[:, None] - k[None, :])) * 0.125 for h in order], 1))
    tpos = np.concatenate([np.arange(TP) % 64, np.arange(TS)])
    tlen = np.concatenate([np.full(TP, 64), np.full(TS, TS)])
    lg = np.stack([logg[2 * b + i // 64] for b in range(2)], 1)
    put("dquery", np.exp(lg[:, :, None] * (tpos + 1.0)))
    put("dstate", 0.125 * np.exp(lg[:, :, None] * (tlen - 1.0 - tpos)))
    put("dchunk", np.concatenate([np.exp(lg * 64.0), np.exp(lg * TS)], 1))
    put("fox8", 8.0 * np.eye(8))
    cols = np.zeros((P, 8))
    cols[:, C_EPS] = EPS
    cols[:, C_ONE] = 1.0
    cols[:, C_REPS] = RWKV_EPS
    cols[:, C_TEPS] = RET_EPS
    cols[:, C_KKB] = 15.0 * np.log(2.0)
    cols[32:64, C_SMALLSC], cols[96:128, C_SMALLSC] = -2.0, -1.0
    cols[32:64, C_SMALLM], cols[96:128, C_SMALLM] = 2.0, 1.0
    cols[32:64, C_SMALLA] = -1.0
    put("cols", cols)
    return con


def fox_rows():
    return np.ascontiguousarray(np.broadcast_to(-8.0 * np.eye(8, dtype=np.float32)[:, :, None], (8, FOX_H, T)))


def blocked(w, cols):
    L, d, m = w.shape
    return w.reshape(L, d // P, P, m // cols, cols).transpose(0, 3, 2, 1, 4).reshape(L, m // cols, P, -1)


def feature_major(x):
    y = np.moveaxis(x, -1, -2)
    return np.moveaxis(y.reshape(*y.shape[:-2], -1, P, y.shape[-1]), -3, -2)


def by_partition(v):
    return np.swapaxes(v.reshape(v.shape[0], -1, P), 1, 2)


def in_blocks(w):
    out = np.zeros((*w.shape[:-1], 32 * P), w.dtype)
    fox, rw, ret = 0, 2056, 2920

    def put(block, at, n, off=0):
        out[..., block * P + off:block * P + off + n] = w[..., at:at + n]

    put(Z_SMALL, fox + 1536, 8)
    put(Z_SMALL, rw + 256, 32, 32)
    put(Z_SMALL, rw + 800, 32, 64)
    put(Z_SMALL, rw + 832, 32, 96)
    put(Z_R, rw, 256)
    put(Z_K, rw + 288, 256)
    put(Z_V, rw + 544, 256)
    put(Z_TQ, ret, 1024)
    put(Z_FQ, fox, 1536)
    put(Z_FG, fox + 1544, 512)
    return out


def layout(i):
    L = DEPTH
    gate_up = []
    for f in ("1", "2"):
        g, u = blocked(i[f"w_ffn{f}_gate"], 256), blocked(i[f"w_ffn{f}_up"], 256)
        gate_up.append(np.stack([g, u], 2).reshape(L, -1, P, SLOT))
    z = blocked(in_blocks(i["w_in"]), 256)
    proj = i["w_ple_proj"].reshape(L, 2, P, D).transpose(0, 2, 1, 3).reshape(L, 1, P, SLOT)
    wcol = np.concatenate([gate_up[0], z, blocked(i["w_out"], 256), proj, gate_up[1], blocked(i["w_ple_gate"], 256)], 1)
    down = [i[f"w_ffn{f}_down"].reshape(L, DSTEPS, 2, P, 2, 512).transpose(0, 4, 1, 3, 2, 5).reshape(L, 2 * DSTEPS, P, 1024)
            for f in ("1", "2")]
    wdown = np.concatenate(down, 1)
    x = np.concatenate([i["x_prompt"][0], i["x_sample"][0]], 0)
    p = np.concatenate([i["p_prompt"][:, 0], i["p_sample"][:, 0]], 1)
    pr = np.zeros((L, P, N_PARAM), np.float32)

    def put(name, a):
        at, n = PARAMS[name]
        pr[:, :a.shape[1], at:at + n] = a

    def rwkv_row(v):
        full = np.zeros((L, 3944), np.float32)
        full[:, 2056:2920] = v
        return by_partition(in_blocks(full)[:, :7 * P])

    for name, key in (("n1", "norm_ffn1"), ("nm", "norm_mix"), ("n2", "norm_ffn2"), ("pn", "ple_norm"),
                      ("w0", "rwkv_w0"), ("a0", "rwkv_a0"), ("kk", "rwkv_k_k"), ("ka", "rwkv_k_a"),
                      ("lnw", "rwkv_ln_w"), ("lnb", "rwkv_ln_b")):
        put(name, by_partition(i[key]))
    put("rk", by_partition(i["rwkv_r_k"].reshape(L, 256)))
    put("mu", rwkv_row(i["rwkv_mu"]))
    put("prev", rwkv_row(i["state_rwkv_shift"][:, 0, 0]))
    put("bf", i["fox_forget_bias"][:, :, None])
    at = PARAMS["low"][0]
    pr[:, 32:64, at:at + 256] = i["rwkv_w_up"]
    pr[:, 64:96, at:at + 256] = i["rwkv_a_up"]
    pr[:, 96:128, at:at + 256] = i["rwkv_g_up"]

    def states(s):
        s = s.reshape(L, 2, 2, HD, HD).transpose(0, 2, 3, 1, 4).reshape(L, P, 2, HD)
        return np.stack([np.zeros_like(s), s], 1)

    return {
        "wcol": wcol, "wdown": wdown, "x_in": feature_major(x), "p_in": feature_major(p), "consts_in": constants(),
        "params_in": pr, "foxl_in": fox_rows(),
        "kc_in": i["cache_fox_k"][:, 0].reshape(L, PAST, 4, P).transpose(0, 2, 3, 1),
        "vc_in": i["cache_fox_v"][:, 0].reshape(L, 4, P, 512).transpose(0, 2, 1, 3),
        "clf_in": i["cache_fox_logf"][:, 0].transpose(0, 2, 1),
        "srwkv_in": states(i["state_rwkv"][:, 0].transpose(0, 1, 3, 2)), "sret_in": states(i["state_ret"][:, 0]),
        "nf_in": by_partition(i["norm_final"][None])[0],
    }


OUTS = {"y_out": (P, DB, T), "k_out": (DEPTH, 4, P, T), "v_out": (DEPTH, 4, P, T), "logf_out": (DEPTH, 8, T),
        "shift_out": (DEPTH, P, N_SHIFTED, 2), "rwkv_out": (DEPTH, 2, P, 2, HD), "ret_out": (DEPTH, 2, P, 2, HD)}


def unlayout(o):
    L = DEPTH

    def halves(a):
        return a[..., :TP, :], a[..., TP:, :]

    y = o["y_out"].transpose(2, 1, 0).reshape(T, D)
    yp, ys = (a[None] for a in halves(y))
    kp, ks = (a.reshape(L, 1, -1, FOX_H, HD) for a in halves(o["k_out"].transpose(0, 3, 1, 2).reshape(L, T, 512)))
    vp, vs = (a.reshape(L, 1, -1, FOX_H, HD) for a in halves(o["v_out"].transpose(0, 3, 1, 2).reshape(L, T, 512)))
    lp, ls = (a[:, None] for a in halves(o["logf_out"].transpose(0, 2, 1)))
    row = o["shift_out"].transpose(0, 3, 2, 1).reshape(L, 2, 7 * P)
    sh = np.concatenate([row[..., P:3 * P], row[..., 32:64], row[..., 3 * P:7 * P], row[..., 64:128]], -1)

    def states(s):
        return s.reshape(L, 2, 2, HD, 2, HD).transpose(0, 1, 4, 2, 3, 5).reshape(L, 2, 4, HD, HD)

    rw = states(o["rwkv_out"]).transpose(0, 1, 2, 4, 3)
    rt = states(o["ret_out"])
    outs = (yp, ys, kp, vp, lp, rw[:, 0:1], sh[:, 0][:, None, None], rt[:, 0:1],
            ks, vs, ls, rw[:, 1:2], sh[:, 1][:, None, None], rt[:, 1:2])
    return tuple(np.ascontiguousarray(a) for a in outs)


def build(nc, shapes):
    args = {n: nc.dram_tensor(n, s, F32, kind="ExternalInput").ap() for n, s in shapes.items()}
    args |= {n: nc.dram_tensor(n, s, F32, kind="ExternalOutput").ap() for n, s in OUTS.items()}
    program(nc, **args)


def kernel(**inputs):
    from concourse import bacc
    from concourse.bass_utils import run_bass_kernel_spmd as run

    arrays = {n: np.ascontiguousarray(a) for n, a in layout({k: np.asarray(v) for k, v in inputs.items()}).items()}
    nc = bacc.Bacc("TRN2", target_bir_lowering=False, num_devices=1)
    build(nc, {n: a.shape for n, a in arrays.items()})
    r = run(nc, [arrays], core_ids=[0])
    return unlayout({n: r.results[0][n] for n in OUTS})
```

```python
from contextlib import ExitStack

import numpy as np

import concourse.bass as bass
from concourse import mybir

F32 = mybir.dt.float32
F32R = mybir.dt.float32r
ALU = mybir.AluOpType
ACT = mybir.ActivationFunctionType
AX_X = mybir.AxisListType.X

P = 128
DEPTH, D, DFF = 2, 1024, 2816
TP, TS = 256, 32
T = TP + TS
PAST = 512
DB = D // P
FB = DFF // P
HD = 64
FOX_H = 8
EPS = 1e-6
RWKV_EPS = 64e-5
RET_EPS = 1e-6

RING = 4
SLOT = DB * 256
N_FFN_SLOTS = FB
N_Z_SLOTS = 16
DSTEPS = FB // 2
N_SPLIT = N_FFN_SLOTS + DSTEPS
POS_FFN = (0, N_SPLIT + N_Z_SLOTS + 5)
POS_Z = N_SPLIT
POS_OUT = POS_Z + N_Z_SLOTS
POS_PROJ = POS_OUT + 4
POS_GATE = POS_FFN[1] + N_SPLIT
N_SLOTS = POS_GATE + 4

Z_SMALL, Z_R, Z_K, Z_V = 0, 1, 3, 5
Z_TQ, Z_TK, Z_TV, Z_TG = 7, 9, 11, 13
Z_FQ, Z_FK, Z_FV, Z_FG = 15, 19, 23, 27
NZ = 31
N_SHIFTED = 7

TILES = ((0, 128), (128, 128), (256, 32))
CH = 32
NCH = T // CH

CONSTS = {}
_at = 0
for _name, _n in (("ident", 128), ("mean", 128), ("headsum", 128), ("headmean", 128), ("rot", 128),
                  ("cos", T), ("sin", T), ("causal", 128), ("causal4", 32), ("levels", 5 * 128),
                  ("level0T", 128), ("before", 128), ("upto", 128), ("restart", 512), ("retmask", 512),
                  ("retmask_s", 128), ("dquery", 2 * T), ("dstate", 2 * T), ("dchunk", 4),
                  ("fox8", 8), ("cols", 8)):
    CONSTS[_name] = (_at, _n)
    _at += _n
N_CONST = _at
C_EPS, C_ONE, C_REPS, C_TEPS, C_KKB, C_SMALLSC, C_SMALLM, C_SMALLA = range(8)

PARAMS = {}
_at = 0
for _name, _n in (("n1", DB), ("nm", DB), ("n2", DB), ("pn", DB), ("mu", 7), ("prev", 7), ("bf", 1), ("w0", 2),
                  ("a0", 2), ("kk", 2), ("ka", 2), ("rk", 2), ("lnw", 2), ("lnb", 2), ("low", 256)):
    PARAMS[_name] = (_at, _n)
    _at += _n
N_PARAM = _at

Z_BANKS = 4
MATS_ORDER = (0, 2, 1)
LEVEL_BANKS = ((6, 7), (0, 1), (2, 3))
U_AT = (0, 0, 256)

MIXIN_PER_LAYER, ZSTORE_PER_LAYER, SH_OUT_PER_LAYER, P_IN_PER_LAYER = 16 * 10, 16 * 13, 16, 16

KK_SCALE = float(2.0 ** 30)
LOG_DECAY = -float(np.exp(-0.5))


def head_of(g):
    return 64 * (g // 2), g % 2


def program(nc, wcol, wfirst, x_in, p_in, consts_in, params_in, foxl_in, kc_in, vc_in, clf_in, srwkv_in, sret_in,
            nf_in, y_out, k_out, v_out, logf_out, shift_out, rwkv_out, ret_out):
    with ExitStack() as ctx:
        def sb(name, *shape):
            return ctx.enter_context(nc.sbuf_tensor(name, list(shape), F32))

        ARENA = 17600
        EXTRA = 4480
        with ExitStack() as first:
            split_w, split_x, split_h, split_e = (
                first.enter_context(nc.sbuf_tensor(name, [P, n], F32R))
                for name, n in (("split_w", NZ * T), ("split_x", ARENA), ("split_h", DB * T), ("split_e", EXTRA)))
        zT = sb("zT", P, NZ, T)
        arena = sb("arena", P, ARENA)
        hT = sb("hT", P, DB, T)
        extra = sb("extra", P, EXTRA)
        xT = sb("xT", P, DB, T)
        wc = sb("wc", P, RING, SLOT)
        rs = sb("rs", P, T)
        con = sb("con", P, N_CONST)
        par = sb("par", P, N_PARAM)
        negp = sb("negp", P, 4)
        nf = sb("nf", P, DB)
        foxL = sb("foxL", P, FOX_H, T)
        foxR = sb("foxR", P, TP + PAST + TS)
        et = sb("et", P, 2, T)

        class Space:

            def __init__(self, t, size):
                self.t, self.size, self.at = t, size, 0

            def take(self, *shape):
                n = int(np.prod(shape))
                v = self.t[:, self.at:self.at + n]
                self.at += n
                assert self.at <= self.size, (self.at, self.size)
                if len(shape) == 2:
                    v = v.rearrange("p (a b) -> p a b", a=shape[0])
                if len(shape) == 3:
                    v = v.rearrange("p (a b c) -> p a b c", a=shape[0], b=shape[1])
                return v

        H = Space(split_x, ARENA)
        hid_hi, hid_lo = (H.take(FB, T) for _ in range(2))
        h_hi, h_lo = (H.take(DB, T) for _ in range(2))
        W = Space(split_w, NZ * T)
        ws = [(W.take(SLOT), W.take(SLOT)) for _ in range(2)]

        h1 = zT[:, 16:16 + DB, :]
        H = Space(split_h, DB * T)
        zh_hi = H.take(DB, T)
        H = Space(split_x, ARENA)
        H.at = 11520
        zh_lo = H.take(DB, T)
        H2 = Space(split_e, 3 * 8 * 128)
        H2.at = 1600
        zw = ((H.take(DB, 128), H.take(DB, 128)), (H.take(DB, 128), H2.take(DB, 128)))

        H = Space(split_x, ARENA)
        H.at = 2 * DB * T
        oh_hi, oh_lo = (H.take(DB, T) for _ in range(2))
        H.at = 11520
        beside = (H.take(SLOT), H.take(SLOT))
        wo = (ws[0], beside, ws[1], beside)

        A = Space(arena, ARENA)
        dz = A.take(N_SHIFTED, T)
        esm = A.take(T)
        sig4 = A.take(4, T)
        gate = A.take(2, T)
        lc = A.take(2, T)
        einc = A.take(2, T)
        einv = A.take(2, T)
        eexc = A.take(2, T)
        eend = A.take(2, T)
        kkf = A.take(2, T)
        bon = A.take(2, T)
        ar = A.take(2, 2, T)
        beta = A.take(2, T)
        bhat = A.take(2, T)
        kappa = A.take(2, T)
        khat = A.take(2, T)
        assert A.at <= 11520
        X = Space(extra, EXTRA)
        tok = X.take(3, 8, 128)
        st = X.take(11, 2, HD)
        M = Space(arena, ARENA)
        M.at = A.at
        u0 = M.take(3, 256)
        mats0 = [M.take(4, 128) for _ in range(2)]
        mats2 = [M.take(4, CH) for _ in range(6)]
        ctm = M.take(3, 512)
        dtm = M.take(3, 512)
        M = Space(dz.rearrange("p a b -> p (a b)"), N_SHIFTED * T)
        mats0 += [M.take(4, 128) for _ in range(3)]

        def over(t):
            return t.rearrange("p a b -> p (a b)")[:, 0:512].rearrange("p (g t) -> p g t", g=4)

        mats0.append(over(sig4[:, 0:2, :]))
        mats1 = [over(t) for t in (sig4[:, 2:4, :], lc, einv, eend, bhat, khat)]
        am, ml, xx, tt, yy, bt = zip(mats0, mats1, mats2)
        atT = eexc
        rott = et
        rgt = (rs[:], esm)
        qdec, kdec = hT[:, 0:2, :], hT[:, 2:4, :]
        R = Space(arena, N_SHIFTED * T + 5 * T)
        rtok = R.take(3, 512)
        smx = R.take(3, 512)
        R = Space(arena, ARENA)
        R.at = A.at + 3 * 256
        rst = R.take(7, 2, HD)
        osq = R.take(2, T)
        assert R.at <= A.at + 3 * 256 + 2 * 512 + 6 * 4 * CH
        og = lc
        F = Space(extra, 3 * 8 * 128)
        cbuf = F.take(TP + PAST + TS)
        clf = F.take(PAST)
        lgf = F.take(T)
        assert F.at <= 1600
        fu, fe = et[:, 0, :], et[:, 1, :]
        F = Space(extra, 3 * 8 * 128)
        vtok = F.take(3, 512)
        pt_s = F.take(2, 5, 128)
        F = Space(arena, ARENA)
        F.at = A.at + 3 * 256 + 2 * 512 + 6 * 4 * CH
        pq = F.take(2, 384)
        pt = F.take(2, 384)
        ps_s = F.take(2, PAST + TS)
        fm = F.take(32)
        F = Space(arena, N_SHIFTED * T + 5 * T)
        kc = F.take(4, PAST + TS)
        F = Space(arena, A.at)
        F.at = A.at - 8 * T
        vc = F.take(4, 512)
        fg = zT[:, Z_FG:Z_FG + 4, :]
        shc = sb("shc", P, N_SHIFTED, 2)
        ow = kkf

        E = Space(arena, ARENA)
        squares = (None, hT, E.take(DB, T), hT)
        proj_sq = E.take(DB, T)
        E = Space(extra, EXTRA)
        proj_e, ple_rs = E.take(DB, T), E.take(T)
        E.at = 3 * 8 * 128
        ple_in = E.take(2, T)
        ple_gate = squares[2]

        bank = [ctx.enter_context(nc.psum_tensor(f"bank{i}", [P, 512], F32)) for i in range(8)]

        def z_raw(n):
            return wc[:, (POS_Z + n // 2) % RING, :].rearrange("p (k n) -> p k n", k=DB)[:, :, n % 2 * 128:n % 2 * 128 + 128]

        def c(name, rows=slice(0, P)):
            a, n = CONSTS[name]
            return con[rows, a:a + n]

        def col(i, rows=slice(0, P)):
            a = CONSTS["cols"][0] + i
            return con[rows, a:a + 1]

        def pa(name, i=0, rows=slice(0, P)):
            a = PARAMS[name][0] + i
            return par[rows, a:a + 1]

        def mats_psum(j, e):
            if j == 2:
                return [bank[6 + e][:, a:a + 128].rearrange("p (g w t) -> p g w t", g=2, w=2) for a in (0, 128, 256)]
            return [bank[3 * e + i][:, :].rearrange("p (g w t) -> p g w t", g=2, w=2) for i in range(3)]

        names = """col0 col1 col2 col3 cast wlo zcast zlo zh_hi zh_lo h_hi h_lo hid_hi hid_lo
            down_used down_ps x_ready sq norm_ps ln rstd h gate_ps up_ps tanh silu hidden z_ps z_ev
            negp vchain schain sh_cp out_ps
            small e_small lowin low_ps e_low gcp ccs kraw ksq kk_ps kln rn bonin bon_ps bon_ok
            lcs dexc dend exps prods tr_ps trc mats_ps masks xt lev y_ps ycp dx_ps dt_ps lvl bv_ps bvc ua_ps uac
            u_ps u_ok s_ps s_ok o_ps o_ok gn_ps gn_sq gn_ln gn_rs
            rot_ps rotd decd fred rtr_ps rtrc sm_ps smd kv_ps rsd ro_ps ro_ok rgate
            fu_ok fe_ok fl_ok lgf_ok fc_ok vt_ps vtc fs_ps fmx fexp fpn ft_ps ftc fo_ps fo_ok
            ss_ps smx sexp spn st_ps stc so_ps so_ok kcnew
            mixout pchain rwkv_done ret_done ocast olo oh_hi oh_lo pj_ps pj_cp pj_sq pn_ps ple_rs ple_e g_ps g_tanh next_w""".split()
        sems = {n: ctx.enter_context(nc.semaphore(n)) for n in names}
        S = sems
        numbers = [s.num for s in sems.values()]
        layer_sems = range(min(numbers), max(numbers) + 1)
        assert len(layer_sems) == len(names)
        for n in ("mixin", "zstore", "sh_out", "p_in"):
            S[n] = ctx.enter_context(nc.semaphore(n))
        start_sem = ctx.enter_context(nc.semaphore("start"))
        clear_sem = ctx.enter_context(nc.semaphore("zeroed"))
        first_sem = {n: ctx.enter_context(nc.semaphore("first_" + n)) for n in ("x", "con", "sq", "ps", "ln", "rs")}
        first_slot = [ctx.enter_context(nc.semaphore(f"first_slot{p}")) for p in range(RING)]
        end_sem = {n: ctx.enter_context(nc.semaphore("end_" + n)) for n in ("y", "st")}

        with nc.Block() as block:
            @block.sync
            def _(sp):
                for b in range(0, DB, 4):
                    sp.dma_start(xT[:, b:b + 4, :], x_in[:, b:b + 4, :]).then_inc(first_sem["x"], 16)
                mean_at, cols_at = CONSTS["mean"][0], CONSTS["cols"][0]
                for a, b, sem in ((mean_at, mean_at + 128, first_sem["con"]), (cols_at, N_CONST, first_sem["con"])):
                    sp.dma_start(con[:, a:b], consts_in[:, a:b]).then_inc(sem, 16)
                sp.dma_start(par[:], params_in[0]).then_inc(first_slot[0], 16)
                for p in range(RING):
                    sp.dma_start(wc[:, p, :], wfirst[0, p]).then_inc(first_slot[p], 16)
                for a, b in ((0, mean_at), (mean_at + 128, cols_at)):
                    sp.dma_start(con[:, a:b], consts_in[:, a:b]).then_inc(start_sem, 16)
                sp.dma_start(nf[:], nf_in).then_inc(start_sem, 16)
                sp.wait_ge(clear_sem, 2)
                sp.dma_start(foxL[32:40, :, :], foxl_in).then_inc(start_sem, 16)

            @block.gpsimd
            def _(pool):
                pool.memset(foxL[:], 0.0).then_inc(clear_sem, 1)
                pool.memset(foxR[:], 0.0).then_inc(clear_sem, 1)
                pool.wait_ge(clear_sem, 2)
                pool.memset(foxR[0:8, :], 1.0).then_inc(clear_sem, 1)

            @block.scalar
            def _(act):
                act.preload_act_table_set("natural_log_exp_and_others")
                act.wait_ge(first_sem["x"], 32)
                for b in range(DB):
                    act.activation(hT[:, b, :], xT[:, b, :], ACT.Square).then_inc(first_sem["sq"], 1)
                act.wait_ge(first_sem["ps"], 1)
                act.wait_ge(first_sem["con"], 32)
                act.activation(rs[:], bank[0][:, 0:T], ACT.Ln, bias=col(C_EPS)).then_inc(first_sem["ln"], 1)
                act.wait_ge(first_sem["ln"], 1)
                act.activation(rs[:], rs[:], ACT.Exp, scale=-0.5).then_inc(first_sem["rs"], 1)

            @block.tensor
            def _(pe):
                pe.wait_ge(first_sem["con"], 32)
                for b in range(DB):
                    pe.wait_ge(first_sem["sq"], b + 1)
                    mm = pe.matmul(bank[0][:, 0:T], c("mean"), hT[:, b, :], start=(b == 0), stop=(b == DB - 1))
                mm.then_inc(first_sem["ps"], 1)

        with nc.Fori(0, DEPTH) as layer:
            with nc.Block() as block:

                @block.sync
                def _(sp):

                    def last_use(p):
                        for f in range(2):
                            s = p - POS_FFN[f]
                            if 0 <= s < N_SPLIT:
                                return "wlo", N_SPLIT * f + s + 1
                        if POS_Z <= p < POS_OUT:
                            return "zlo", min(2 * (p - POS_Z) + 2, NZ)
                        if POS_OUT <= p < POS_OUT + 4:
                            return "olo", p - POS_OUT + 1
                        return "pj_ps", DB

                    def load_cols(p0, n):
                        for p in range(p0, p0 + n):
                            if p >= RING:
                                sem, count = last_use(p - RING)
                                sp.wait_ge(S[sem], count)
                            sp.dma_start(wc[:, p % RING, :], wcol[layer, p]).then_inc(S[f"col{p % RING}"], 16)

                    for p in range(RING):
                        sp.wait_ge(first_slot[p], 16 if p else 32)
                        if p == RING - 1:
                            sp.wait_ge(start_sem, 64)
                        sp.nop().then_inc(S[f"col{p}"], 16)
                    load_cols(RING, N_SLOTS - RING)
                    sp.wait_ge(S["ple_e"], DB)
                    sp.dma_start(par[:], params_in[layer + 1]).then_inc(S["next_w"], 16)
                    for p in (3, 0, 1, 2):
                        sp.wait_ge(S["wlo"], 2 * N_SPLIT + 1 + (p + 1) % RING)
                        sp.dma_start(wc[:, p, :], wfirst[layer + 1, p]).then_inc(S["next_w"], 16)
                    sp.wait_ge(S["next_w"], 16 * (RING + 1))

                @block.gpsimd
                def _(pool):
                    pool.dma_start(st[:, 0, :, :], srwkv_in[layer, 0]).then_inc(S["mixin"], 16)
                    pool.dma_start(st[:, 9, :, :], srwkv_in[layer, 1]).then_inc(S["mixin"], 16)
                    pool.dma_start(clf[0:8, :], clf_in[layer]).then_inc(S["mixin"], 16)

                    def rest(n, i=0):
                        hi, lo = zw[n % 2]
                        pool.wait_ge(S["zcast"], i * 8 + n + 1)
                        pool.tensor_tensor(lo, z_raw(n), hi, ALU.subtract).then_inc(S["zlo"], 1)

                    rest(0)
                    rest(1)
                    with pool.Fori(0, 2) as i:
                        for q in range(8):
                            rest(q + 2, i)
                    for n in range(18, 22):
                        rest(n)
                    pool.wait_ge(S["lgf_ok"], 1)
                    pool.dma_start(logf_out[layer], lgf[0:8, :]).then_inc(S["zstore"], 16)
                    for n in range(22, NZ):
                        rest(n)
                    pool.wait_ge(S["zstore"], layer * ZSTORE_PER_LAYER + 16)
                    pool.wait_ge(S["z_ev"], Z_BANKS + NZ)
                    for b in range(4):
                        pool.dma_start(k_out[layer, b], zT[:, Z_FK + b, :]).then_inc(S["zstore"], 16)
                        pool.dma_start(v_out[layer, b], zT[:, Z_FV + b, :]).then_inc(S["zstore"], 16)
                    pool.wait_ge(S["sh_cp"], 1)
                    pool.dma_start(shift_out[layer], shc[:]).then_inc(S["sh_out"], 16)
                    pool.wait_ge(S["uac"], 6)
                    pool.dma_start(rst[:, 0, :, :], sret_in[layer, 0]).then_inc(S["mixin"], 16)
                    pool.dma_start(rst[:, 5, :, :], sret_in[layer, 1]).then_inc(S["mixin"], 16)
                    pool.wait_ge(S["s_ok"], 18)
                    pool.dma_start(rwkv_out[layer, 0], st[:, 8, :, :]).then_inc(S["zstore"], 16)
                    pool.dma_start(rwkv_out[layer, 1], st[:, 10, :, :]).then_inc(S["zstore"], 16)
                    pool.wait_ge(S["rsd"], 10)
                    pool.dma_start(ret_out[layer, 0], rst[:, 4, :, :]).then_inc(S["zstore"], 16)
                    pool.dma_start(ret_out[layer, 1], rst[:, 6, :, :]).then_inc(S["zstore"], 16)
                    pool.wait_ge(S["o_ok"], 6)
                    pool.wait_ge(S["ro_ok"], 6)
                    for b in range(4):
                        pool.dma_start(kc[:, b, 0:PAST], kc_in[layer, b]).then_inc(S["mixin"], 16)
                    pool.wait_ge(S["gn_rs"], 1)
                    pool.dma_start(vc[:], vc_in[layer]).then_inc(S["mixin"], 16)
                    pool.dma_start(ple_in, p_in[layer]).then_inc(S["p_in"], 16)
                    def link(n, ins):
                        ins.then_inc(S["pchain"], 1)
                        pool.wait_ge(S["pchain"], n)

                    link(1, pool.tensor_tensor(ow, ow, einv, ALU.mult))
                    for b in range(2):
                        link(2 + b, pool.tensor_scalar(ow[:, b, :], ow[:, b, :], pa("lnw", b), pa("lnb", b), ALU.mult, ALU.add))
                    pool.wait_ge(S["bon_ok"], 2)
                    link(4, pool.tensor_tensor(ow, ow, bon, ALU.add))
                    pool.wait_ge(S["gcp"], 2)
                    pool.tensor_tensor(hT[:, 4:6, :], ow, gate, ALU.mult).then_inc(S["rwkv_done"], 1)
                    pool.wait_ge(S["zstore"], layer * ZSTORE_PER_LAYER + 16 * 13)
                    pool.wait_ge(S["sh_out"], layer * SH_OUT_PER_LAYER + 16)
                    pool.wait_ge(S["p_in"], layer * P_IN_PER_LAYER + 16)
                    pool.nop().then_inc(S["mixout"], 1)

                @block.scalar
                def _(act):
                    n_chain = [0]

                    def link(ins):
                        n_chain[0] += 1
                        ins.then_inc(S["schain"], 1)
                        act.wait_ge(S["schain"], n_chain[0])

                    def square(s, b):
                        act.wait_ge(S["x_ready"], 8 * (s if s < 3 else 4) + b + 1)
                        act.activation(squares[s][:, b, :], xT[:, b, :], ACT.Square).then_inc(S["sq"], 1)

                    def rstd(s):
                        act.wait_ge(S["norm_ps"], s)
                        act.activation(rs[:], bank[0][:, 0:T], ACT.Ln, bias=col(C_EPS)).then_inc(S["ln"], 1)
                        act.wait_ge(S["ln"], s)
                        act.activation(rs[:], rs[:], ACT.Exp, scale=-0.5).then_inc(S["rstd"], 1)

                    def norm(s, meanwhile=lambda: None):
                        for b in range(DB):
                            square(s, b)
                        meanwhile()
                        rstd(s)

                    def cast(f, s, i=0):
                        p = POS_FFN[f] + s
                        act.wait_ge(S[f"col{p % RING}"], i * 16 + 16 * (p // RING + 1))
                        if s >= 2:
                            d = s - 2
                            if d >= N_SPLIT:
                                act.wait_ge(S["g_ps"], 2 * (d - N_SPLIT) + 2)
                            elif d == N_SPLIT - 1:
                                act.wait_ge(S["down_ps"], DB * f + DB)
                            elif d < N_FFN_SLOTS:
                                act.wait_ge(S[("gate_ps", "up_ps")[d % 2]], i * 4 + (FB * f + 2 * (d // 2) + 2))
                            else:
                                act.wait_ge(S["down_used"], i * 4 + ((DSTEPS - 1) * f + d - N_FFN_SLOTS + 1))
                        act.activation(ws[s % 2][0], wc[:, p % RING, :], ACT.Copy).then_inc(S["cast"], 1)

                    def ffn(f):
                        for b in range(DB):
                            act.wait_ge(S["h"], 2 * DB * f + b + 1)
                            act.activation(h_hi[:, b, :], hT[:, b, :], ACT.Copy).then_inc(S["h_hi"], 1)
                        if f == 0:
                            cast(f, 1)
                        act.preload_act_table_set("exp_and_others")

                        def two(i, jj):
                            cast(f, 2 * jj + 2, i)
                            for q in (2 * jj, 2 * jj + 1):
                                act.wait_ge(S["gate_ps"], i * 4 + (FB * f + q + 1))
                                act.wait_ge(S["hid_lo"], i * 4 + (FB * f + q + 1))
                                act.activation(et[:, q % 2, :], bank[2 * (q % 4)][:, 0:T], ACT.Tanh, scale=0.5)\
                                   .then_inc(S["tanh"], 1)
                            cast(f, 2 * jj + 3, i)
                            for q in (2 * jj, 2 * jj + 1):
                                act.wait_ge(S["hidden"], i * 4 + (FB * f + 4 + q + 1))
                                dst = hid_hi[:, q, :] if isinstance(i, int) else hid_hi[:, bass.ds(i * 4 + q, 1), :]
                                act.activation(dst, et[:, q % 2, :], ACT.Copy).then_inc(S["hid_hi"], 1)

                        with act.Fori(0, FB // 4) as i:
                            two(i, 0)
                            two(i, 1)
                        two(0, FB // 2 - 1)
                        if f == 0:
                            act.preload_act_table_set("natural_log_exp_and_others")
                        cast(f, N_FFN_SLOTS + 2)
                        with act.Fori(0, 2) as i:
                            for u in range(4):
                                cast(f, N_FFN_SLOTS + 3 + u, i)

                    cast(0, 0)
                    ffn(0)
                    def z_cast(n, i=0):
                        p = POS_Z + n // 2
                        act.wait_ge(S[f"col{p % RING}"], i * 16 + 16 * (p // RING + 1))
                        if n >= 2:
                            act.wait_ge(S["z_ps"], i * 8 + n - 1)
                        act.activation(zw[n % 2][0], z_raw(n), ACT.Copy).then_inc(S["zcast"], 1)

                    norm(1, lambda: (z_cast(0), z_cast(1)))
                    for b in range(DB):
                        act.wait_ge(S["h"], DB + b + 1)
                        act.activation(zh_hi[:, b, :], h1[:, b, :], ACT.Copy).then_inc(S["zh_hi"], 1)

                    def z_copy(n, q):
                        act.wait_ge(S["z_ps"], n + 1)
                        if isinstance(n, int) and n >= Z_FG:
                            return act.activation(zT[:, n, :], bank[q][:, 0:T], ACT.Exp, scale=-1.0).then_inc(S["z_ev"], 1)
                        return act.activation(zT[:, n, :] if isinstance(n, int) else zT[:, bass.ds(n, 1), :],
                                              bank[q][:, 0:T], ACT.Copy).then_inc(S["z_ev"], 1)
                    with act.Fori(0, 2) as i:
                        for q in range(8):
                            z_cast(q + 2, i)
                            z_copy(i * 8 + q, q % Z_BANKS)

                    def z_block(n):
                        if n + 2 < NZ:
                            z_cast(n + 2)
                        z_copy(n, n % Z_BANKS)

                    def z_slot(s):
                        for n in range(2 * s, min(2 * s + 2, NZ)):
                            z_block(n)

                    act.wait_ge(S["small"], N_SHIFTED)
                    act.activation(esm, zT[:, Z_SMALL, :], ACT.Exp, scale=col(C_SMALLSC)).then_inc(S["e_small"], 1)
                    z_block(16)
                    act.wait_ge(S["kraw"], 2)
                    act.activation(bhat, kkf, ACT.Square).then_inc(S["ksq"], 1)
                    act.wait_ge(S["fu_ok"], 1)
                    link(act.activation(fe[0:8, :], fe[0:8, :], ACT.Exp))
                    act.activation(fe[0:8, :], fe[0:8, :], ACT.Ln, bias=col(C_ONE, slice(0, 8))).then_inc(S["fl_ok"], 1)
                    z_block(17)
                    act.wait_ge(S["negp"], 1)
                    for i in range(4):
                        act.wait_ge(S["low_ps"], i + 1)
                        act.activation(sig4[:, i, :], bank[4 + i][:, 0:T], ACT.Exp, scale=-1.0,
                                       bias=negp[:, i:i + 1]).then_inc(S["e_low"], 1)
                    z_slot(9)
                    for b in range(2):
                        act.wait_ge(S["low_ps"], 5 + b)
                        act.activation(gate[:, b, :], bank[6 + b][:, 0:T], ACT.Copy).then_inc(S["gcp"], 1)
                    for b in range(2):
                        act.activation(rgt[b], zT[:, Z_TG + b, :], ACT.Exp, scale=-1.0).then_inc(S["rgate"], 1)
                    z_slot(10)
                    for b in range(2):
                        act.wait_ge(S["kln"], b + 1)
                        act.wait_ge(S["ksq"], 1)
                        link(act.activation(khat[:, b, :], khat[:, b, :], ACT.Ln, scale=KK_SCALE))
                        act.activation(khat[:, b, :], khat[:, b, :], ACT.Exp, scale=-0.5, bias=col(C_KKB))\
                           .then_inc(S["rn"], 1)
                    z_block(22)
                    act.wait_ge(S["lcs"], 2)
                    act.activation(einc, lc, ACT.Exp).then_inc(S["exps"], 1)
                    act.activation(einv, lc, ACT.Exp, scale=-1.0).then_inc(S["exps"], 1)
                    act.wait_ge(S["dexc"], 1)
                    act.activation(eexc, eexc, ACT.Exp).then_inc(S["exps"], 1)
                    act.wait_ge(S["dend"], 1)
                    act.activation(eend, eend, ACT.Exp).then_inc(S["exps"], 1)
                    z_block(23)
                    for s in range(12, 16):
                        z_slot(s)
                    act.wait_ge(S["zstore"], layer * ZSTORE_PER_LAYER + 16)
                    for j in range(3):
                        n = TILES[j][1]
                        for k in range(2):
                            act.wait_ge(S["tr_ps"], 2 * j + k + 1)
                            act.activation(tok[0:n, j, 4 * k:4 * k + 4, :].rearrange("p a b -> p (a b)"),
                                           bank[4 + (2 * j + k + 2) % 4][0:n, :], ACT.Copy).then_inc(S["trc"], 1)
                    for j in range(3):
                        n = TILES[j][1]
                        act.wait_ge(S["bv_ps"], 3)
                        act.activation(u0[0:n, j, :], bank[4 + j % 2][0:n, U_AT[j]:U_AT[j] + 256], ACT.Copy)\
                           .then_inc(S["bvc"], 1)
                    for s in range(1, 5):
                        for j in range(3):
                            n = TILES[j][1]
                            act.wait_ge(S["y_ps"], 3 * (s - 1) + j + 1)
                            act.activation(yy[j][0:n, :, 0:n],
                                           bank[LEVEL_BANKS[j][0]][0:n, :].rearrange("p (g t) -> p g t", g=4)[:, :, 0:n],
                                           ACT.Copy).then_inc(S["ycp"], 1)
                    for j in range(3):
                        t0, n = TILES[j]
                        act.wait_ge(S["ua_ps"], 2 * j + 1)
                        act.activation(u0[0:n, j, :], bank[4 + j % 2][0:n, U_AT[j]:U_AT[j] + 256], ACT.Copy)\
                           .then_inc(S["uac"], 1)
                        act.wait_ge(S["ua_ps"], 2 * j + 2)
                        act.activation(atT[:, :, t0:t0 + n],
                                       bank[LEVEL_BANKS[j][0]][:, 0:256].rearrange("p (b t) -> p b t", b=2)[:, :, 0:n],
                                       ACT.Copy).then_inc(S["uac"], 1)

                    for j in range(3):
                        n = TILES[j][1]
                        act.wait_ge(S["rtr_ps"], j + 1)
                        act.activation(rtok[0:n, j, :], bank[6 + j % 2][0:n, :], ACT.Copy).then_inc(S["rtrc"], 1)

                    for j in range(3):
                        n = TILES[j][1]
                        act.wait_ge(S["vt_ps"], j + 1)
                        act.activation(vtok[0:n, j, :], bank[2 + j % 2][0:n, :], ACT.Copy).then_inc(S["vtc"], 1)

                    rs2 = (einv, osq)
                    for which, eps in enumerate((col(C_REPS), col(C_TEPS))):
                        for b in range(2):
                            act.wait_ge(S["gn_ps"], 5 + 2 * which + b)
                            act.activation(rs2[which][:, b, :], bank[4 + 2 * which + b][:, 0:T], ACT.Ln, bias=eps)\
                               .then_inc(S["gn_ln"], 1)
                        act.wait_ge(S["gn_ln"], 2 * which + 2)
                        act.activation(rs2[which], rs2[which], ACT.Exp, scale=-0.5).then_inc(S["gn_rs"], 1)

                    for h in range(FOX_H):
                        act.wait_ge(S["fmx"], h + 1)
                        if h >= 2:
                            act.wait_ge(S["ft_ps"], h - 1)
                        sp_ = bank[h % 2]
                        act.activation(pq[:, h % 2, 0:128], sp_[:, 0:128], ACT.Exp, scale=0.125,
                                       bias=fm[:, 8 + 2 * (h % 2):9 + 2 * (h % 2)],
                                       accum_out=fm[:, 12 + 2 * (h % 2):13 + 2 * (h % 2)]).then_inc(S["fexp"], 1)
                        act.activation(pq[:, h % 2, 128:384], sp_[:, 128:384], ACT.Exp, scale=0.125,
                                       bias=fm[:, 9 + 2 * (h % 2):10 + 2 * (h % 2)],
                                       accum_out=fm[:, 13 + 2 * (h % 2):14 + 2 * (h % 2)]).then_inc(S["fexp"], 1)
                        act.wait_ge(S["ft_ps"], h + 1)
                        if h >= 2:
                            act.wait_ge(S["fo_ps"], h - 1)
                        act.activation(pt[:, h % 2, :], bank[2 + h % 2][:, 0:384], ACT.Copy).then_inc(S["ftc"], 1)

                    def out_cast(s):
                        act.wait_ge(S[f"col{(POS_OUT + s) % RING}"], 16 * ((POS_OUT + s) // RING + 1))
                        act.activation(wo[s][0], wc[:, (POS_OUT + s) % RING, :], ACT.Copy).then_inc(S["ocast"], 1)

                    act.wait_ge(S["mixout"], 1)
                    act.wait_ge(S["ret_done"], 1)
                    out_cast(0)
                    act.wait_ge(S["rwkv_done"], 1)
                    act.activation(oh_hi[:, 4:8, :], hT[:, 4:8, :], ACT.Copy).then_inc(S["oh_hi"], 1)
                    for g in range(2):
                        act.wait_ge(S["smx"], g + 1)
                        act.activation(ps_s[:, g, 0:PAST], bank[2 * g][:, :], ACT.Exp, scale=0.125,
                                       bias=fm[:, 20 + g:21 + g], accum_out=fm[:, 22 + g:23 + g]).then_inc(S["sexp"], 1)
                        act.activation(ps_s[:, g, PAST:], ps_s[:, g, PAST:], ACT.Exp, scale=0.125,
                                       bias=fm[:, 20 + g:21 + g], accum_out=fm[:, 24 + g:25 + g]).then_inc(S["sexp"], 1)
                        if g == 0:
                            act.wait_ge(S["fo_ok"], FOX_H)
                            act.activation(oh_hi[:, 0:4, 0:TP], hT[:, 0:4, 0:TP], ACT.Copy).then_inc(S["oh_hi"], 1)
                        act.wait_ge(S["st_ps"], 2 * g + 1)
                        act.activation(pt_s[:, g, 0:4, :].rearrange("p a b -> p (a b)"), bank[4][:, :], ACT.Copy)\
                           .then_inc(S["stc"], 1)
                        act.wait_ge(S["st_ps"], 2 * g + 2)
                        act.activation(pt_s[0:TS, g, 4, :], bank[5][0:TS, 0:128], ACT.Copy).then_inc(S["stc"], 1)

                    act.wait_ge(S["so_ok"], 2)
                    act.activation(oh_hi[:, 0:4, TP:T], hT[:, 0:4, TP:T], ACT.Copy).then_inc(S["oh_hi"], 1)
                    out_cast(1)
                    out_cast(2)
                    act.wait_ge(S["out_ps"], 2)
                    cast(1, 0)
                    act.wait_ge(S["out_ps"], 4)
                    out_cast(3)
                    square(2, 0)
                    square(2, 1)
                    act.wait_ge(S["out_ps"], 6)
                    cast(1, 1)
                    for b in range(2, DB):
                        square(2, b)
                    rstd(2)
                    for b in range(DB):
                        act.wait_ge(S["pj_ps"], b + 1)
                        act.activation(proj_e[:, b, :], bank[4 + b % 4][:, 0:T], ACT.Copy).then_inc(S["pj_cp"], 1)
                        act.wait_ge(S["pj_cp"], b + 1)
                        act.activation(proj_sq[:, b, :], proj_e[:, b, :], ACT.Square).then_inc(S["pj_sq"], 1)
                    act.wait_ge(S["pn_ps"], 1)
                    link(act.activation(ple_rs, bank[7][:, 0:T], ACT.Ln, bias=col(C_EPS)))
                    act.activation(ple_rs, ple_rs, ACT.Exp, scale=-0.5).then_inc(S["ple_rs"], 1)
                    ffn(1)

                    cast(1, N_SPLIT)
                    for b in range(DB):
                        act.wait_ge(S["x_ready"], 3 * DB + b + 1)
                        act.activation(h_hi[:, b, :], xT[:, b, :], ACT.Copy).then_inc(S["h_hi"], 1)
                    cast(1, N_SPLIT + 1)
                    for b in range(DB):
                        if b in (0, 2):
                            cast(1, N_SPLIT + 2 + b // 2)
                        act.wait_ge(S["g_ps"], b + 1)
                        act.activation(ple_gate[:, b, :], bank[b][:, 0:T], ACT.Tanh, scale=0.5).then_inc(S["g_tanh"], 1)
                        if b:
                            square(3, b - 1)
                    square(3, DB - 1)
                    act.preload_act_table_set("natural_log_exp_and_others")
                    rstd(3)

                @block.vector
                def _(dve):
                    n_chain = [0]

                    def link(ins):
                        n_chain[0] += 1
                        ins.then_inc(S["vchain"], 1)
                        dve.wait_ge(S["vchain"], n_chain[0])

                    def norm(s, gains, out=hT):
                        if s:
                            dve.wait_ge(S["rstd"], s)
                        dve.wait_ge(S["x_ready"], 8 * (s + 1))
                        for b in range(DB):
                            dve.scalar_tensor_tensor(out[:, b, :], xT[:, b, :], pa(gains, b), rs[:],
                                                     ALU.mult, ALU.mult).then_inc(S["h"], 1)

                    def rest(f, s, i=0):
                        hi, lo = ws[s % 2]
                        dve.wait_ge(S["cast"], i * 4 + (N_SPLIT * f + s + 1))
                        dve.tensor_tensor(lo, wc[:, (POS_FFN[f] + s) % RING, :], hi, ALU.subtract).then_inc(S["wlo"], 1)

                    def lo_of(src, b, n):
                        dve.wait_ge(S["h_hi"], DB * n + b + 1)
                        dve.tensor_tensor(h_lo[:, b, :], src[:, b, :], h_hi[:, b, :], ALU.subtract).then_inc(S["h_lo"], 1)

                    def ffn(f):
                        for b in range(DB):
                            lo_of(hT, b, f)
                        if f == 0:
                            rest(0, 0)
                            rest(0, 1)

                        def two(i, jj):
                            rest(f, 2 * jj + 2, i)
                            for q in (2 * jj, 2 * jj + 1):
                                e = et[:, q % 2, :]
                                dve.wait_ge(S["tanh"], i * 4 + (FB * f + q + 1))
                                dve.scalar_tensor_tensor(e, e, 1.0, bank[2 * (q % 4)][:, 0:T], ALU.add, ALU.mult)\
                                   .then_inc(S["silu"], 1)
                            for q in (2 * jj, 2 * jj + 1):
                                e = et[:, q % 2, :]
                                dve.wait_ge(S["silu"], i * 4 + (FB * f + q + 1))
                                dve.wait_ge(S["up_ps"], i * 4 + (FB * f + q + 1))
                                dve.scalar_tensor_tensor(e, e, 0.5, bank[2 * (q % 4) + 1][:, 0:T], ALU.mult, ALU.mult)\
                                   .then_inc(S["hidden"], 1)
                            rest(f, 2 * jj + 3, i)
                            for q in (2 * jj, 2 * jj + 1):
                                hi, lo = (x[:, q, :] if isinstance(i, int) else x[:, bass.ds(i * 4 + q, 1), :]
                                          for x in (hid_hi, hid_lo))
                                dve.wait_ge(S["hid_hi"], i * 4 + (FB * f + q + 1))
                                dve.tensor_tensor(lo, et[:, q % 2:q % 2 + 1, :] if len(lo.shape) == 3 else et[:, q % 2, :],
                                                  hi, ALU.subtract).then_inc(S["hid_lo"], 1)

                        with dve.Fori(0, FB // 4) as i:
                            two(i, 0)
                            two(i, 1)
                        two(0, FB // 2 - 1)
                        rest(f, N_FFN_SLOTS + 2)
                        if f == 1:
                            dve.wait_ge(S["ple_rs"], 1)
                            for b in range(DB):
                                dve.scalar_tensor_tensor(proj_e[:, b, :], proj_e[:, b, :], pa("pn", b), ple_rs,
                                                         ALU.mult, ALU.mult).then_inc(S["ple_e"], 1)
                        with dve.Fori(0, 2) as i:
                            for u in range(4):
                                rest(f, N_FFN_SLOTS + 3 + u, i)
                        if f == 1:
                            rest(1, N_SPLIT)
                        for b in range(DB):
                            dve.wait_ge(S["down_ps"], DB * f + b + 1)
                            dve.scalar_tensor_tensor(xT[:, b, :], bank[b][:, 0:T], 0.5, xT[:, b, :],
                                                     ALU.mult, ALU.add).then_inc(S["x_ready"], 1)

                    def sigmoid_of(e):
                        link(dve.tensor_scalar(e, e, 1.0, None, ALU.add))
                        link(dve.reciprocal(e, e))

                    dve.nop().then_inc(S["x_ready"], 8)
                    dve.nop().then_inc(S["hidden"], 4)
                    dve.nop().then_inc(S["hid_lo"], 2)
                    dve.nop().then_inc(S["z_ev"], Z_BANKS)
                    dve.wait_ge(S["col0"], 16)
                    a = PARAMS["w0"][0]
                    dve.tensor_scalar(negp[:], par[:, a:a + 4], -1.0, None, ALU.mult).then_inc(S["negp"], 1)
                    norm(0, "n1")
                    ffn(0)
                    norm(1, "nm", h1)
                    for b in range(DB):
                        dve.wait_ge(S["zh_hi"], b + 1)
                        dve.tensor_tensor(zh_lo[:, b, :], h1[:, b, :], zh_hi[:, b, :], ALU.subtract).then_inc(S["zh_lo"], 1)

                    dve.wait_ge(S["z_ev"], Z_BANKS + N_SHIFTED)
                    zs = zT[:, 0:N_SHIFTED, :]
                    link(dve.tensor_tensor(dz[:, :, 1:T], zs[:, :, 0:T - 1], zs[:, :, 1:T], ALU.subtract))
                    link(dve.tensor_scalar(dz[:, :, 0:1], zs[:, :, 0:1], -1.0, None, ALU.mult))
                    prev = par[:, PARAMS["prev"][0]:PARAMS["prev"][0] + 7].unsqueeze(2)
                    link(dve.tensor_tensor(dz[:, :, TP:TP + 1], prev, zs[:, :, TP:TP + 1], ALU.subtract))
                    link(dve.tensor_copy(shc[:, :, 0:1], zs[:, :, TP - 1:TP]))
                    dve.tensor_copy(shc[:, :, 1:2], zs[:, :, T - 1:T]).then_inc(S["sh_cp"], 1)
                    dve.wait_ge(S["sh_cp"], 1)
                    for b in range(N_SHIFTED):
                        dve.scalar_tensor_tensor(zT[:, b, :], dz[:, b, :], pa("mu", b), zT[:, b, :],
                                                 ALU.mult, ALU.add).then_inc(S["small"], 1)
                    dve.wait_ge(S["small"], N_SHIFTED)
                    dve.wait_ge(S["e_small"], 1)
                    sigmoid_of(esm)
                    dve.tensor_scalar(dz[:, 0, :], esm, col(C_SMALLM), col(C_SMALLA), ALU.mult, ALU.add)\
                       .then_inc(S["lowin"], 1)
                    r, k, v = (zT[:, z:z + 2, :] for z in (Z_R, Z_K, Z_V))
                    for b in range(2):
                        dve.tensor_scalar(kkf[:, b, :], k[:, b, :], pa("kk", b), None, ALU.mult)\
                           .then_inc(S["kraw"], 1)
                    e8 = slice(0, 8)
                    link(dve.tensor_scalar(fu[e8, :], zT[e8, Z_SMALL, :], pa("bf", 0, e8), None, ALU.add))
                    link(dve.tensor_scalar(fe[e8, :], fu[e8, :], -1.0, None, ALU.mult))
                    dve.tensor_tensor(fe[e8, :], fe[e8, :], fu[e8, :], ALU.min).then_inc(S["fu_ok"], 1)
                    dve.wait_ge(S["fl_ok"], 1)
                    dve.scalar_tensor_tensor(lgf[e8, :], fu[e8, :], 0.0, fe[e8, :], ALU.min, ALU.subtract)\
                       .then_inc(S["lgf_ok"], 1)
                    dve.wait_ge(S["lgf_ok"], 1)
                    dve.wait_ge(S["mixin"], layer * MIXIN_PER_LAYER + 48)
                    w = con[e8, CONSTS["fox8"][0]:CONSTS["fox8"][0] + 8]
                    unit = foxR[e8, :]
                    link(dve.tensor_tensor_scan(cbuf[e8, 0:TP], unit[:, 0:TP], lgf[e8, 0:TP], 0.0, ALU.mult, ALU.add))
                    link(dve.tensor_tensor_scan(cbuf[e8, TP:TP + PAST], unit[:, 0:PAST], clf[e8, :], 0.0, ALU.mult, ALU.add))
                    link(dve.tensor_tensor_scan(cbuf[e8, TP + PAST:], unit[:, 0:TS], lgf[e8, TP:T],
                                                cbuf[e8, TP + PAST - 1:TP + PAST], ALU.mult, ALU.add))
                    link(dve.tensor_copy(foxR[32:40, :], cbuf[e8, :]))
                    for q0, k0, n in ((0, 0, TP), (TP, TP + PAST, TS)):
                        dve.tensor_tensor(foxL[e8, :, q0:q0 + n],
                                          cbuf[e8, k0:k0 + n].unsqueeze(1).to_broadcast([8, FOX_H, n]),
                                          w.unsqueeze(2).to_broadcast([8, FOX_H, n]), ALU.mult).then_inc(S["fc_ok"], 1)
                    dve.wait_ge(S["e_low"], 4)
                    sigmoid_of(sig4)
                    lw, aa = sig4[:, 0:2, :], sig4[:, 2:4, :]
                    link(dve.tensor_scalar(lw, lw, LOG_DECAY, None, ALU.mult))
                    for b in range(2):
                        dve.tensor_tensor_scan(lc[:, b, :], c("restart")[:, 0:T], lw[:, b, :], 0.0,
                                               ALU.mult, ALU.add).then_inc(S["lcs"], 1)
                    dve.wait_ge(S["lcs"], 2)
                    dve.tensor_tensor(eexc, lc, lw, ALU.subtract).then_inc(S["dexc"], 1)
                    chunks = lc.rearrange("p b (n u) -> p (b n) u", u=CH)
                    dve.tensor_tensor(eend.rearrange("p b (n u) -> p (b n) u", u=CH),
                                      chunks[:, :, CH - 1:CH].to_broadcast([P, 2 * NCH, CH]), chunks,
                                      ALU.subtract).then_inc(S["dend"], 1)
                    for b in range(2):
                        dve.wait_ge(S["kk_ps"], b + 1)
                        dve.tensor_scalar(khat[:, b, :], bank[4 + b][:, 0:T], 1e-24, None, ALU.max).then_inc(S["kln"], 1)
                    dve.wait_ge(S["rn"], 2)
                    link(dve.tensor_tensor(kkf, kkf, khat, ALU.mult))
                    for b in range(2):
                        link(dve.tensor_scalar(khat[:, b, :], aa[:, b, :], -1.0, pa("ka", b), ALU.add, ALU.mult))
                    link(dve.scalar_tensor_tensor(k, khat, 1.0, k, ALU.add, ALU.mult))
                    for b in range(2):
                        dve.scalar_tensor_tensor(bon[:, b, :], r[:, b, :], pa("rk", b), k[:, b, :],
                                                 ALU.mult, ALU.mult).then_inc(S["bonin"], 1)
                    dve.wait_ge(S["exps"], 4)
                    link(dve.tensor_tensor(aa, kkf, aa, ALU.mult))
                    link(dve.tensor_tensor(ar[:, :, 0, :], kkf, eexc, ALU.mult))
                    link(dve.tensor_tensor(ar[:, :, 1, :], r, einc, ALU.mult))
                    link(dve.scalar_tensor_tensor(beta, aa, -1.0, einv, ALU.mult, ALU.mult))
                    link(dve.scalar_tensor_tensor(bhat, aa, -1.0, eend, ALU.mult, ALU.mult))
                    link(dve.tensor_tensor(kappa, k, einv, ALU.mult))
                    dve.tensor_tensor(khat, k, eend, ALU.mult).then_inc(S["prods"], 1)
                    dve.wait_ge(S["prods"], 1)
                    for b in range(2):
                        dve.wait_ge(S["bon_ps"], b + 1)
                        dve.tensor_tensor(bon[:, b, :], bank[6 + b][:, 0:T], v[:, b, :], ALU.mult).then_inc(S["bon_ok"], 1)

                    for b in range(2):
                        dve.wait_ge(S["rgate"], b + 1)
                        sigmoid_of(rgt[b])
                        link(dve.tensor_tensor(zT[:, Z_TG + b, :], zT[:, Z_TG + b, :], rgt[b], ALU.mult))
                    cos2 = c("cos").unsqueeze(1).to_broadcast([P, 2, T])
                    for w_ in range(2):
                        qk = zT[:, Z_TQ + 2 * w_:Z_TQ + 2 * w_ + 2, :]
                        for b in range(2):
                            dve.wait_ge(S["rot_ps"], 2 * w_ + b + 1)
                            dve.tensor_tensor(rott[:, b, :], bank[4 + b][:, 0:T], c("sin"), ALU.mult).then_inc(S["rotd"], 1)
                        link(dve.tensor_tensor(qk, qk, cos2, ALU.mult))
                        dve.wait_ge(S["rotd"], 2 * w_ + 2)
                        link(dve.tensor_tensor(qk, qk, rott[:], ALU.add))

                    def four(x, j):
                        n = TILES[j][1]
                        return x[j][0:n, :, 0:n]

                    def mask(name, k, j, i=0):
                        n = TILES[j][1]
                        m = c(name)[0:n, i * 128:i * 128 + n]
                        return m.unsqueeze(1).to_broadcast([n, k, n])

                    for o, j in enumerate(MATS_ORDER):
                        n = TILES[j][1]
                        rows = slice(0, n)
                        for par_ in range(2):
                            gs = slice(2 * par_, 2 * par_ + 2)
                            first, second, third = mats_psum(j, par_)
                            dve.wait_ge(S["mats_ps"], 6 * o + 3 * par_ + (3 if j == 2 else 1))
                            dve.tensor_copy(am[j][rows, gs, 0:n], first[rows, :, 0, 0:n]).then_inc(S["masks"], 1)
                            dve.wait_ge(S["mats_ps"], 6 * o + 3 * par_ + 2)
                            dve.tensor_tensor(xx[j][rows, gs, 0:n], second[rows, :, 0, 0:n], mask("level0T", 2, j),
                                              ALU.mult).then_inc(S["masks"], 1)
                            cts = ctm[rows, j, :].rearrange("p (g t) -> p g t", g=4)[:, gs, 0:n]
                            dve.tensor_tensor(cts, second[rows, :, 1, 0:n], mask("upto", 2, j), ALU.mult)\
                               .then_inc(S["masks"], 1)
                            dve.wait_ge(S["mats_ps"], 6 * o + 3 * par_ + 3)
                            dve.tensor_tensor(bt[j][rows, gs, 0:n], third[rows, :, 0, 0:n], mask("before", 2, j),
                                              ALU.mult).then_inc(S["masks"], 1)
                            dts = dtm[rows, j, :].rearrange("p (g t) -> p g t", g=4)[:, gs, 0:n]
                            dve.tensor_tensor(dts, third[rows, :, 1, 0:n], mask("upto", 2, j), ALU.mult)\
                               .then_inc(S["masks"], 1)
                        dve.wait_ge(S["masks"], 10 * (o + 1))
                        link(dve.tensor_tensor(four(tt, j), four(am, j), mask("levels", 4, j, 0), ALU.mult))
                        dve.tensor_tensor(four(xx, j), four(xx, j), mask("ident", 4, j), ALU.add).then_inc(S["xt"], 1)
                        dve.tensor_tensor(four(tt, j), four(tt, j), mask("ident", 4, j), ALU.add).then_inc(S["xt"], 1)
                    for j in range(3):
                        dve.tensor_tensor(four(ml, j), four(am, j), mask("levels", 4, j, 1), ALU.mult).then_inc(S["lev"], 1)
                    dq, ds_ = (c(x).rearrange("p (b t) -> p b t", b=2) for x in ("dquery", "dstate"))
                    dve.wait_ge(S["z_ev"], Z_BANKS + NZ)
                    dve.tensor_tensor(kdec, zT[:, Z_TK:Z_TK + 2, :], ds_, ALU.mult).then_inc(S["decd"], 1)
                    dve.tensor_tensor(qdec, zT[:, Z_TQ:Z_TQ + 2, :], dq, ALU.mult).then_inc(S["decd"], 1)
                    for s in range(1, 5):
                        if s < 4:
                            for j in range(3):
                                dve.wait_ge(S["y_ps"], 3 * (s - 1) + j + 1)
                                dve.tensor_tensor(four(ml, j), four(am, j), mask("levels", 4, j, s + 1), ALU.mult)\
                                   .then_inc(S["lev"], 1)
                        for j in range(3):
                            n = TILES[j][1]
                            d_x, d_t = (bank[q][0:n, :].rearrange("p (g t) -> p g t", g=4)[:, :, 0:n]
                                        for q in LEVEL_BANKS[j][::-1])
                            dve.wait_ge(S["dx_ps"], 3 * (s - 1) + j + 1)
                            dve.tensor_tensor(four(xx, j), four(xx, j), d_x, ALU.add).then_inc(S["lvl"], 1)
                            if s < 4:
                                dve.wait_ge(S["dt_ps"], 3 * (s - 1) + j + 1)
                                dve.tensor_tensor(four(tt, j), four(tt, j), d_t, ALU.add).then_inc(S["lvl"], 1)
                        sigmoid_of(fg[:, s - 1, :])

                    def ret_scores(j):
                        n = TILES[j][1]
                        m = (c("retmask")[0:n, :] if j < 2 else c("retmask_s")[0:n, :]).rearrange("p (g t) -> p g t", g=4)
                        for e in range(2):
                            dve.wait_ge(S["sm_ps"], 2 * j + e + 1)
                            dve.tensor_tensor(smx[0:n, j, :].rearrange("p (g t) -> p g t", g=4)[:, 2 * e:2 * e + 2, 0:n],
                                              bank[4 + e][0:n, 0:256].rearrange("p (g t) -> p g t", g=2)[:, :, 0:n],
                                              m[:, 2 * e:2 * e + 2, :], ALU.mult).then_inc(S["smd"], 1)

                    def ret_state(i):
                        old, new = (i, i + 1) if i < 4 else (5, 6)
                        dch = c("dchunk")
                        dve.wait_ge(S["kv_ps"], 5)
                        if i == 0:
                            dve.wait_ge(S["mixin"], layer * MIXIN_PER_LAYER + 80)
                        if 1 <= i < 4:
                            dve.wait_ge(S["rsd"], 2 * i)
                        for b in range(2):
                            s = 128 * (i // 2) + 64 * b
                            dve.scalar_tensor_tensor(rst[:, new, b, :], rst[:, old, b, :],
                                                     dch[:, 2 * (i // 4) + b:2 * (i // 4) + b + 1],
                                                     bank[6 + i % 2][:, s:s + HD], ALU.mult, ALU.add).then_inc(S["rsd"], 1)

                    with_chunk = {1: [(ret_scores, 0)], 3: [(ret_scores, 1)], 4: [(ret_scores, 2)],
                                  6: [(ret_state, 0), (ret_state, 1)], 7: [(ret_state, 2), (ret_state, 3)],
                                  8: [(ret_state, 4)]}
                    dve.wait_ge(S["uac"], 6)
                    for i in range(NCH):
                        j, q = (i // 4, i % 4) if i < 8 else (2, 0)
                        rows = slice(32 * q, 32 * q + 32)
                        old, new = (i, i + 1) if i < 8 else (9, 10)
                        dve.wait_ge(S["u_ps"], i + 1)
                        for e in range(2):
                            dve.tensor_tensor(u0[rows, j, 128 * e:128 * e + 128], u0[rows, j, 128 * e:128 * e + 128],
                                              bank[e][rows, 0:128], ALU.add).then_inc(S["u_ok"], 1)
                        for b in range(2):
                            dve.wait_ge(S["s_ps"], 2 * i + b + 1)
                            end = CH * (i + 1) - 1
                            dve.scalar_tensor_tensor(st[:, new, b, :], st[:, old, b, :], einc[:, b, end:end + 1],
                                                     bank[2 + b][:, 0:HD], ALU.mult, ALU.add).then_inc(S["s_ok"], 1)
                        for step, which in with_chunk.get(i, ()):
                            step(which)
                    for j in range(3):
                        t0, n = TILES[j]
                        for e in range(2):
                            dve.wait_ge(S["o_ps"], 2 * j + e + 1)
                            rows = slice(64 * e, 64 * e + 64)
                            dve.tensor_copy(ow[rows, :, t0:t0 + n],
                                            bank[4 + 2 * (j % 2) + e][rows, 0:256].rearrange("p (b t) -> p b t", b=2)[:, :, 0:n])\
                               .then_inc(S["o_ok"], 1)

                    for j in range(3):
                        t0, n = TILES[j]
                        for e in range(2):
                            dve.wait_ge(S["ro_ps"], 2 * j + e + 1)
                            rows = slice(64 * e, 64 * e + 64)
                            dve.tensor_copy(og[rows, :, t0:t0 + n],
                                            bank[2 * (j % 2) + e][rows, 0:256].rearrange("p (b t) -> p b t", b=2)[:, :, 0:n])\
                               .then_inc(S["ro_ok"], 1)

                    for which, (o, sq) in enumerate(((ow, kappa), (og, osq))):
                        dve.wait_ge(S["o_ok"] if which == 0 else S["ro_ok"], 6)
                        for b in range(2):
                            dve.wait_ge(S["gn_ps"], 2 * which + 1 + b)
                            link(dve.tensor_tensor(o[:, b, :], o[:, b, :], bank[4 + 2 * which + b][:, 0:T], ALU.subtract))
                        dve.tensor_tensor(sq, o, o, ALU.mult).then_inc(S["gn_sq"], 1)

                    def fox_max(h):
                        e = h % 2
                        sc = bank[e]
                        diag = sc[:, 0:384].rearrange("p (k t) -> p k t", k=3)[:, 0:3:2, :]
                        dve.wait_ge(S["fs_ps"], h + 1)
                        link(dve.tensor_tensor(diag, diag, c("causal").unsqueeze(1).to_broadcast([P, 2, 128]), ALU.add))
                        dve.tensor_reduce(fm[:, 0:1], sc[:, 0:128], AX_X, ALU.max).then_inc(S["fred"], 1)
                        dve.tensor_reduce(fm[:, 1:2], sc[:, 128:384], AX_X, ALU.max).then_inc(S["fred"], 1)
                        dve.wait_ge(S["fred"], 2 * h + 2)
                        dve.tensor_scalar(fm[:, 8 + 2 * e:10 + 2 * e], fm[:, 0:2], -0.125, None, ALU.mult)\
                           .then_inc(S["fmx"], 1)

                    def ret_out():
                        dve.wait_ge(S["gn_rs"], 2)
                        link(dve.tensor_tensor(og, og, osq, ALU.mult))
                        dve.tensor_tensor(hT[:, 6:8, :], og, zT[:, Z_TG:Z_TG + 2, :], ALU.mult).then_inc(S["ret_done"], 1)
                        dve.tensor_copy(kc[:, :, PAST:], zT[:, Z_FK:Z_FK + 4, TP:T]).then_inc(S["kcnew"], 1)

                    def fox_out(h):
                        b, e = h // 2, h % 2
                        rows = slice(64 * e, 64 * e + 64)
                        dve.wait_ge(S["fo_ps"], h + 1)
                        dve.tensor_tensor(hT[rows, b, 0:TP], bank[4 + b % 2][rows, 0:TP], fg[rows, b, 0:TP], ALU.mult)\
                           .then_inc(S["fo_ok"], 1)

                    def fox_normed(h):
                        e = h % 2
                        dve.wait_ge(S["fexp"], 2 * h + 2)
                        link(dve.reciprocal(fm[:, 16 + 2 * e:18 + 2 * e], fm[:, 12 + 2 * e:14 + 2 * e]))
                        link(dve.tensor_scalar(pq[:, e, 0:128], pq[:, e, 0:128], fm[:, 16 + 2 * e:17 + 2 * e], None, ALU.mult))
                        dve.tensor_scalar(pq[:, e, 128:384], pq[:, e, 128:384], fm[:, 17 + 2 * e:18 + 2 * e], None, ALU.mult)\
                           .then_inc(S["fpn"], 1)

                    fox_max(0)
                    fox_max(1)
                    fox_normed(0)
                    for h in range(FOX_H):
                        if h + 1 < FOX_H:
                            fox_normed(h + 1)
                        if h + 2 < FOX_H:
                            fox_max(h + 2)
                        fox_out(h)
                        if h == 1:
                            ret_out()
                    def out_lo(bs, ts, n):
                        dve.wait_ge(S["oh_hi"], n + 1)
                        dve.tensor_tensor(oh_lo[:, bs, ts], hT[:, bs, ts], oh_hi[:, bs, ts], ALU.subtract)\
                           .then_inc(S["oh_lo"], 1)

                    def out_rest(s):
                        hi, lo = wo[s]
                        dve.wait_ge(S["ocast"], s + 1)
                        dve.tensor_tensor(lo, wc[:, (POS_OUT + s) % RING, :], hi, ALU.subtract).then_inc(S["olo"], 1)

                    out_rest(0)
                    for g in range(2):
                        dve.wait_ge(S["ss_ps"], g + 1)
                        link(dve.tensor_tensor(ps_s[:, g, PAST:], bank[2 * g + 1][:, 0:TS], c("causal4"), ALU.add))
                        link(dve.tensor_reduce(fm[:, 26:27], ps_s[:, g, PAST:], AX_X, ALU.max))
                        link(dve.tensor_reduce(fm[:, 27:28], bank[2 * g][:, :], AX_X, ALU.max))
                        link(dve.tensor_tensor(fm[:, 28:29], fm[:, 26:27], fm[:, 27:28], ALU.max))
                        dve.tensor_scalar(fm[:, 20 + g:21 + g], fm[:, 28:29], -0.125, None, ALU.mult).then_inc(S["smx"], 1)
                        out_lo((slice(4, 8), slice(0, 4))[g], (slice(0, T), slice(0, TP))[g], g)
                        dve.wait_ge(S["sexp"], 2 * g + 2)
                        link(dve.tensor_tensor(fm[:, 29:30], fm[:, 22 + g:23 + g], fm[:, 24 + g:25 + g], ALU.add))
                        link(dve.reciprocal(fm[:, 30:31], fm[:, 29:30]))
                        dve.tensor_scalar(ps_s[:, g, :], ps_s[:, g, :], fm[:, 30:31], None, ALU.mult).then_inc(S["spn"], 1)
                    for e in range(2):
                        dve.wait_ge(S["so_ps"], e + 1)
                        rows = slice(64 * e, 64 * e + 64)
                        dve.tensor_tensor(hT[rows, 0:4, TP:T], bank[6 + e][rows, 0:128].rearrange("p (b t) -> p b t", b=4),
                                          fg[rows, :, TP:T], ALU.mult).then_inc(S["so_ok"], 1)

                    out_lo(slice(0, 4), slice(TP, T), 2)
                    out_rest(1)
                    out_rest(2)
                    for b in range(DB):
                        if b == 4:
                            out_rest(3)
                        dve.wait_ge(S["out_ps"], b + 1)
                        dve.tensor_tensor(xT[:, b, :], bank[b][:, 0:T], xT[:, b, :], ALU.add).then_inc(S["x_ready"], 1)

                    rest(1, 0)
                    rest(1, 1)
                    norm(2, "n2")
                    ffn(1)

                    for b in range(DB):
                        lo_of(xT, b, 2)
                    rest(1, N_SPLIT + 1)
                    dve.wait_ge(S["ple_e"], DB)
                    for b in range(DB):
                        if b in (0, 2):
                            rest(1, N_SPLIT + 2 + b // 2)
                        dve.wait_ge(S["g_tanh"], b + 1)
                        link(dve.scalar_tensor_tensor(proj_e[:, b, :], ple_gate[:, b, :], 1.0, proj_e[:, b, :],
                                                      ALU.add, ALU.mult))
                        dve.scalar_tensor_tensor(xT[:, b, :], proj_e[:, b, :], 0.5, xT[:, b, :], ALU.mult, ALU.add)\
                           .then_inc(S["x_ready"], 1)

                @block.tensor
                def _(pe):
                    def slot(p):
                        return wc[:, p % RING, :].rearrange("p (k n) -> p k n", k=DB)

                    def norm(s):
                        for b in range(DB):
                            pe.wait_ge(S["sq"], 8 * (s - 1) + b + 1)
                            mm = pe.matmul(bank[0][:, 0:T], c("mean"), squares[s][:, b, :], start=(b == 0), stop=(b == DB - 1))
                        mm.then_inc(S["norm_ps"], 1)

                    def arrived(p, more=0):
                        pe.wait_ge(S[f"col{p % RING}"], more * 16 + 16 * (p // RING + 1))

                    def ffn(f):
                        def split(s, i=0, k=DB):
                            pe.wait_ge(S["cast"], i * 4 + (N_SPLIT * f + s + 1))
                            return [x.rearrange("p (k n) -> p k n", k=k) for x in ws[s % 2]]

                        def lo_there(s, i=0):
                            pe.wait_ge(S["wlo"], i * 4 + (N_SPLIT * f + s + 1))

                        def columns(i, s):
                            hi, lo = split(s, i)
                            blocks = (s // 2 * 2, s // 2 * 2 + 1)
                            for w, (x, there) in enumerate(((h_hi, "h_hi"), (h_lo, "h_lo"))):
                                for q in blocks:
                                    o = bank[2 * (q % 4) + s % 2][:, 0:T]
                                    cs = slice(q % 2 * 128, q % 2 * 128 + 128)
                                    if s % 2 == 0 and w == 0:
                                        pe.wait_ge(S["hidden"], i * 4 + (FB * f + q + 1))
                                    for k in range(DB):
                                        if s == 0 and q == 0:
                                            pe.wait_ge(S[there], DB * f + k + 1)
                                        pe.matmul(o, hi[:, k, cs], x[:, k, :], start=(w == 0 and k == 0), stop=False)
                            lo_there(s, i)
                            for q in blocks:
                                o = bank[2 * (q % 4) + s % 2][:, 0:T]
                                cs = slice(q % 2 * 128, q % 2 * 128 + 128)
                                for k in range(DB):
                                    mm = pe.matmul(o, lo[:, k, cs], h_hi[:, k, :], start=False, stop=(k == DB - 1))
                                mm.then_inc(S["up_ps" if s % 2 else "gate_ps"], 1)

                        with pe.Fori(0, FB // 4) as i:
                            for s in range(4):
                                columns(i, s)
                        columns(0, N_FFN_SLOTS - 2)
                        columns(0, N_FFN_SLOTS - 1)

                        def down(j, i=0):
                            s = N_FFN_SLOTS + j
                            hi, lo = split(s, i, 2)

                            def product(w, x, kk, m, start=False, stop=False):
                                k = 2 * j + kk
                                rhs = x[:, k, :] if isinstance(i, int) else x[:, bass.ds(i * 8 + k, 1), :]
                                return pe.matmul(bank[m][:, 0:T], w[:, kk, m * 128:m * 128 + 128], rhs,
                                                 start=start, stop=stop)

                            if j == DSTEPS - 1:
                                lo_there(s)
                                for m in range(DB):
                                    for kk in range(2):
                                        product(hi, hid_hi, kk, m)
                                        product(hi, hid_lo, kk, m)
                                        mm = product(lo, hid_hi, kk, m, stop=(kk == 1))
                                    mm.then_inc(S["down_ps"], 1)
                                return
                            for m in (4, 5, 6, 7, 0, 1, 2, 3):
                                if j == 0 and m == 0:
                                    pe.wait_ge(S["hidden"], FB * f + 4 + FB)
                                for kk in range(2):
                                    product(hi, hid_hi, kk, m, start=(j == 0 and kk == 0))
                                    product(hi, hid_lo, kk, m)
                            lo_there(s, i)
                            for m in range(DB):
                                for kk in range(2):
                                    mm = product(lo, hid_hi, kk, m)
                            mm.then_inc(S["down_used"], 1)

                        pe.wait_ge(S["hid_lo"], FB * f + 2 + FB - 2)
                        down(0)
                        with pe.Fori(0, 2) as i:
                            for u in range(4):
                                down(1 + u, i)
                        down(DSTEPS - 2)
                        pe.wait_ge(S["hid_lo"], FB * f + 2 + FB)
                        down(DSTEPS - 1)

                    def heads(fn):
                        for g in range(4):
                            fn(g, *head_of(g))

                    ffn(0)
                    norm(1)

                    def z_slot(i, s, blocks=2):
                        for n in range(2 * s, 2 * s + blocks):
                            o = bank[n % Z_BANKS][:, 0:T]
                            hi, lo = zw[n % 2]
                            pe.wait_ge(S["z_ev"], i * 8 + n + 1)
                            pe.wait_ge(S["zcast"], i * 8 + n + 1)
                            for w, (x, there) in enumerate(((zh_hi, "zh_hi"), (zh_lo, "zh_lo"))):
                                for k in range(DB):
                                    if n == 0:
                                        pe.wait_ge(S[there], k + 1)
                                    pe.matmul(o, hi[:, k, :], x[:, k, :], start=(w == 0 and k == 0), stop=False)
                            pe.wait_ge(S["zlo"], i * 8 + n + 1)
                            for k in range(DB):
                                mm = pe.matmul(o, lo[:, k, :], zh_hi[:, k, :], start=False, stop=(k == DB - 1))
                            mm.then_inc(S["z_ps"], 1)

                    with pe.Fori(0, 2) as i:
                        for s in range(4):
                            z_slot(i, s)
                    z_slot(0, 8)

                    pe.wait_ge(S["lowin"], 1)
                    low = par[:, PARAMS["low"][0]:PARAMS["low"][0] + 256]
                    def low_rank(i):
                        rows = slice(32 * (i // 2 + 1), 32 * (i // 2 + 2))
                        rhs = zT[rows, Z_SMALL, :] if i // 2 == 1 else dz[rows, 0, :]
                        pe.matmul(bank[4 + i if i < 4 else 2 + i][:, 0:T], low[rows, (i % 2) * 128:(i % 2) * 128 + 128],
                                  rhs, start=True, stop=True).then_inc(S["low_ps"], 1)

                    for i in range(4):
                        low_rank(i)
                    z_slot(0, 9)
                    pe.wait_ge(S["e_low"], 4)
                    for i in range(4, 6):
                        low_rank(i)
                    pe.wait_ge(S["ksq"], 1)
                    for b in range(2):
                        pe.matmul(bank[4 + b][:, 0:T], c("headsum"), bhat[:, b, :], start=True, stop=True)\
                          .then_inc(S["kk_ps"], 1)
                    for s in range(10, 12):
                        z_slot(0, s)

                    def rotate(b):
                        pe.matmul(bank[4 + b % 2][:, 0:T], c("rot"), zT[:, Z_TQ + b, :], start=True, stop=True)\
                          .then_inc(S["rot_ps"], 1)

                    pe.wait_ge(S["kln"], 2)
                    rotate(0)
                    rotate(1)
                    pe.wait_ge(S["gcp"], 2)
                    for b in range(2):
                        pe.wait_ge(S["bonin"], b + 1)
                        pe.matmul(bank[6 + b][:, 0:T], c("headsum"), bon[:, b, :], start=True, stop=True)\
                          .then_inc(S["bon_ps"], 1)
                    for s in range(12, 15):
                        z_slot(0, s)
                    pe.wait_ge(S["prods"], 1)
                    pe.wait_ge(S["mixin"], layer * MIXIN_PER_LAYER + 48)
                    pe.wait_ge(S["bon_ok"], 2)
                    pe.wait_ge(S["rotd"], 2)
                    rotate(2)
                    rotate(3)
                    z_slot(0, 15, 1)
                    for j in range(3):
                        t0, n = TILES[j]
                        for k in range(2):
                            i4 = 2 * j + k
                            if i4 == 2:
                                pe.wait_ge(S["rotd"], 4)
                            if i4 >= 4:
                                pe.wait_ge(S["trc"], i4 - 3)
                            srcs = ((ar[:, :, 0, :], bhat), (khat, zT[:, Z_V:Z_V + 2, :]))[k]
                            for i in range(4):
                                mm = pe.transpose(bank[4 + (2 * j + k + 2) % 4][0:n, 128 * i:128 * i + 128], srcs[i // 2][:, i % 2, t0:t0 + n],
                                                  c("ident"))
                            mm.then_inc(S["tr_ps"], 1)
                    pe.wait_ge(S["trc"], 6)
                    pe.wait_ge(S["z_ev"], Z_BANKS + NZ)
                    for o, j in enumerate(MATS_ORDER):
                        t0, n = TILES[j]
                        ts_ = slice(t0, t0 + n)
                        for e in range(2):
                            rows = slice(64 * e, 64 * e + 64)
                            for i, view in enumerate(mats_psum(j, e)):
                                if o == 2:
                                    pe.wait_ge(S["masks"], 5 * e + (1, 3, 5)[i])
                                for b in range(2):
                                    if i == 0:
                                        mm = pe.matmul(view[0:n, b, 0, 0:n], ar[rows, b, 0, ts_],
                                                       beta[rows, b, ts_], start=True, stop=True)
                                    else:
                                        mm = pe.matmul(view[0:n, b, :, 0:n], (beta, kappa)[i - 1][rows, b, ts_],
                                                       ar[rows, b, :, ts_], start=True, stop=True)
                                mm.then_inc(S["mats_ps"], 1)
                    pe.wait_ge(S["masks"], 30)
                    for j in range(3):
                        n = TILES[j][1]
                        for g in range(4):
                            par_, b = g // 2, g % 2
                            at = U_AT[j] + HD * g
                            mm = pe.matmul(bank[4 + j % 2][0:n, at:at + HD], bt[j][0:n, g, 0:n],
                                           tok[0:n, j, 6 + b, 64 * par_:64 * par_ + 64], start=True, stop=True)
                        mm.then_inc(S["bv_ps"], 1)
                    pe.wait_ge(S["xt"], 6)
                    for s in range(1, 5):
                        for j in range(3):
                            n = TILES[j][1]
                            pe.wait_ge(S["lev"], 3 * (s - 1) + j + 1)
                            if s > 1:
                                pe.wait_ge(S["lvl"], 6 * (s - 2) + 2 * j + 2)
                            for g in range(4):
                                mm = pe.matmul(bank[LEVEL_BANKS[j][0]][0:n, 128 * g:128 * g + n], ml[j][0:n, g, 0:n],
                                               xx[j][0:n, g, 0:n], start=True, stop=True)
                            mm.then_inc(S["y_ps"], 1)
                        for j in range(3):
                            n = TILES[j][1]
                            pe.wait_ge(S["ycp"], 3 * (s - 1) + j + 1)
                            for g in range(4):
                                mm = pe.matmul(bank[LEVEL_BANKS[j][1]][0:n, 128 * g:128 * g + n], tt[j][0:n, g, 0:n],
                                               yy[j][0:n, g, 0:n], start=True, stop=True)
                            mm.then_inc(S["dx_ps"], 1)
                            if s < 4:
                                for g in range(4):
                                    mm = pe.matmul(bank[LEVEL_BANKS[j][0]][0:n, 128 * g:128 * g + n],
                                                   yy[j][0:n, g, 0:n], tt[j][0:n, g, 0:n], start=True, stop=True)
                                mm.then_inc(S["dt_ps"], 1)
                    pe.wait_ge(S["bvc"], 3)
                    for j in range(3):
                        n = TILES[j][1]
                        pe.wait_ge(S["lvl"], 18 + j + 1)
                        if j == 2:
                            pe.wait_ge(S["uac"], 1)
                        for g in range(4):
                            at = U_AT[j] + HD * g
                            mm = pe.matmul(bank[4 + j % 2][0:n, at:at + HD], xx[j][0:n, g, 0:n],
                                           u0[0:n, j, HD * g:HD * g + HD], start=True, stop=True)
                        mm.then_inc(S["ua_ps"], 1)
                        for g in range(4):
                            par_, b = g // 2, g % 2
                            mm = pe.matmul(bank[LEVEL_BANKS[j][0]][64 * par_:64 * par_ + 64, 128 * b:128 * b + n],
                                           tok[0:n, j, b, 64 * par_:64 * par_ + 64], xx[j][0:n, g, 0:n],
                                           start=True, stop=True)
                        mm.then_inc(S["ua_ps"], 1)
                    pe.wait_ge(S["uac"], 6)

                    def ret_tok(j):
                        t0, n = TILES[j]
                        if j == 2:
                            pe.wait_ge(S["rtrc"], 1)
                        pe.wait_ge(S["decd"], 2)
                        for i in range(4):
                            src = kdec[:, i, t0:t0 + n] if i < 2 else zT[:, Z_TV + i - 2, t0:t0 + n]
                            mm = pe.transpose(bank[6 + j % 2][0:n, 128 * i:128 * i + 128], src, c("ident"))
                        mm.then_inc(S["rtr_ps"], 1)

                    def ret_scores(j):
                        t0, n = TILES[j]
                        for e in range(2):
                            if j:
                                pe.wait_ge(S["smd"], 2 * (j - 1) + e + 1)
                            hs = slice(64 * e, 64 * e + 64)
                            for b in range(2):
                                mm = pe.matmul(bank[4 + e][0:n, 128 * b:128 * b + n], zT[hs, Z_TK + b, t0:t0 + n],
                                               zT[hs, Z_TQ + b, t0:t0 + n], start=True, stop=True)
                            mm.then_inc(S["sm_ps"], 1)

                    def ret_kv(i):
                        j, rows = (i // 2, slice(64 * (i % 2), 64 * (i % 2) + 64)) if i < 4 else (2, slice(0, TS))
                        if i == 0:
                            pe.wait_ge(S["rtrc"], 3)
                        for b in range(2):
                            for e in range(2):
                                s = 128 * (i // 2) + 64 * b
                                fs = slice(128 * b + 64 * e, 128 * b + 64 * e + 64)
                                mm = pe.matmul(bank[6 + i % 2][64 * e:64 * e + 64, s:s + HD], rtok[rows, j, fs],
                                               rtok[rows, j, 256 + fs.start:256 + fs.stop], start=True, stop=True)
                        mm.then_inc(S["kv_ps"], 1)

                    with_chunk = {0: [(ret_tok, 0)], 1: [(ret_scores, 0)], 2: [(ret_tok, 1)], 3: [(ret_scores, 1)],
                                  4: [(ret_tok, 2), (ret_scores, 2)], 5: [(ret_kv, 0), (ret_kv, 1), (ret_kv, 2)],
                                  6: [(ret_kv, 3), (ret_kv, 4)]}
                    for i in range(NCH):
                        j, q = (i // 4, i % 4) if i < 8 else (2, 0)
                        rows = slice(32 * q, 32 * q + 32)
                        s_at = i if i < 8 else 9
                        if i:
                            pe.wait_ge(S["s_ok"], 2 * i)
                        for g in range(4):
                            hp, b = head_of(g)
                            mm = pe.matmul(bank[g // 2][rows, HD * b:HD * b + HD], atT[hp:hp + 64, b, CH * i:CH * i + CH],
                                           st[hp:hp + 64, s_at, b, :], start=True, stop=True)
                        mm.then_inc(S["u_ps"], 1)
                        for b in range(2):
                            for e in range(2):
                                hs = slice(64 * e, 64 * e + 64)
                                pe.matmul(bank[2 + b][hs, 0:HD], tok[rows, j, 4 + b, hs], tok[rows, j, 6 + b, hs],
                                          start=True, stop=False)
                        pe.wait_ge(S["u_ok"], 2 * i + 2)
                        for b in range(2):
                            for e in range(2):
                                hs = slice(64 * e, 64 * e + 64)
                                g = 2 * e + b
                                mm = pe.matmul(bank[2 + b][hs, 0:HD], tok[rows, j, 2 + b, hs],
                                               u0[rows, j, HD * g:HD * g + HD], start=False, stop=True)
                            mm.then_inc(S["s_ps"], 1)
                        for step, which in with_chunk.get(i, ()):
                            step(which)
                    pe.wait_ge(S["rsd"], 10)
                    pe.wait_ge(S["smd"], 6)
                    for j in range(3):
                        t0, n = TILES[j]
                        for e in range(2):
                            if j >= 2:
                                pe.wait_ge(S["o_ok"], 2 * (j - 2) + e + 1)
                            hs = slice(64 * e, 64 * e + 64)
                            bk = bank[4 + 2 * (j % 2) + e]
                            for b in range(2):
                                g = 2 * e + b
                                o = bk[hs, 128 * b:128 * b + n]
                                pe.matmul(o, tok[0:n, j, 6 + b, hs], dtm[0:n, j, 128 * g:128 * g + n], start=True, stop=False)
                                for q in range(n // CH):
                                    i = 4 * j + q
                                    pe.matmul(o[:, CH * q:CH * q + CH], st[hs, i if i < 8 else 9, b, :],
                                              ar[hs, b, 1, CH * i:CH * i + CH], start=False, stop=False)
                                mm = pe.matmul(o, u0[0:n, j, HD * g:HD * g + HD], ctm[0:n, j, 128 * g:128 * g + n],
                                               start=False, stop=True)
                            mm.then_inc(S["o_ps"], 1)

                    for j in range(3):
                        t0, n = TILES[j]
                        for e in range(2):
                            if j >= 2:
                                pe.wait_ge(S["ro_ok"], 2 * (j - 2) + e + 1)
                            hs = slice(64 * e, 64 * e + 64)
                            bk = bank[2 * (j % 2) + e]
                            for b in range(2):
                                g = 2 * e + b
                                o = bk[hs, 128 * b:128 * b + n]
                                pe.matmul(o, rtok[0:n, j, 256 + 128 * b + 64 * e:256 + 128 * b + 64 * e + 64],
                                          smx[0:n, j, 128 * g:128 * g + n], start=True, stop=False)
                                nch = 2 if j < 2 else 1
                                w = n // nch
                                for q in range(nch):
                                    i = 2 * j + q if j < 2 else 5
                                    mm = pe.matmul(o[:, w * q:w * q + w], rst[hs, i, b, :],
                                                   qdec[hs, b, t0 + w * q:t0 + w * q + w], start=False, stop=(q == nch - 1))
                            mm.then_inc(S["ro_ps"], 1)
                    def head_sums(which, src):
                        for b in range(2):
                            pe.matmul(bank[4 + 2 * which + b][:, 0:T], c("headmean"), src[:, b, :], start=True, stop=True)\
                              .then_inc(S["gn_ps"], 1)

                    pe.wait_ge(S["o_ok"], 6)
                    head_sums(0, ow)
                    pe.wait_ge(S["ro_ok"], 6)
                    head_sums(1, og)
                    for j in range(3):
                        t0, n = TILES[j]
                        if j == 2:
                            pe.wait_ge(S["vtc"], 1)
                        for b in range(4):
                            mm = pe.transpose(bank[2 + j % 2][0:n, 128 * b:128 * b + 128], zT[:, Z_FV + b, t0:t0 + n],
                                              c("ident"))
                        mm.then_inc(S["vt_ps"], 1)
                    pe.wait_ge(S["fc_ok"], 2)

                    def scores(h):
                        b, hs = h // 2, slice(64 * (h % 2), 64 * (h % 2) + 64)
                        if h >= 2:
                            pe.wait_ge(S["fexp"], 2 * h - 2)
                        for q, k1, at in ((0, 128, 0), (128, 256, 128)):
                            o = bank[h % 2][:, at:at + k1]
                            pe.matmul(o, zT[hs, Z_FQ + b, q:q + 128], zT[hs, Z_FK + b, 0:k1], start=True, stop=False)
                            mm = pe.matmul(o, foxL[:, h, q:q + 128], foxR[:, 0:k1], start=False, stop=True)
                        mm.then_inc(S["fs_ps"], 1)

                    for which, sq in enumerate((kappa, osq)):
                        pe.wait_ge(S["gn_sq"], which + 1)
                        head_sums(which, sq)
                        scores(which)
                    pe.wait_ge(S["vtc"], 3)
                    for h in range(FOX_H):
                        b, e = h // 2, h % 2
                        hs = slice(64 * e, 64 * e + 64)
                        if h == FOX_H - 1:
                            pe.wait_ge(S["mixin"], layer * MIXIN_PER_LAYER + 160)
                        pe.wait_ge(S["fpn"], h + 1)
                        if h >= 2:
                            pe.wait_ge(S["ftc"], h - 1)
                        for i in range(3):
                            mm = pe.transpose(bank[2 + e][:, 128 * i:128 * i + 128], pq[:, e, 128 * i:128 * i + 128], c("ident"))
                        mm.then_inc(S["ft_ps"], 1)
                        if h + 2 < FOX_H:
                            scores(h + 2)
                        if h == 0:
                            pe.wait_ge(S["gn_ln"], 4)
                        pe.wait_ge(S["ftc"], h + 1)
                        if h >= 4:
                            pe.wait_ge(S["fo_ok"], h - 3)
                        o = bank[4 + b % 2][hs, :]
                        pe.matmul(o[:, 0:256], vtok[:, 0, HD * h:HD * h + HD], pt[:, e, 0:256], start=True, stop=False)
                        pe.matmul(o[:, 128:256], vtok[:, 1, HD * h:HD * h + HD], pt[:, e, 256:384], start=False, stop=True)\
                          .then_inc(S["fo_ps"], 1)
                    pe.wait_ge(S["fexp"], 16)
                    pe.wait_ge(S["ftc"], 8)
                    pe.wait_ge(S["kcnew"], 1)
                    for g in range(2):
                        hs = slice(64 * g, 64 * g + 64)
                        for i, (k0, k1) in enumerate(((0, PAST), (PAST, PAST + TS))):
                            for b in range(4):
                                o = bank[2 * g + i][TS * b:TS * b + TS, 0:k1 - k0]
                                pe.matmul(o, zT[hs, Z_FQ + b, TP:T], kc[hs, b, k0:k1], start=True, stop=False)
                                mm = pe.matmul(o, foxL[:, 2 * b + g, TP:T], foxR[:, TP + k0:TP + k1], start=False, stop=True)
                        mm.then_inc(S["ss_ps"], 1)
                    pe.wait_ge(S["fo_ok"], 8)
                    for g in range(2):
                        hs = slice(64 * g, 64 * g + 64)
                        pe.wait_ge(S["spn"], g + 1)
                        if g:
                            pe.wait_ge(S["stc"], 2)
                        for i in range(4):
                            mm = pe.transpose(bank[4][:, 128 * i:128 * i + 128], ps_s[:, g, 128 * i:128 * i + 128], c("ident"))
                        mm.then_inc(S["st_ps"], 1)
                        pe.transpose(bank[5][0:TS, 0:128], ps_s[:, g, PAST:], c("ident")).then_inc(S["st_ps"], 1)
                        pe.wait_ge(S["stc"], 2 * g + 2)
                        for b in range(4):
                            h = 2 * b + g
                            o = bank[6 + g][hs, TS * b:TS * b + TS]
                            for i in range(4):
                                pe.matmul(o, vc[:, i, HD * h:HD * h + HD], pt_s[:, g, i, TS * b:TS * b + TS],
                                          start=(i == 0), stop=False)
                            mm = pe.matmul(o, vtok[0:TS, 2, HD * h:HD * h + HD], pt_s[0:TS, g, 4, TS * b:TS * b + TS],
                                           start=False, stop=True)
                        mm.then_inc(S["so_ps"], 1)

                    for s in range(4):
                        hi, lo = (x.rearrange("p (k n) -> p k n", k=DB) for x in wo[s])
                        pe.wait_ge(S["ocast"], s + 1)
                        for half in range(2):
                            ks = (range(4, 8), range(4))[half]
                            for x, there in ((oh_hi, "oh_hi"), (oh_lo, "oh_lo")):
                                if s == 0:
                                    pe.wait_ge(S[there], (1, 3)[half])
                                for cc in range(2):
                                    for k in ks:
                                        pe.matmul(bank[2 * s + cc][:, 0:T], hi[:, k, cc * 128:cc * 128 + 128], x[:, k, :],
                                                  start=(x is oh_hi and k == 4), stop=False)
                        pe.wait_ge(S["olo"], s + 1)
                        for cc in range(2):
                            for k in range(DB):
                                mm = pe.matmul(bank[2 * s + cc][:, 0:T], lo[:, k, cc * 128:cc * 128 + 128],
                                               oh_hi[:, k, :], start=False, stop=(k == DB - 1))
                            mm.then_inc(S["out_ps"], 1)

                    norm(2)

                    pe.wait_ge(S["x_ready"], 24)
                    pe.wait_ge(S["p_in"], layer * P_IN_PER_LAYER + 16)
                    arrived(POS_PROJ)
                    proj = wc[:, POS_PROJ % RING, :].rearrange("p (k n) -> p k n", k=2)
                    for b in range(DB):
                        if b >= 4:
                            pe.wait_ge(S["pj_cp"], b - 3)
                        for k in range(2):
                            mm = pe.matmul(bank[4 + b % 4][:, 0:T], proj[:, k, b * 128:b * 128 + 128], ple_in[:, k, :],
                                           start=(k == 0), stop=(k == 1))
                        mm.then_inc(S["pj_ps"], 1)
                    pe.wait_ge(S["pj_cp"], DB)
                    for b in range(DB):
                        pe.wait_ge(S["pj_sq"], b + 1)
                        mm = pe.matmul(bank[7][:, 0:T], c("mean"), proj_sq[:, b, :], start=(b == 0), stop=(b == DB - 1))
                    mm.then_inc(S["pn_ps"], 1)
                    pe.wait_ge(S["ple_rs"], 1)
                    ffn(1)

                    for s in range(4):
                        pe.wait_ge(S["cast"], 2 * N_SPLIT + s + 1)
                        hi, lo = (x.rearrange("p (k n) -> p k n", k=DB) for x in ws[(N_SPLIT + s) % 2])
                        order = ((hi, h_hi), (lo, h_hi), (hi, h_lo)) if s == 0 else ((hi, h_hi), (hi, h_lo), (lo, h_hi))
                        for n, (w, x) in enumerate(order):
                            if w is lo:
                                pe.wait_ge(S["wlo"], 2 * N_SPLIT + s + 1)
                            for cc in range(2):
                                for k in range(DB):
                                    if s == 0 and cc == 0 and w is hi:
                                        pe.wait_ge(S["h_hi" if x is h_hi else "h_lo"], 2 * DB + k + 1)
                                    mm = pe.matmul(bank[2 * s + cc][:, 0:T], w[:, k, cc * 128:cc * 128 + 128], x[:, k, :],
                                                   start=(n == 0 and k == 0), stop=(n == 2 and k == DB - 1))
                                if n == 2:
                                    mm.then_inc(S["g_ps"], 1)
                    pe.wait_ge(S["g_tanh"], 1)
                    norm(3)

            nc.all_engine_barrier(sems_to_clear=layer_sems)

        with nc.Block() as block:
            @block.vector
            def _(dve):
                for b in range(DB):
                    dve.scalar_tensor_tensor(hT[:, b, :], xT[:, b, :], nf[:, b:b + 1], rs[:], ALU.mult, ALU.mult)\
                       .then_inc(end_sem["y"], 1)

            @block.sync
            def _(sp):
                for b in range(DB):
                    sp.wait_ge(end_sem["y"], b + 1)
                    sp.dma_start(y_out[:, b, :], hT[:, b, :]).then_inc(end_sem["st"], 16)
                sp.wait_ge(end_sem["st"], 16 * DB)


def constants():
    con = np.zeros((P, N_CONST), np.float32)

    def put(name, a):
        at, n = CONSTS[name]
        a = np.asarray(a, np.float64).reshape(a.shape[0], -1)
        assert a.shape[1] == n, (name, a.shape, n)
        con[:a.shape[0], at:at + n] = a

    i = np.arange(P)
    same = (i[:, None] // HD == i[None, :] // HD).astype(np.float64)
    put("ident", np.eye(P))
    put("mean", np.full((P, P), 1.0 / D))
    put("headsum", same)
    put("headmean", same / HD)
    rot = np.zeros((P, P))
    for b in (0, 64):
        for k in range(32):
            rot[b + 32 + k, b + k] = -1.0
            rot[b + k, b + 32 + k] = 1.0
    put("rot", rot)
    pos = np.concatenate([np.arange(TP), PAST + np.arange(TS)]).astype(np.float32)
    inv = (np.float32(1.0) / np.float32(10000.0) ** (np.arange(32, dtype=np.float32) / np.float32(32))).astype(np.float32)
    ang = (pos[None, :] * inv[i % 32][:, None]).astype(np.float32)
    put("cos", np.cos(ang.astype(np.float64)))
    put("sin", np.sin(ang.astype(np.float64)))
    put("causal", np.where(i[:, None] >= i[None, :], 0.0, -1e30))
    k = np.arange(TS)
    put("causal4", np.where((i % TS)[:, None] >= k[None, :], 0.0, -1e30))
    u = i % CH
    chunk = i[:, None] // CH == i[None, :] // CH
    lv = []
    for s in range(5):
        w = 1 << s
        lv.append(chunk & (u[:, None] // (2 * w) == u[None, :] // (2 * w))
                  & (u[:, None] // w % 2 == 1) & (u[None, :] // w % 2 == 0))
    put("levels", np.concatenate(lv, axis=1))
    put("level0T", lv[0].T)
    put("before", chunk & (i[:, None] < i[None, :]))
    put("upto", chunk & (i[:, None] <= i[None, :]))
    put("restart", np.broadcast_to((np.arange(512) % CH != 0).astype(np.float64), (P, 512)))
    logg = np.log(1.0 - 2.0 ** (-5.0 - np.arange(4)))
    order = [2 * (g % 2) + g // 2 for g in range(4)]
    c64 = i[:, None] // 64 == i[None, :] // 64
    put("retmask", np.stack([np.exp(logg[h] * np.abs(i[:, None] - i[None, :])) * c64 * 0.125 for h in order], 1))
    put("retmask_s", np.stack([np.exp(logg[h] * np.abs(k[:, None] - k[None, :])) * 0.125 for h in order], 1))
    tpos = np.concatenate([np.arange(TP) % 64, np.arange(TS)])
    tlen = np.concatenate([np.full(TP, 64), np.full(TS, TS)])
    lg = np.stack([logg[2 * b + i // 64] for b in range(2)], 1)
    put("dquery", np.exp(lg[:, :, None] * (tpos + 1.0)))
    put("dstate", 0.125 * np.exp(lg[:, :, None] * (tlen - 1.0 - tpos)))
    put("dchunk", np.concatenate([np.exp(lg * 64.0), np.exp(lg * TS)], 1))
    put("fox8", 8.0 * np.eye(8))
    cols = np.zeros((P, 8))
    cols[:, C_EPS] = EPS
    cols[:, C_ONE] = 1.0
    cols[:, C_REPS] = RWKV_EPS
    cols[:, C_TEPS] = RET_EPS
    cols[:, C_KKB] = 15.0 * np.log(2.0)
    cols[32:64, C_SMALLSC], cols[96:128, C_SMALLSC] = -2.0, -1.0
    cols[32:64, C_SMALLM], cols[96:128, C_SMALLM] = 2.0, 1.0
    cols[32:64, C_SMALLA] = -1.0
    put("cols", cols)
    return con


def fox_rows():
    return np.ascontiguousarray(np.broadcast_to(-8.0 * np.eye(8, dtype=np.float32)[:, :, None], (8, FOX_H, T)))


def blocked(w, cols):
    L, d, m = w.shape
    return w.reshape(L, d // P, P, m // cols, cols).transpose(0, 3, 2, 1, 4).reshape(L, m // cols, P, -1)


def feature_major(x):
    y = np.moveaxis(x, -1, -2)
    return np.moveaxis(y.reshape(*y.shape[:-2], -1, P, y.shape[-1]), -3, -2)


def by_partition(v):
    return np.swapaxes(v.reshape(v.shape[0], -1, P), 1, 2)


def in_blocks(w):
    out = np.zeros((*w.shape[:-1], 32 * P), w.dtype)
    fox, rw, ret = 0, 2056, 2920

    def put(block, at, n, off=0):
        out[..., block * P + off:block * P + off + n] = w[..., at:at + n]

    put(Z_SMALL, fox + 1536, 8)
    put(Z_SMALL, rw + 256, 32, 32)
    put(Z_SMALL, rw + 800, 32, 64)
    put(Z_SMALL, rw + 832, 32, 96)
    put(Z_R, rw, 256)
    put(Z_K, rw + 288, 256)
    put(Z_V, rw + 544, 256)
    put(Z_TQ, ret, 1024)
    put(Z_FQ, fox, 1536)
    put(Z_FG, fox + 1544, 512)
    return out


def layout(i):
    L = DEPTH
    gate_up = []
    for f in ("1", "2"):
        g, u = blocked(i[f"w_ffn{f}_gate"], 256), blocked(i[f"w_ffn{f}_up"], 256)
        gate_up.append(np.stack([g, u], 2).reshape(L, -1, P, SLOT))
    z = blocked(in_blocks(i["w_in"]), 256)
    proj = i["w_ple_proj"].reshape(L, 2, P, D).transpose(0, 2, 1, 3).reshape(L, 1, P, SLOT)
    down = [i[f"w_ffn{f}_down"].reshape(L, DSTEPS, 2, P, D).transpose(0, 1, 3, 2, 4).reshape(L, DSTEPS, P, SLOT)
            for f in ("1", "2")]
    wcol = np.concatenate([gate_up[0], down[0], z, blocked(i["w_out"], 256), proj,
                           gate_up[1], down[1], blocked(i["w_ple_gate"], 256)], 1)
    x = np.concatenate([i["x_prompt"][0], i["x_sample"][0]], 0)
    p = np.concatenate([i["p_prompt"][:, 0], i["p_sample"][:, 0]], 1)
    pr = np.zeros((L, P, N_PARAM), np.float32)

    def put(name, a):
        at, n = PARAMS[name]
        pr[:, :a.shape[1], at:at + n] = a

    def rwkv_row(v):
        full = np.zeros((L, 3944), np.float32)
        full[:, 2056:2920] = v
        return by_partition(in_blocks(full)[:, :7 * P])

    for name, key in (("n1", "norm_ffn1"), ("nm", "norm_mix"), ("n2", "norm_ffn2"), ("pn", "ple_norm"),
                      ("w0", "rwkv_w0"), ("a0", "rwkv_a0"), ("kk", "rwkv_k_k"), ("ka", "rwkv_k_a"),
                      ("lnw", "rwkv_ln_w"), ("lnb", "rwkv_ln_b")):
        put(name, by_partition(i[key]))
    put("rk", by_partition(i["rwkv_r_k"].reshape(L, 256)))
    put("mu", rwkv_row(i["rwkv_mu"]))
    put("prev", rwkv_row(i["state_rwkv_shift"][:, 0, 0]))
    put("bf", i["fox_forget_bias"][:, :, None])
    at = PARAMS["low"][0]
    pr[:, 32:64, at:at + 256] = i["rwkv_w_up"]
    pr[:, 64:96, at:at + 256] = i["rwkv_a_up"]
    pr[:, 96:128, at:at + 256] = i["rwkv_g_up"]

    def states(s):
        s = s.reshape(L, 2, 2, HD, HD).transpose(0, 2, 3, 1, 4).reshape(L, P, 2, HD)
        return np.stack([np.zeros_like(s), s], 1)

    return {
        "wcol": wcol, "wfirst": np.concatenate([wcol[:, :RING], wcol[:1, :RING]], 0),
        "x_in": feature_major(x), "p_in": feature_major(p), "consts_in": constants(),
        "params_in": np.concatenate([pr, pr[:1]], 0), "foxl_in": fox_rows(),
        "kc_in": i["cache_fox_k"][:, 0].reshape(L, PAST, 4, P).transpose(0, 2, 3, 1),
        "vc_in": i["cache_fox_v"][:, 0].reshape(L, 4, P, 512).transpose(0, 2, 1, 3),
        "clf_in": i["cache_fox_logf"][:, 0].transpose(0, 2, 1),
        "srwkv_in": states(i["state_rwkv"][:, 0].transpose(0, 1, 3, 2)), "sret_in": states(i["state_ret"][:, 0]),
        "nf_in": by_partition(i["norm_final"][None])[0],
    }


OUTS = {"y_out": (P, DB, T), "k_out": (DEPTH, 4, P, T), "v_out": (DEPTH, 4, P, T), "logf_out": (DEPTH, 8, T),
        "shift_out": (DEPTH, P, N_SHIFTED, 2), "rwkv_out": (DEPTH, 2, P, 2, HD), "ret_out": (DEPTH, 2, P, 2, HD)}


def unlayout(o):
    L = DEPTH

    def halves(a):
        return a[..., :TP, :], a[..., TP:, :]

    y = o["y_out"].transpose(2, 1, 0).reshape(T, D)
    yp, ys = (a[None] for a in halves(y))
    kp, ks = (a.reshape(L, 1, -1, FOX_H, HD) for a in halves(o["k_out"].transpose(0, 3, 1, 2).reshape(L, T, 512)))
    vp, vs = (a.reshape(L, 1, -1, FOX_H, HD) for a in halves(o["v_out"].transpose(0, 3, 1, 2).reshape(L, T, 512)))
    lp, ls = (a[:, None] for a in halves(o["logf_out"].transpose(0, 2, 1)))
    row = o["shift_out"].transpose(0, 3, 2, 1).reshape(L, 2, 7 * P)
    sh = np.concatenate([row[..., P:3 * P], row[..., 32:64], row[..., 3 * P:7 * P], row[..., 64:128]], -1)

    def states(s):
        return s.reshape(L, 2, 2, HD, 2, HD).transpose(0, 1, 4, 2, 3, 5).reshape(L, 2, 4, HD, HD)

    rw = states(o["rwkv_out"]).transpose(0, 1, 2, 4, 3)
    rt = states(o["ret_out"])
    outs = (yp, ys, kp, vp, lp, rw[:, 0:1], sh[:, 0][:, None, None], rt[:, 0:1],
            ks, vs, ls, rw[:, 1:2], sh[:, 1][:, None, None], rt[:, 1:2])
    return tuple(np.ascontiguousarray(a) for a in outs)


def build(nc, shapes):
    args = {n: nc.dram_tensor(n, s, F32, kind="ExternalInput").ap() for n, s in shapes.items()}
    args |= {n: nc.dram_tensor(n, s, F32, kind="ExternalOutput").ap() for n, s in OUTS.items()}
    program(nc, **args)


def kernel(**inputs):
    from concourse import bacc
    from concourse.bass_utils import run_bass_kernel_spmd as run

    arrays = {n: np.ascontiguousarray(a) for n, a in layout({k: np.asarray(v) for k, v in inputs.items()}).items()}
    nc = bacc.Bacc("TRN2", target_bir_lowering=False, num_devices=1)
    build(nc, {n: a.shape for n, a in arrays.items()})
    r = run(nc, [arrays], core_ids=[0])
    return unlayout({n: r.results[0][n] for n in OUTS})
```
